# Optimizing a Trainium2 kernel written in Bass

```python
import math
import jax, jax.numpy as jnp
from jax import lax
import numpy as np

D_MODEL = 1024
BATCH = 1
SEQ = 1024
DEPTH = 2
DEC_BATCH = 8
DEC_SEQ = 4
PAST_LEN = 2048
PAGE_SIZE = 128

N_A_LAYERS = DEPTH // 2
N_B_LAYERS = DEPTH - N_A_LAYERS
GLA_HEADS = 4
GLA_DK = D_MODEL // (2 * GLA_HEADS)
GLA_DV = D_MODEL // GLA_HEADS
GLA_QK = GLA_HEADS * GLA_DK
GLA_VD = GLA_HEADS * GLA_DV
GLA_GATE_RANK = 16
GLA_GATE_TAU = 16.0
GLA_CHUNK = 64
GLA_SPLITS = (GLA_QK, 2 * GLA_QK, 2 * GLA_QK + GLA_VD, 2 * GLA_QK + 2 * GLA_VD)
GLA_IN = 2 * GLA_QK + 2 * GLA_VD + GLA_GATE_RANK
ATT_HEAD_DIM = 64
ATT_HEADS = D_MODEL // ATT_HEAD_DIM
ATT_KV_HEADS = max(1, ATT_HEADS // 8)
ATT_GROUP = ATT_HEADS // ATT_KV_HEADS
D_ATT = ATT_HEADS * ATT_HEAD_DIM
KV_W = ATT_KV_HEADS * ATT_HEAD_DIM
WINDOW = 128
WIN_BUF = min(WINDOW, PAST_LEN)
N_BUCKETS = 32
MAX_DISTANCE = 128
D_FF = 2816
CONV_W = 3
EPS = 1e-6

kernel_name = 'yoco_gla_swa_sink_convffn_step'

def rms_norm(x, g):
    xf = x.astype(jnp.float32)
    y = xf * lax.rsqrt(jnp.mean(xf * xf, axis=-1, keepdims=True) + EPS)
    return (y * g.astype(jnp.float32)).astype(x.dtype)

def gla_chunked(q, k, v, g, s0):
    B, L = q.shape[:2]
    C = min(GLA_CHUNK, L)
    n = L // C
    def to_chunks(t):
        return jnp.moveaxis(t.reshape(B, n, C, *t.shape[2:]), 1, 0).astype(jnp.float32)
    qc, kc, vc, gc = to_chunks(q), to_chunks(k), to_chunks(v), to_chunks(g)
    causal = jnp.tril(jnp.ones((C, C), bool))[None, :, :, None, None]
    def step(S, inp):
        qi, ki, vi, gi = inp
        b = jnp.cumsum(gi, axis=1)
        b_last = b[:, -1]
        o_inter = jnp.einsum('bchk,bhkv->bchv', qi * jnp.exp(b), S)
        diff = b[:, :, None] - b[:, None, :]
        decay = jnp.exp(jnp.where(causal, diff, -jnp.inf))
        A = jnp.einsum('bihk,bjhk,bijhk->bhij', qi, ki, decay)
        o_intra = jnp.einsum('bhij,bjhv->bihv', A, vi)
        k_dec = ki * jnp.exp(b_last[:, None] - b)
        S_new = jnp.exp(b_last)[..., None] * S + jnp.einsum('bchk,bchv->bhkv', k_dec, vi)
        return S_new, o_inter + o_intra
    S_fin, o = lax.scan(step, s0.astype(jnp.float32), (qc, kc, vc, gc))
    o = jnp.moveaxis(o, 0, 1).reshape(B, L, GLA_HEADS, GLA_DV)
    return o, S_fin

def gla_mixer(a, s0, w_in, w_gate_up, b_gate, g_out, w_out):
    B, L, _ = a.shape
    proj = a @ w_in
    q, k, v, r, glr = jnp.split(proj, GLA_SPLITS, axis=-1)
    gk = jax.nn.log_sigmoid((glr @ w_gate_up + b_gate).astype(jnp.float32)) / GLA_GATE_TAU
    shp = (B, L, GLA_HEADS, GLA_DK)
    o, s_fin = gla_chunked(q.reshape(shp) * GLA_DK ** -0.5, k.reshape(shp),
                           v.reshape(B, L, GLA_HEADS, GLA_DV), gk.reshape(shp), s0)
    o = rms_norm(o, g_out) * jax.nn.silu(r.reshape(B, L, GLA_HEADS, GLA_DV).astype(jnp.float32))
    return o.reshape(B, L, GLA_VD).astype(a.dtype) @ w_out, s_fin

def t5_rel_bias(n, table):
    n = jnp.maximum(n, 0)
    max_exact = N_BUCKETS // 2
    nf = jnp.maximum(n, 1).astype(jnp.float32)
    large = max_exact + (jnp.log(nf / max_exact) / math.log(MAX_DISTANCE / max_exact)
                         * (N_BUCKETS - max_exact)).astype(jnp.int32)
    bucket = jnp.where(n < max_exact, n, jnp.minimum(large, N_BUCKETS - 1))
    b = table.astype(jnp.float32)[bucket]
    return jnp.moveaxis(b, -1, 0).reshape(ATT_KV_HEADS, ATT_GROUP, *n.shape)

def sink_attend(q, k, v, bias, valid, sinks):
    s = jnp.einsum('bqngd,bknd->bngqk', q, k).astype(jnp.float32) * ATT_HEAD_DIM ** -0.5 + bias
    s = jnp.where(valid, s, -jnp.inf)
    sink = sinks.astype(jnp.float32)[None, :, :, None, None]
    m = jnp.maximum(jnp.max(s, axis=-1, keepdims=True), sink)
    p = jnp.exp(s - m)
    denom = jnp.sum(p, axis=-1, keepdims=True) + jnp.exp(sink - m)
    return jnp.einsum('bngqk,bknd->bqngd', (p / denom).astype(v.dtype), v)

def swa_prompt(q, k, v, table, sinks):
    B, S = q.shape[:2]
    nblk = S // WINDOW
    qb = jnp.moveaxis(q.reshape(B, nblk, WINDOW, ATT_KV_HEADS, ATT_GROUP, ATT_HEAD_DIM), 1, 0)
    kp = jnp.concatenate([jnp.zeros_like(k[:, :WINDOW]), k], axis=1)
    vp = jnp.concatenate([jnp.zeros_like(v[:, :WINDOW]), v], axis=1)
    qi = jnp.arange(WINDOW)[:, None]
    kj = jnp.arange(2 * WINDOW)[None, :]
    n = qi + WINDOW - kj
    band = (n >= 0) & (n < WINDOW)
    bias = t5_rel_bias(n, table)
    def one_block(args):
        qblk, i = args
        kblk = lax.dynamic_slice_in_dim(kp, i * WINDOW, 2 * WINDOW, axis=1)
        vblk = lax.dynamic_slice_in_dim(vp, i * WINDOW, 2 * WINDOW, axis=1)
        valid = band & ((i > 0) | (kj >= WINDOW))
        return sink_attend(qblk, kblk, vblk, bias, valid, sinks)
    o = lax.map(one_block, (qb, jnp.arange(nblk)))
    return jnp.moveaxis(o, 0, 1).reshape(B, S, D_ATT)

def swa_sample(q, k_all, v_all, table, sinks):
    B, L = q.shape[:2]
    qpos = PAST_LEN + jnp.arange(L)
    kpos = PAST_LEN - WIN_BUF + jnp.arange(k_all.shape[1])
    n = qpos[:, None] - kpos[None, :]
    valid = (n >= 0) & (n < WINDOW)
    o = sink_attend(q, k_all, v_all, t5_rel_bias(n, table), valid, sinks)
    return o.reshape(B, L, D_ATT)

def conv_ffn(x, prev, w_up, conv_w, conv_b, w_down):
    L = x.shape[1]
    up = x @ w_up
    u, val = up[..., :D_FF], up[..., D_FF:]
    u_pad = jnp.concatenate([prev.astype(u.dtype), u], axis=1)
    c = conv_b
    for j in range(CONV_W):
        c = c + conv_w[j] * u_pad[:, j:j + L]
    h = jax.nn.gelu(c, approximate=True) * val
    return h @ w_down, u_pad[:, -(CONV_W - 1):]

def trunk(x, gla_state, conv_state, k_buf, v_buf, p):
    prompt = k_buf is None
    B, L, _ = x.shape
    h = x
    new_gla, new_conv = [], []
    for l in range(DEPTH):
        a = rms_norm(h, p['g_mix_pre'][l])
        if l < N_A_LAYERS:
            s0 = jnp.zeros((B, GLA_HEADS, GLA_DK, GLA_DV), jnp.float32) if prompt else gla_state[l]
            m, s_fin = gla_mixer(a, s0, p['w_in_a'][l], p['w_gate_up'][l], p['b_gate'][l],
                                 p['g_gla_out'][l], p['w_out_a'][l])
            new_gla.append(s_fin)
        else:
            if l == N_A_LAYERS:
                kv = rms_norm(h, p['g_kv']) @ p['w_kv']
                k_new = kv[..., :KV_W].reshape(B, L, ATT_KV_HEADS, ATT_HEAD_DIM)
                v_new = kv[..., KV_W:].reshape(B, L, ATT_KV_HEADS, ATT_HEAD_DIM)
                if prompt:
                    k_all, v_all = k_new, v_new
                else:
                    k_all = jnp.concatenate([k_buf.astype(k_new.dtype), k_new], axis=1)
                    v_all = jnp.concatenate([v_buf.astype(v_new.dtype), v_new], axis=1)
                k_out, v_out = k_all[:, -WIN_BUF:], v_all[:, -WIN_BUF:]
            j = l - N_A_LAYERS
            q = (a @ p['w_q_b'][j]).reshape(B, L, ATT_KV_HEADS, ATT_GROUP, ATT_HEAD_DIM)
            sinks = p['sinks'][j].reshape(ATT_KV_HEADS, ATT_GROUP)
            if prompt:
                o = swa_prompt(q, k_all, v_all, p['rel_bias'], sinks)
            else:
                o = swa_sample(q, k_all, v_all, p['rel_bias'], sinks)
            m = o @ p['w_o_b'][j]
        h = h + rms_norm(m, p['g_mix_post'][l])
        prev = jnp.zeros((B, CONV_W - 1, D_FF), h.dtype) if prompt else conv_state[l]
        f, c_new = conv_ffn(rms_norm(h, p['g_ffn_pre'][l]), prev, p['w_up'][l], p['conv_w'][l],
                            p['conv_b'][l], p['w_down'][l])
        new_conv.append(c_new)
        h = h + rms_norm(f, p['g_ffn_post'][l])
    return h, jnp.stack(new_gla), jnp.stack(new_conv), k_out, v_out

def setup_inputs(seed: int = 0) -> dict:
    key = jax.random.key(seed)
    keys = list(jax.random.split(key, 32))
    def nrm(shape, scale):
        return scale * jax.random.normal(keys.pop(), shape, jnp.float32)
    def gain(shape):
        return 1.0 + 0.05 * jax.random.normal(keys.pop(), shape, jnp.float32)
    out = {}
    out['x_prompt'] = nrm((BATCH, SEQ, D_MODEL), 1.0)
    out['x_sample'] = nrm((DEC_BATCH, DEC_SEQ, D_MODEL), 1.0)
    out['state_gla'] = nrm((N_A_LAYERS, DEC_BATCH, GLA_HEADS, GLA_DK, GLA_DV), 0.5)
    out['cache_conv'] = nrm((DEPTH, DEC_BATCH, CONV_W - 1, D_FF), 1.0)
    out['cache_k_win'] = nrm((DEC_BATCH, WIN_BUF, ATT_KV_HEADS, ATT_HEAD_DIM), 1.0)
    out['cache_v_win'] = nrm((DEC_BATCH, WIN_BUF, ATT_KV_HEADS, ATT_HEAD_DIM), 1.0)
    out['g_mix_pre'] = gain((DEPTH, D_MODEL))
    out['g_mix_post'] = gain((DEPTH, D_MODEL))
    out['g_ffn_pre'] = gain((DEPTH, D_MODEL))
    out['g_ffn_post'] = gain((DEPTH, D_MODEL))
    out['w_in_a'] = nrm((N_A_LAYERS, D_MODEL, GLA_IN), D_MODEL ** -0.5)
    out['w_gate_up'] = nrm((N_A_LAYERS, GLA_GATE_RANK, GLA_QK), GLA_GATE_RANK ** -0.5)
    out['b_gate'] = nrm((N_A_LAYERS, GLA_QK), 0.1)
    out['g_gla_out'] = gain((N_A_LAYERS, GLA_DV))
    out['w_out_a'] = nrm((N_A_LAYERS, GLA_VD, D_MODEL), GLA_VD ** -0.5)
    out['g_kv'] = gain((D_MODEL,))
    out['w_kv'] = nrm((D_MODEL, 2 * KV_W), D_MODEL ** -0.5)
    out['rel_bias'] = nrm((N_BUCKETS, ATT_HEADS), 0.5)
    out['w_q_b'] = nrm((N_B_LAYERS, D_MODEL, D_ATT), D_MODEL ** -0.5)
    out['sinks'] = nrm((N_B_LAYERS, ATT_HEADS), 0.5)
    out['w_o_b'] = nrm((N_B_LAYERS, D_ATT, D_MODEL), D_ATT ** -0.5)
    out['w_up'] = nrm((DEPTH, D_MODEL, 2 * D_FF), D_MODEL ** -0.5)
    out['conv_w'] = nrm((DEPTH, CONV_W, D_FF), CONV_W ** -0.5)
    out['conv_b'] = nrm((DEPTH, D_FF), 0.02)
    out['w_down'] = nrm((DEPTH, D_FF, D_MODEL), D_FF ** -0.5)
    return out

def reference(x_prompt, x_sample, state_gla, cache_conv, cache_k_win, cache_v_win,
              g_mix_pre, g_mix_post, g_ffn_pre, g_ffn_post,
              w_in_a, w_gate_up, b_gate, g_gla_out, w_out_a,
              g_kv, w_kv, rel_bias, w_q_b, sinks, w_o_b,
              w_up, conv_w, conv_b, w_down):
    p = {'g_mix_pre': g_mix_pre, 'g_mix_post': g_mix_post, 'g_ffn_pre': g_ffn_pre,
         'g_ffn_post': g_ffn_post, 'w_in_a': w_in_a, 'w_gate_up': w_gate_up, 'b_gate': b_gate,
         'g_gla_out': g_gla_out, 'w_out_a': w_out_a, 'g_kv': g_kv, 'w_kv': w_kv,
         'rel_bias': rel_bias, 'w_q_b': w_q_b, 'sinks': sinks, 'w_o_b': w_o_b,
         'w_up': w_up, 'conv_w': conv_w, 'conv_b': conv_b, 'w_down': w_down}
    y_prompt, gla_p, conv_p, k_win_p, v_win_p = trunk(x_prompt, None, None, None, None, p)
    y_sample, gla_s, conv_s, k_win_s, v_win_s = trunk(x_sample, state_gla, cache_conv,
                                                      cache_k_win, cache_v_win, p)
    return (y_prompt, y_sample, gla_p, gla_s, conv_p, conv_s, k_win_p, k_win_s, v_win_p, v_win_s)


_drawn_inputs = setup_inputs


def setup_inputs(seed=0):
    import zlib

    import numpy as np

    out = dict(_drawn_inputs(seed))
    spreads = {}
    factors = {'sinks': 8.0, 'conv_b': 3.24}
    for name, (base, spread) in spreads.items():
        noise = np.random.default_rng([zlib.crc32(name.encode()), seed]).standard_normal(out[name].shape)
        drawn = base * np.exp(spread * noise) if base else spread * noise
        out[name] = __import__('jax').numpy.asarray(drawn.astype(out[name].dtype))
    for name, factor in factors.items():
        out[name] = (out[name] * factor).astype(out[name].dtype)
    return out
```

```python
import math
from contextlib import ExitStack

import numpy as np

import concourse.bass as bass
from concourse import mybir

fp32 = mybir.dt.float32
fp32r = mybir.dt.float32r
bf16 = mybir.dt.bfloat16
ALU = mybir.AluOpType
ACT = mybir.ActivationFunctionType
AX = mybir.AxisListType

P = 128
D = 1024
KT = D // P
SEQ, NB, LS = 1024, 8, 4
SAMP = NB * LS
T = SEQ + SAMP
NC, CW = 3, T // 3
H, DK, DV = 4, 128, 256
RANK = 16
CH = 128
NCHUNK = SEQ // CH
TAU = 16.0
LEVELS = (64, 32, 16, 8)
FINE = 8
GATE_FLOOR = -20.0 * TAU
HD, NQ, NKV = 64, 16, 2
WIN = 128
NBLK = SEQ // WIN
FF = 2816
FT = FF // P
FG = FT // 2
UP = 2 + SEQ
UW = UP + NB * (2 + LS)
CV = UW - 2
EPS = 1e-6
NEG = -1e30
RL = 383
HW = 9

G_MIX_PRE, G_MIX_POST, G_FFN_PRE, G_FFN_POST, G_KV, G_GLA = 0, 16, 32, 48, 64, 72
NGAIN = 74

W_GLR = 0
W_M0 = 1
W_F0 = W_M0 + H * HW
W_KV = W_F0 + FT * 3
W_M1 = W_KV + 3
W_F1 = W_M1 + NKV * HW
W_END = W_F1 + FT * 3 + 1


def build(nc, wall, xT, gains, ffnpar, wgate, state, kcT, vc, ck, cv, onehot, masks, smask, bmask,
          scanm, ident_in, bmask4, smask4, table, sinks,
          yT, gla_p, gla_s, conv_new, kwin_p, kwin_s, vwin_p, vwin_s):
    h_dram = nc.dram_tensor("h_scratch", [NC, P, KT, CW], fp32, kind="Internal").ap()
    r_dram = nc.dram_tensor("bias_scratch", [NQ * P * RL], fp32, kind="Internal").ap()
    kt_dram = nc.dram_tensor("kt_scratch", [P, T], fp32, kind="Internal").ap()
    v_dram = nc.dram_tensor("v_scratch", [T, P], fp32, kind="Internal").ap()

    ctx = ExitStack()
    with ctx:
        base = nc.sbuf_base
        at = [((base if isinstance(base, int) else base()) + 31) // 32 * 32]
        top = {"at": 0}

        def place(name, shape, dt=fp32, offset=None):
            size = math.prod(shape[1:]) * (2 if dt == bf16 else 4)
            size = (size + 31) // 32 * 32
            off = at[0] if offset is None else offset
            if offset is None:
                at[0] += size
            top["at"] = max(top["at"], off + size)
            return nc.alloc_sbuf_tensor_at(name, shape, dt, offset=off)

        def sem(name):
            return ctx.enter_context(nc.semaphore(name))

        AH_AT = at[0]
        AH = place("act_hi", [P, KT, T], fp32r)
        AL = place("act_lo", [P, KT, T], fp32r)
        AC_AT = at[0]
        ACC = place("acc", [P, NC, KT, CW])
        WR = place("w_raw", [P, 3, KT * P])
        WH = place("w_hi", [P, 3, KT * P], fp32r)
        WL = place("w_lo", [P, 3, KT * P], fp32r)
        ident = place("ident", [P, P])
        ones = place("ones", [P, P])
        GC = place("gain_cols", [P, NGAIN])
        SINK = place("sinks_b", [P, NQ])
        arena = at[0]

        HC = place("h_chunk", [P, NC, KT, CW])
        SQ = place("squares", [P, 2, KT, CW])
        RS = place("rstd", [P, NC, CW])
        

        at[0] = arena
        Qb = at[0]
        Q = place("gq", [P, T])
        K = place("gk", [P, T])
        Z = place("gb", [P, T])
        B8 = place("gb8", [P, T])
        OH0 = place("go_hi", [P, 2, T], fp32r, offset=Qb)
        OL0 = place("go_lo", [P, 2, T], fp32r, offset=Qb + 2 * T * 4)
        KD = place("gkd", [P, NCHUNK, P], offset=Qb + T * 4)
        KDS = place("gkd_s", [SAMP, P], offset=Qb)
        S = place("gstate", [P, DV], offset=Qb + 2 * T * 4)
        KDM = place("gkd_masked", [SAMP, NB, P], offset=Qb + 3 * T * 4)
        Tb = at[0]
        T1 = place("gt1", [P, T])
        KTl = place("gkt", [P, T])
        SB = place("gstates", [P, NB, DV], offset=Tb)
        QTb = at[0]
        QT = place("gqt", [P, T])
        AT = place("gat", [P, T])
        SQ0 = place("gsq", [P, 2, T], offset=QTb)
        Vb = at[0]
        V = place("gv", [P, 9, DV])
        RS0 = place("grs", [P, T], offset=Vb)
        R = place("gr", [P, 2, T])
        O = place("go", [P, 2, T])
        GLR = place("glr", [RANK + 1, T])
        WG = place("wgate", [RANK + 1, P])
        EL = place("gel", [P, 16])
        MLEV = place("mlev", [P, 5, CH], bf16)
        SMASK = place("smask_t", [SAMP, SAMP], bf16)
        BMASK = place("bmask_t", [SAMP, NB])
        SCM = place("scan_masks", [P, 2, T], bf16)
        

        at[0] = arena
        U = place("u", [P, UW])
        C = place("c", [P, UW])
        HF = place("hf", [P, T])
        HH = place("h_hi", [P, 2, T], fp32r)
        HL = place("h_lo", [P, 2, T], fp32r)
        PAR = place("par", [P, FT, 20])
        PC = place("par_tile", [P, 20])
        CN = place("conv_new_t", [P, FT, 18])
        

        at[0] = arena + (NC + 2) * KT * CW * 4 + NC * CW * 4 + 64
        KTT = place("kT", [P, T])
        VTT = place("vT", [P, T])
        KVTOK = place("kv_tok", [P, 11, P], offset=arena + NC * KT * CW * 4)
        at[0] = AC_AT
        TBB = place("table_cols", [33, NQ, P])
        RB = place("bias_rows", [P, NQ, RL])
        at[0] = AH_AT
        OHR = place("onehot_t", [33, RL])
        TBL = place("table_t", [33, NQ])
        at[0] = arena
        KG = place("kg", [P, T])
        KCG = place("kcg", [P, NB, WIN])
        VG = place("vg", [P, 9, HD])
        VCG = place("vcg", [P, NB, HD])
        Q1 = place("q1", [P, 2, T])
        BI = place("bias", [P, 4, 2 * WIN])
        SS = place("scores", [P, 2, 2, 2 * WIN])
        PT = place("probs_t", [P, 2, 4, P])
        OT = place("o_tok", [P, 2, P])
        OH1 = place("o_hi", [P, 2, T], fp32r)
        OL1 = place("o_lo", [P, 2, T], fp32r)
        ST = place("stats", [P, 2, 16])
        SX = place("s_scores", [P, T])
        PX = place("s_probs_t", [P, NB, P])
        PXN = place("s_probs_new_t", [SAMP, P])
        SBC = place("s_bias", [P, WIN + LS])
        BM4 = place("s_mask", [P, NB])
        SM4 = place("s_mask_new", [P, SAMP])
        SKS = place("s_sinks", [P, NKV * 2])
        SKG = place("sinks_group", [P, 8])

        PS = ctx.enter_context(nc.psum_tensor("banks", [P, 8, 512], fp32))

        c_in = sem("constants_in")
        one = sem("ones_set")
        w_in = [sem(f"w_in{i}") for i in range(3)]
        w_hi, w_lo = sem("w_hi_done"), sem("w_lo_done")
        tb_one, tb_in, tb_cols = sem("table_ones"), sem("table_in"), sem("table_cols_done")
        rb_full, rb_row, rb_out = sem("bias_row_full"), sem("bias_row_copied"), sem("bias_rows_out")
        h_in = [sem(f"h_in{c}") for c in range(NC)]
        h_out = [sem(f"h_out{c}") for c in range(NC)]
        sq_done, ss_done, ms_done = sem("squares_done"), sem("square_sums_done"), sem("mean_squares_done")
        rs_done, po_done, ha_done = sem("rstd_done"), sem("post_norm_done"), sem("residual_done")
        nm_done, ah_done, al_done = sem("pre_norm_done"), sem("act_hi_done"), sem("act_lo_done")
        az_done = sem("acc_zeroed")
        dn_full, dn_add = sem("down_full"), sem("down_added")
        glr_full, glr_ev = sem("glr_full"), sem("glr_copied")
        m0c_in, wg_in = sem("m0_constants_in"), sem("wgate_in")
        m0_full, m0_ev = sem("gla_proj_full"), sem("gla_proj_copied")
        az, ln = sem("gate_abs"), sem("gate_log")
        gt = sem("gate_made")
        cs = sem("gate_summed")
        lv_d, lv_e, lv_qk, lv_pe, lv_m, lv_a = (sem(f"level_{x}") for x in ("diff", "exp", "qk", "scores", "masked", "added"))
        in_d, in_e, in_qk = sem("inter_diff"), sem("inter_exp"), sem("inter_qk")
        vt_full, vt_ev, kd_full, kd_ev, kdm = (sem(x) for x in ("v_tok_full", "v_tok_copied", "k_tok_full", "k_tok_copied", "k_masked"))
        st_in, st_out, gp_out = sem("states_in"), sem("states_out"), sem("gla_p_out")
        o_full, o_ev, s_full, s_upd = (sem(x) for x in ("o_full", "o_copied", "state_full", "state_updated"))
        os_full, os_ev, ss_full, ss_upd = (sem(x) for x in ("os_full", "os_copied", "sstate_full", "sstate_updated"))
        gq_sq, gq_ss, gq_ms, gq_rs, gq_si, gq_o, gq_h, gq_l = (sem("gn_" + x) for x in ("sq", "ss", "ms", "rs", "silu", "o", "hi", "lo"))
        fp_in, u0_set = sem("ffn_par_in"), sem("u_zeroed")
        pc, pre = sem("par_copied"), sem("prefix_copied")
        u_full, u_ev, v_full, h_made = sem("u_full"), sem("u_copied"), sem("val_full"), sem("h_made")
        cb, cv1, cv2, cn, gl, hh, hl = (sem("ffn_" + x) for x in ("bias", "conv1", "conv2", "cache", "gelu", "hi", "lo"))
        cn_out = sem("conv_new_out")
        kv_full, kv_ev, kt_full, kt_ev = sem("kv_full"), sem("kv_copied"), sem("kvt_full"), sem("kvt_copied")
        kw_out, kv_out = sem("windows_out"), sem("kv_out")
        kg_in, bi_in, a_c_in = sem("kv_head_in"), sem("bias_in"), sem("attn_constants_in")
        skg = sem("sinks_copied")
        q_full, q_ev = sem("q_full"), sem("q_copied")
        sf, sa, mx, mm_, nm, ex, es, den, rc = (sem("att_" + x) for x in ("scores", "biased", "max", "maxsink", "negmax", "exp", "expsink", "den", "rden"))
        tf, te, of, on, xf, xh, xl = (sem("att_" + x) for x in ("pt", "pt_copied", "o", "o_scaled", "ot", "hi", "lo"))
        xsf, xsa, xsb, xmx, xex, xrc, xsc, xtf, xte, xof, xoh, xol = (sem("samp_" + x) for x in ("scores", "biased", "masked", "max", "exp", "rden", "scaled", "pt", "pt_copied", "o", "hi", "lo"))

        def chunk(c):
            return slice(c * CW, (c + 1) * CW)

        def col(x):
            return GC[:, x:x + 1]

        def bc(ap, n):
            shape = list(ap.shape)
            return ap.unsqueeze(len(shape)).broadcast_to(shape + [n])

        steps = []
        n_stat = n_all = n_act = n_post = 0
        for B in range(5):
            kinds = {0: ["pre0", "pre1", "pre2"],
                     1: ["post0", "post1", "pre0", "post2", "pre1", "pre2"],
                     2: ["post0", "post1", "kv0", "post2", "kv1", "kv2", "mix0", "mix1", "mix2"],
                     3: ["post0", "post1", "pre0", "post2", "pre1", "pre2"],
                     4: ["post0", "post1", "post2"]}[B]
            here = []
            for k in kinds:
                kind, c = k[:-1], int(k[-1])
                here.append(dict(kind=kind, c=c, stat=n_stat, k=n_all, act=n_act, post=n_post))
                n_all += 1
                n_stat += kind != "mix"
                n_act += kind != "post"
                n_post += kind == "post"
            steps.append(here)
        flat = [s for b in steps for s in b]
        ACTS = [sum(s["kind"] != "post" for b in steps[:B + 1] for s in b) for B in range(5)]
        STATS = [sum(s["kind"] != "mix" for b in steps[:B + 1] for s in b) for B in range(5)]
        POSTS = [sum(s["kind"] == "post" for b in steps[:B + 1] for s in b) for B in range(5)]
        DOWNS = [0, H, H + FG, H + FG + 2 * NKV, H + 2 * FG + 2 * NKV]
        POST_G = {1: G_MIX_POST, 2: G_FFN_POST, 3: G_MIX_POST + 8, 4: G_FFN_POST + 8}
        PRE_G = {(0, "pre"): G_MIX_PRE, (1, "pre"): G_FFN_PRE, (2, "kv"): G_KV, (2, "mix"): G_MIX_PRE + 8,
                 (3, "pre"): G_FFN_PRE + 8}

        def free_squares(eng, k):
            if k >= 2:
                p = flat[k - 2]
                if p["kind"] == "post":
                    eng.wait_ge(ss_done, p["stat"] + 1)
                else:
                    eng.wait_ge(al_done, p["act"] + 1)

        def act_boundary(act, B):
            for s in steps[B]:
                c, k = s["c"], s["k"]
                if s["kind"] == "post":
                    act.wait_ge(dn_add, 24 * DOWNS[B] - 24 + 8 * (c + 1))
                    free_squares(act, k)
                    nc.scalar.activation(SQ[:, k % 2], ACC[:, c], ACT.Square).then_inc(sq_done, 1)
                elif s["kind"] != "mix":
                    if B == 0:
                        act.wait_ge(h_in[c], 16)
                    else:
                        act.wait_ge(ha_done, POSTS[B - 1] + c + 1)
                    free_squares(act, k)
                    nc.scalar.activation(SQ[:, k % 2], HC[:, c], ACT.Square).then_inc(sq_done, 1)
                if s["kind"] != "mix":
                    act.wait_ge(ms_done, 2 * s["stat"] + 2)
                    nc.scalar.activation(RS[:, c], RS[:, c], ACT.Sqrt).then_inc(rs_done, 1)
                if s["kind"] != "post":
                    act.wait_ge(nm_done, s["act"] + 1)
                    if s["kind"] == "mix":
                        act.wait_ge(kv_full, 2 * c + 2)
                    nc.scalar.activation(AH[:, :, chunk(c)], SQ[:, k % 2], ACT.Copy).then_inc(ah_done, 1)

        def dve_boundary(dve, B):
            for s in steps[B]:
                c, k = s["c"], s["k"]
                if s["kind"] != "mix":
                    dve.wait_ge(ss_done, s["stat"] + 1)
                    nc.vector.tensor_scalar(RS[:, c], PS[:, 6 + s["stat"] % 2, 0:CW], 1.0 / D, EPS,
                                            ALU.mult, ALU.add).then_inc(ms_done, 1)
                    dve.wait_ge(ms_done, 2 * s["stat"] + 1)
                    nc.vector.reciprocal(RS[:, c], RS[:, c]).then_inc(ms_done, 1)
                    dve.wait_ge(rs_done, s["stat"] + 1)
                if s["kind"] == "post":
                    for n in range(KT):
                        g = POST_G[B] + n
                        last = nc.vector.scalar_tensor_tensor(ACC[:, c, n], ACC[:, c, n], col(g), RS[:, c],
                                                              ALU.mult, ALU.mult)
                    last.then_inc(po_done, 1)
                    dve.wait_ge(po_done, s["post"] + 1)
                    dve.wait_ge(h_in[c], 16 * (B + 1))
                    nc.vector.tensor_tensor(HC[:, c], HC[:, c], ACC[:, c], ALU.add).then_inc(ha_done, 1)
                else:
                    if s["kind"] == "mix":
                        free_squares(dve, k)
                    for n in range(KT):
                        g = PRE_G[B, s["kind"]] + n
                        last = nc.vector.scalar_tensor_tensor(SQ[:, k % 2, n], HC[:, c, n], col(g), RS[:, c],
                                                              ALU.mult, ALU.mult)
                    last.then_inc(nm_done, 1)

        def pool_boundary(pool, B):
            for s in steps[B]:
                c, k = s["c"], s["k"]
                if s["kind"] != "post":
                    pool.wait_ge(ah_done, s["act"] + 1)
                    nc.gpsimd.tensor_tensor(AL[:, :, chunk(c)], SQ[:, k % 2],
                                            AH[:, :, chunk(c)].bitcast(fp32), ALU.subtract).then_inc(al_done, 1)
            if B < 4:
                if B:
                    pool.wait_ge(ha_done, POSTS[B])
                else:
                    pool.wait_ge(rb_out, 16)
                nc.gpsimd.memset(ACC[:], 0.0).then_inc(az_done, 1)

        def pe_boundary(pe, B):
            for s in steps[B]:
                if s["kind"] != "mix":
                    st = s["stat"]
                    pe.wait_ge(sq_done, st + 1)
                    if st >= 2:
                        pe.wait_ge(ms_done, 2 * (st - 2) + 1)
                    if B:
                        pe.wait_ge(dn_add, 24 * DOWNS[B])
                    for n in range(KT):
                        last = nc.tensor.matmul(PS[:, 6 + st % 2, 0:CW], ones[:], SQ[:, s["k"] % 2, n],
                                                start=(n == 0), stop=(n == KT - 1))
                    last.then_inc(ss_done, 1)
                if s["kind"] == "kv":
                    pe_kv(pe, s["c"], s["act"])

        def sp_boundary(sp, B):
            if B == 1:
                sp.wait_ge(st_out, 16 * H)
                sp.wait_ge(gp_out, 16 * H)
            if B < 4:
                for c in range(NC):
                    if B:
                        sp.wait_ge(dn_add, 24 * DOWNS[B])
                        src = xT[c] if B == 1 else h_dram[c]
                    else:
                        src = xT[c]
                    if B > 1:
                        sp.wait_ge(h_out[c], 16 * (B - 1))
                    sp.dma_start(HC[:, c], src).then_inc(h_in[c], 16)
                if B:
                    for c in range(NC):
                        sp.wait_ge(ha_done, POSTS[B - 1] + c + 1)
                        sp.dma_start(h_dram[c], HC[:, c]).then_inc(h_out[c], 16)
            else:
                for c in range(NC):
                    sp.wait_ge(dn_add, 24 * DOWNS[B])
                    sp.wait_ge(h_out[c], 16 * (B - 1))
                    sp.dma_start(HC[:, c], h_dram[c]).then_inc(h_in[c], 16)
                for c in range(NC):
                    sp.wait_ge(ha_done, POSTS[B - 1] + c + 1)
                    sp.dma_start(yT[c], HC[:, c]).then_inc(h_out[c], 16)

        def w_load(sp, b, slot):
            sp.wait_ge(w_lo, b - 2)
            sp.dma_start(WR[:, slot], wall[bass.ds(b, 1)].rearrange("a p n -> p (a n)")).then_inc(w_in[slot], 16)

        def w_round(act, b, third, slot):
            act.wait_ge(w_in[slot], 16 * third + 16)
            nc.scalar.activation(WH[:, slot], WR[:, slot], ACT.Copy).then_inc(w_hi, 1)

        def w_rest(pool, b, slot):
            pool.wait_ge(w_hi, b + 1)
            nc.gpsimd.tensor_tensor(WL[:, slot], WR[:, slot], WH[:, slot].bitcast(fp32),
                                    ALU.subtract).then_inc(w_lo, 1)

        def w_rests(pool, first, end):
            b = first
            while b < end and b % 3:
                w_rest(pool, b, b % 3)
                b += 1
            whole = (end - b) // 3
            if whole > 0:
                with pool.Fori(0, whole) as i:
                    for s in range(3):
                        w_rest(pool, 3 * i + b + s, s)
            for x in range(b + 3 * max(whole, 0), end):
                w_rest(pool, x, x % 3)

        def w_loads(sp, first, end):
            b = first
            while b < end and b % 3:
                w_load(sp, b, b % 3)
                b += 1
            whole = (end - b) // 3
            if whole > 0:
                with sp.Fori(0, whole) as i:
                    for s in range(3):
                        w_load(sp, 3 * i + b + s, s)
            for x in range(b + 3 * max(whole, 0), end):
                w_load(sp, x, x % 3)

        def project(pe, bank, slot, c, full, hi=None, lo=None):
            for k in range(KT):
                wh, wl = WH[:, slot, k * P:(k + 1) * P], WL[:, slot, k * P:(k + 1) * P]
                for w, a, first in ((wl, AH, True), (wh, AL, False), (wh, AH, False)):
                    last = nc.tensor.matmul(PS[:, bank, 0:CW], w, a[:, k, chunk(c)],
                                            start=(k == 0 and first), stop=(k == KT - 1 and w is wh and a is AH))
            last.then_inc(full, 1)

        def down(pe, slots, hi, lo, n_before, idle=False):
            for c in range(NC):
                for n in range(KT):
                    m = c * KT + n
                    if m >= 2 or not idle:
                        pe.wait_ge(dn_add, n_before + max(m - 1, 0))
                    for t in range(2):
                        wh = WH[:, slots[t], n * P:(n + 1) * P]
                        wl = WL[:, slots[t], n * P:(n + 1) * P]
                        for x, (w, a) in enumerate(((wl, hi), (wh, lo), (wh, hi))):
                            last = nc.tensor.matmul(PS[:, 6 + m % 2, 0:CW], w, a[:, t, chunk(c)],
                                                    start=(t == 0 and x == 0), stop=(t == 1 and x == 2))
                    last.then_inc(dn_full, 1)

        def down_add(dve, n_before):
            for m in range(NC * KT):
                dve.wait_ge(dn_full, n_before + m + 1)
                a = ACC[:, m // KT, m % KT]
                nc.vector.tensor_tensor(a, a, PS[:, 6 + m % 2, 0:CW], ALU.add).then_inc(dn_add, 1)

        def pe_gla(pe):
            pe.wait_ge(w_lo, W_GLR + 1)
            for c in range(NC):
                pe.wait_ge(al_done, c + 1)
                project(pe, c, W_GLR % 3, c, glr_full)
            pe.wait_ge(m0c_in, 16 * 4)
            pe.wait_ge(glr_ev, NC + 1)
            with pe.Fori(0, H) as h:
                b0 = HW * h + W_M0
                slot = [(W_M0 + p) % 3 for p in range(HW)]

                def level(n):
                    pe.wait_ge(lv_qk, 5 * h + n + 1)
                    if n:
                        pe.wait_ge(lv_m, 5 * h + n)
                    for c in range(NCHUNK):
                        x = slice(c * CH, (c + 1) * CH)
                        last = nc.tensor.matmul(PS[:, 6 + c // 4, (c % 4) * CH:(c % 4 + 1) * CH], KTl[:, x], QT[:, x],
                                                start=True, stop=True)
                    if n == 4:
                        x = slice(SEQ, T)
                        last = nc.tensor.matmul(PS[0:SAMP, 5, 0:SAMP], KTl[:, x], QT[:, x], start=True, stop=True)
                    last.then_inc(lv_pe, 1)

                pe.wait_ge(wg_in, 16 * h + 16)
                for c in range(NC):
                    nc.tensor.matmul(PS[:, 3 + c, 0:CW], WG[:], GLR[:, chunk(c)], start=True, stop=True).then_inc(m0_full, 1)
                for p in range(6):
                    pe.wait_ge(w_lo, b0 + p + 1)
                    for c in range(NC):
                        x = 3 + 3 * p + c
                        if p:
                            pe.wait_ge(m0_ev, 21 * h + x - 5)
                        project(pe, 3 * (p % 2) + c, slot[p], c, m0_full)
                    if p >= 2:
                        level(p - 2)
                pe.wait_ge(m0_ev, 21 * h + 21)
                for i in range(9):
                    n = CH if i < 8 else SAMP
                    for d in range(2):
                        last = nc.tensor.transpose(PS[0:n, i // 2, (i % 2) * DV + d * P:(i % 2) * DV + (d + 1) * P],
                                                   O[:, d, i * CH:i * CH + n], ident[:])
                last.then_inc(vt_full, 1)
                level(4)
                pe.wait_ge(in_qk, 2 * h + 1)
                pe.wait_ge(lv_a, 4 * h + 4)
                for c in range(NCHUNK):
                    nc.tensor.transpose(PS[:, 6 + c // 4, (c % 4) * CH:(c % 4 + 1) * CH], KTl[:, c * CH:(c + 1) * CH], ident[:])
                nc.tensor.transpose(PS[0:SAMP, 5, 0:P], KTl[:, SEQ:T], ident[:]).then_inc(kd_full, 1)
                pe.wait_ge(lv_a, 4 * h + 4)
                pe.wait_ge(in_qk, 2 * h + 2)
                pe.wait_ge(vt_ev, h + 1)
                pe.wait_ge(kd_ev, h + 1)
                for c in range(NCHUNK):
                    x = slice(c * CH, (c + 1) * CH)
                    if c >= 2:
                        pe.wait_ge(o_ev, 8 * h + c - 1)
                    if c:
                        pe.wait_ge(s_upd, 8 * h + c)
                    for d in range(2):
                        out = PS[:, c % 2, d * CH:(d + 1) * CH]
                        if c:
                            nc.tensor.matmul(out, S[:, d * P:(d + 1) * P], QT[:, x], start=True, stop=False)
                        last = nc.tensor.matmul(out, V[:, c, d * P:(d + 1) * P], AT[:, x], start=(c == 0), stop=True)
                    last.then_inc(o_full, 1)
                    nc.tensor.matmul(PS[:, 2 + c % 2, 0:DV], KD[:, c], V[:, c], start=True, stop=True).then_inc(s_full, 1)
                pe.wait_ge(st_in, 16 * h + 16)
                pe.wait_ge(vt_ev, h + 1)
                for d in range(2):
                    nc.tensor.matmul(PS[:, 4 + d, 0:SAMP], V[0:SAMP, 8, d * P:(d + 1) * P],
                                     AT[0:SAMP, SEQ:T], start=True, stop=False, skip_group_check=True)
                    for b in range(NB):
                        x = b * LS
                        last = nc.tensor.matmul(PS[:, 4 + d, x:x + LS], SB[:, b, d * P:(d + 1) * P],
                                                QT[:, SEQ + b * LS:SEQ + (b + 1) * LS], start=False, stop=(b == NB - 1),
                                                skip_group_check=True)
                last.then_inc(os_full, 1)
                pe.wait_ge(kdm, h + 1)
                for b in range(NB):
                    if b >= 2:
                        pe.wait_ge(ss_upd, 8 * h + b - 1)
                    nc.tensor.matmul(PS[:, 6 + b % 2, 0:DV], KDM[:, b], V[0:SAMP, 8, :],
                                     start=True, stop=True).then_inc(ss_full, 1)
                pe.wait_ge(gq_sq, h + 1)
                pe.wait_ge(s_upd, 8 * h + 8)
                for c in range(NC):
                    for d in range(2):
                        last = nc.tensor.matmul(PS[:, c, 0:CW], ones[:], SQ0[:, d, chunk(c)], start=(d == 0), stop=(d == 1))
                last.then_inc(gq_ss, 1)
                pe.wait_ge(gq_l, h + 1)
                pe.wait_ge(w_lo, b0 + 8)
                pe.wait_ge(ss_upd, 8 * h + 8)
                down(pe, (slot[6], slot[7]), OH0, OL0, 24 * h, idle=True)
                pe.wait_ge(dn_add, 24 * h + 24)

        def halves(buf, L):
            v = buf[:, 0:SEQ].rearrange("p (n s) -> p n s", s=2 * L)
            return v[:, :, 0:L], v[:, :, L:2 * L], v[:, :, L - 1:L]

        def dve_gla(dve):
            dve.wait_ge(al_done, ACTS[0])
            nc.vector.memset(GLR[:], 1.0).then_inc(glr_ev, 1)
            dve.wait_ge(m0c_in, 16 * 4)
            with dve.Fori(0, H) as h:
                dve.wait_ge(m0_ev, 21 * h + 3)
                nc.vector.scalar_tensor_tensor(T1[:], Z[:], -1.0, Z[:], ALU.mult, ALU.min).then_inc(az, 1)
                dve.wait_ge(ln, 2 * h + 2)
                nc.vector.scalar_tensor_tensor(Z[:], Z[:], 0.0, T1[:], ALU.min, ALU.subtract).then_inc(gt, 1)
                dve.wait_ge(gt, 2 * h + 1)
                nc.vector.tensor_scalar(B8[:], Z[:], GATE_FLOOR, None, ALU.max).then_inc(gt, 1)
                dve.wait_ge(gt, 2 * h + 2)
                nc.vector.tensor_tensor_scan(Z[:], SCM[:, 0], Z[:], 0.0, ALU.mult, ALU.add).then_inc(cs, 1)
                nc.vector.tensor_tensor_scan(B8[:], SCM[:, 1], B8[:], 0.0, ALU.mult, ALU.add).then_inc(cs, 1)
                dve.wait_ge(cs, 2 * h + 2)
                for n, L in enumerate(LEVELS):
                    left, right, ref = halves(Z, L)
                    tl, tr, _ = halves(T1, L)
                    shape = list(left.shape)
                    if n == 1:
                        dve.wait_ge(lv_m, 5 * h + 1)
                    if n >= 2:
                        dve.wait_ge(lv_a, 4 * h + n - 1)
                    nc.vector.tensor_tensor(tl, ref.broadcast_to(shape), left, ALU.subtract)
                    nc.vector.tensor_tensor(tr, right, ref.broadcast_to(shape), ALU.subtract).then_inc(lv_d, 1)
                    dve.wait_ge(lv_e, 5 * h + n + 1)
                    if n:
                        dve.wait_ge(lv_pe, 5 * h + n)
                    else:
                        dve.wait_ge(m0_ev, 21 * h + 9)
                    nc.vector.tensor_tensor(QT[:, 0:SEQ], Q[:, 0:SEQ], T1[:, 0:SEQ], ALU.mult)
                    nc.vector.tensor_tensor(KTl[:, 0:SEQ], K[:, 0:SEQ], T1[:, 0:SEQ], ALU.mult).then_inc(lv_qk, 1)
                    dve.wait_ge(lv_qk, 5 * h + n + 1)
                    mask_scores(dve, h, n)
                f = B8[:, 0:SEQ].rearrange("p (n s) -> p n s", s=FINE)
                o = T1[:, 0:SEQ].rearrange("p (n s) -> p n s", s=FINE)
                dve.wait_ge(lv_a, 4 * h + 3)
                nc.vector.tensor_tensor(o, f, f[:, :, FINE // 2 - 1:FINE // 2].broadcast_to(list(f.shape)), ALU.subtract)
                f = B8[:, SEQ:T].rearrange("p (n s) -> p n s", s=LS)
                o = T1[:, SEQ:T].rearrange("p (n s) -> p n s", s=LS)
                nc.vector.tensor_tensor(o, f, f[:, :, 1:2].broadcast_to(list(f.shape)), ALU.subtract).then_inc(lv_d, 1)
                dve.wait_ge(lv_e, 5 * h + 5)
                nc.vector.tensor_tensor(QT[:], Q[:], QT[:], ALU.mult)
                nc.vector.tensor_tensor(KTl[:], K[:], KTl[:], ALU.mult).then_inc(lv_qk, 1)
                mask_scores(dve, h, 4)
                f = Z[:, 0:SEQ].rearrange("p (n s) -> p n s", s=CH)
                o = T1[:, 0:SEQ].rearrange("p (n s) -> p n s", s=CH)
                dve.wait_ge(lv_a, 4 * h + 4)
                nc.vector.tensor_tensor(o, f[:, :, CH - 1:CH].broadcast_to(list(f.shape)), f, ALU.subtract)
                f = Z[:, SEQ:T].rearrange("p (n s) -> p n s", s=LS)
                o = T1[:, SEQ:T].rearrange("p (n s) -> p n s", s=LS)
                nc.vector.tensor_tensor(o, f[:, :, LS - 1:LS].broadcast_to(list(f.shape)), f, ALU.subtract).then_inc(in_d, 1)
                dve.wait_ge(in_e, h + 1)
                nc.vector.tensor_tensor(KTl[:], K[:], T1[:], ALU.mult).then_inc(in_qk, 1)
                nc.vector.tensor_tensor(QT[:], Q[:], QT[:], ALU.mult).then_inc(in_qk, 1)
                dve.wait_ge(kd_ev, h + 1)
                nc.vector.tensor_tensor(KDM[:], KDS[:].unsqueeze(1).broadcast_to([SAMP, NB, P]), bc(BMASK[:], P),
                                        ALU.mult).then_inc(kdm, 1)
                for c in range(NCHUNK):
                    dve.wait_ge(s_full, 8 * h + c + 1)
                    if c == 0:
                        nc.vector.tensor_copy(S[:], PS[:, 2, 0:DV]).then_inc(s_upd, 1)
                    else:
                        dve.wait_ge(s_upd, 8 * h + c)
                        nc.vector.scalar_tensor_tensor(S[:], S[:], EL[:, c:c + 1], PS[:, 2 + c % 2, 0:DV],
                                                       ALU.mult, ALU.add).then_inc(s_upd, 1)
                for b in range(NB):
                    dve.wait_ge(ss_full, 8 * h + b + 1)
                    nc.vector.scalar_tensor_tensor(SB[:, b], SB[:, b], EL[:, 8 + b:9 + b], PS[:, 6 + b % 2, 0:DV],
                                                   ALU.mult, ALU.add).then_inc(ss_upd, 1)
                dve.wait_ge(gq_ss, h + 1)
                for c in range(NC):
                    nc.vector.tensor_scalar(RS0[:, chunk(c)], PS[:, c, 0:CW], 1.0 / DV, EPS, ALU.mult,
                                            ALU.add).then_inc(gq_ms, 1)
                for c in range(NC):
                    dve.wait_ge(gq_ms, 6 * h + c + 1)
                    nc.vector.reciprocal(RS0[:, chunk(c)], RS0[:, chunk(c)]).then_inc(gq_ms, 1)
                dve.wait_ge(gq_rs, h + 1)
                for d in range(2):
                    nc.vector.scalar_tensor_tensor(O[:, d], O[:, d], col(G_GLA + d), RS0[:], ALU.mult, ALU.mult).then_inc(gq_o, 1)
                dve.wait_ge(gq_o, 3 * h + 2)
                dve.wait_ge(gq_si, h + 1)
                nc.vector.tensor_tensor(O[:], O[:], R[:], ALU.mult).then_inc(gq_o, 1)
                dve.wait_ge(gq_h, h + 1)
                dve.wait_ge(gp_out, 16 * h + 16)
                nc.vector.tensor_tensor(OL0[:], O[:], OH0[:].bitcast(fp32), ALU.subtract).then_inc(gq_l, 1)
                dve.wait_ge(az_done, 1)
                down_add(dve, 24 * h)
                dve.wait_ge(st_out, 16 * h + 16)

        def mask_scores(dve, h, n):
            dve.wait_ge(lv_pe, 5 * h + n + 1)
            dst = AT if n == 0 else T1
            nc.vector.tensor_tensor(dst[:, 0:SEQ].rearrange("p (c i) -> p c i", i=CH),
                                             PS[:, 6:8].rearrange("p b (c i) -> p (b c) i", i=CH),
                                             MLEV[:, n:n + 1].broadcast_to([P, NCHUNK, CH]), ALU.mult).then_inc(lv_m, 1)
            if n == 4:
                nc.vector.tensor_tensor(AT[0:SAMP, SEQ:T], PS[0:SAMP, 5, 0:SAMP], SMASK[:], ALU.mult)
            if n:
                dve.wait_ge(lv_m, 5 * h + n + 1)
                nc.vector.tensor_tensor(AT[:, 0:SEQ], AT[:, 0:SEQ], T1[:, 0:SEQ], ALU.add).then_inc(lv_a, 1)

        def act_gla(act):
            act.wait_ge(al_done, ACTS[0])
            for c in range(NC):
                act.wait_ge(glr_full, c + 1)
                act.wait_ge(glr_ev, 1)
                nc.scalar.activation(GLR[0:RANK, chunk(c)], PS[0:RANK, c, 0:CW], ACT.Copy).then_inc(glr_ev, 1)
            w_round(act, 3, 1, 0)
            with act.Fori(0, H) as h:
                slot = [(W_M0 + p) % 3 for p in range(HW)]
                third = [(W_M0 + p) // 3 for p in range(2 * HW)]

                def copy(dst, x0, **kw):
                    for c in range(NC):
                        x = x0 + c
                        act.wait_ge(m0_full, 21 * h + x + 1)
                        nc.scalar.activation(dst[:, chunk(c)], PS[:, (x + 3) % 6, 0:CW], ACT.Copy, **kw).then_inc(m0_ev, 1)

                def round_next(p):
                    w_round(act, HW * h + W_M0 + p + 3, 3 * h + third[p + 3], slot[p])

                copy(Z, 0)
                act.wait_ge(az, h + 1)
                nc.scalar.activation(T1[:], T1[:], ACT.Exp).then_inc(ln, 1)
                act.wait_ge(ln, 2 * h + 1)
                nc.scalar.activation(T1[:], T1[:], ACT.Ln, bias=1.0).then_inc(ln, 1)
                copy(Q, 3, scale=DK ** -0.5)
                round_next(0)
                copy(K, 6)
                round_next(1)

                def level(n):
                    act.wait_ge(lv_d, 5 * h + n + 1)
                    x = slice(0, SEQ)
                    if n < 4:
                        nc.scalar.activation(T1[:, x], T1[:, x], ACT.Exp, scale=1.0 / TAU).then_inc(lv_e, 1)
                    else:
                        act.wait_ge(lv_pe, 5 * h + 4)
                        nc.scalar.activation(QT[:], T1[:], ACT.Exp, scale=1.0 / TAU)
                        nc.scalar.activation(KTl[:], T1[:], ACT.Exp, scale=-1.0 / TAU).then_inc(lv_e, 1)

                level(0)
                copy(O[:, 0], 9)
                round_next(2)
                level(1)
                copy(O[:, 1], 12)
                round_next(3)
                level(2)
                copy(R[:, 0], 15)
                round_next(4)
                level(3)
                copy(R[:, 1], 18)
                round_next(5)
                act.wait_ge(vt_full, h + 1)
                for i in range(4):
                    nc.scalar.activation(V[:, 2 * i:2 * i + 2], PS[:, i].rearrange("p (a n) -> p a n", a=2), ACT.Copy)
                nc.scalar.activation(V[0:SAMP, 8], PS[0:SAMP, 4, 0:DV], ACT.Copy).then_inc(vt_ev, 1)
                level(4)
                act.wait_ge(in_d, h + 1)
                nc.scalar.activation(T1[:], T1[:], ACT.Exp, scale=1.0 / TAU)
                nc.scalar.activation(EL[:, 0:8], Z[:, CH - 1:SEQ:CH], ACT.Exp, scale=1.0 / TAU)
                nc.scalar.activation(EL[:, 8:16], Z[:, SEQ + LS - 1:T:LS], ACT.Exp, scale=1.0 / TAU)
                act.wait_ge(lv_pe, 5 * h + 5)
                nc.scalar.activation(QT[:], Z[:], ACT.Exp, scale=1.0 / TAU).then_inc(in_e, 1)
                act.wait_ge(kd_full, h + 1)
                act.wait_ge(in_qk, 2 * h + 2)
                nc.scalar.activation(KD[:].rearrange("p c n -> p (c n)").rearrange("p (b x) -> p b x", b=2), PS[:, 6:8], ACT.Copy)
                nc.scalar.activation(KDS[:], PS[0:SAMP, 5, 0:P], ACT.Copy).then_inc(kd_ev, 1)
                act.dma_start(SB[:], state[bass.ds(h, 1)].rearrange("a k b v -> k (a b) v")).then_inc(st_in, 16)
                for c in range(NCHUNK):
                    act.wait_ge(o_full, 8 * h + c + 1)
                    nc.scalar.activation(O[:, :, c * CH:(c + 1) * CH],
                                         PS[:, c % 2, 0:2 * CH].rearrange("p (d i) -> p d i", d=2), ACT.Copy).then_inc(o_ev, 1)
                act.wait_ge(os_full, h + 1)
                nc.scalar.activation(O[:, :, SEQ:T], PS[:, 4:6, 0:SAMP], ACT.Copy).then_inc(os_ev, 1)
                act.wait_ge(s_upd, 8 * h + 8)
                act.dma_start(gla_p[bass.ds(h, 1)].rearrange("a k v -> k (a v)"), S[:]).then_inc(gp_out, 16)
                act.wait_ge(o_ev, 8 * h + 8)
                act.wait_ge(os_ev, h + 1)
                nc.scalar.activation(SQ0[:], O[:], ACT.Square).then_inc(gq_sq, 1)
                nc.scalar.activation(R[:], R[:], ACT.Silu).then_inc(gq_si, 1)
                act.wait_ge(ss_upd, 8 * h + 8)
                act.dma_start(gla_s[bass.ds(h, 1)].rearrange("a k b v -> k (a b) v"), SB[:]).then_inc(st_out, 16)
                act.wait_ge(gq_ms, 6 * h + 6)
                nc.scalar.activation(RS0[:], RS0[:], ACT.Sqrt).then_inc(gq_rs, 1)
                act.wait_ge(gq_o, 3 * h + 3)
                nc.scalar.activation(OH0[:], O[:], ACT.Copy).then_inc(gq_h, 1)
                act.wait_ge(dn_full, 24 * h + 24)
                round_next(6)
                round_next(7)
                round_next(8)

        def sp_gla(sp):
            for dst, src in ((MLEV, masks), (SMASK, smask), (BMASK, bmask), (SCM, scanm)):
                sp.dma_start(dst[:], src).then_inc(m0c_in, 16)
            sp.wait_ge(al_done, ACTS[0])
            w_loads(sp, 3, 4)
            with sp.Fori(0, H) as h:
                sp.dma_start(WG[:], wgate[bass.ds(h, 1)].rearrange("a r n -> r (a n)")).then_inc(wg_in, 16)
                for p in range(HW):
                    if p == HW - 1:
                        sp.wait_ge(m0_ev, 21 * h + 21)
                    w_load(sp, HW * h + W_M0 + p + 3, (W_M0 + p) % 3)

        def pe_kv(pe, c, act):
            pe.wait_ge(al_done, act + 1)
            for x in range(2):
                if c == 0:
                    pe.wait_ge(w_lo, W_KV + x + 1)
                project(pe, 3 * x + c, (W_KV + x) % 3, c, kv_full)

        def act_kv(act):
            for c in range(NC):
                for x, dst in ((0, KTT), (1, VTT)):
                    act.wait_ge(kv_full, 2 * c + x + 1)
                    nc.scalar.activation(dst[:, chunk(c)], PS[:, 3 * x + c, 0:CW], ACT.Copy).then_inc(kv_ev, 1)
            for x in range(3):
                w_round(act, W_KV + x + 3, (W_KV + x) // 3 + 1, (W_KV + x) % 3)
            act.wait_ge(kt_full, 1)
            act.wait_ge(al_done, ACTS[2])
            for i in range(3):
                n = 4 if i < 2 else 3
                last = nc.scalar.activation(KVTOK[:, 4 * i:4 * i + n].rearrange("p a n -> p (a n)"), PS[:, i, 0:n * P], ACT.Copy)
            last.then_inc(kt_ev, 1)

        def pe_kv_tokens(pe):
            pe.wait_ge(kv_ev, 2 * NC)
            tiles = [(VTT, i) for i in range(9)] + [(KTT, 7), (KTT, 8)]
            for x, (src, i) in enumerate(tiles):
                n = CH if i < 8 else SAMP
                last = nc.tensor.transpose(PS[0:n, x // 4, (x % 4) * P:(x % 4 + 1) * P], src[:, i * CH:i * CH + n], ident[:])
            last.then_inc(kt_full, 1)

        def sp_kv(sp):
            sp.wait_ge(kv_ev, 2 * NC)
            sp.dma_start(kt_dram, KTT[:]).then_inc(kv_out, 16)
            sp.wait_ge(kt_ev, 1)
            sp.dma_start(v_dram[0:SEQ].rearrange("(t p) d -> p t d", p=P), KVTOK[:, 0:8]).then_inc(kv_out, 16)
            sp.dma_start(v_dram[SEQ:T], KVTOK[0:SAMP, 8]).then_inc(kv_out, 16)
            sp.dma_start(vwin_p, KVTOK[:, 7]).then_inc(kw_out, 16)
            sp.dma_start(kwin_p, KVTOK[:, 9]).then_inc(kw_out, 16)
            for dst, tile, old in ((vwin_s, 8, cv), (kwin_s, 10, ck)):
                for b in range(NB):
                    sp.dma_start(dst[b, WIN - LS:WIN], KVTOK[b * LS:(b + 1) * LS, tile]).then_inc(kw_out, 16)
                sp.dma_start(dst[:, 0:WIN - LS], old[:, LS:WIN]).then_inc(kw_out, 16)

        def first_of_all(T_):
            return isinstance(T_, int) and T_ == 0

        def pe_ffn(pe, l):
            w0, d0, acts = (W_F0, W_F1)[l], (DOWNS[1], DOWNS[3])[l], (ACTS[1], ACTS[3])[l]

            def tile(T_, b, s, first):
                pe.wait_ge(w_lo, b + 1)
                for c in range(NC):
                    if first:
                        pe.wait_ge(al_done, acts - NC + c + 1)
                    if not first_of_all(T_):
                        pe.wait_ge(u_ev, 3 * T_ + c - 2)
                    project(pe, c, s % 3, c, u_full)
                pe.wait_ge(w_lo, b + 2)
                for c in range(NC):
                    if not first_of_all(T_):
                        pe.wait_ge(h_made, 3 * T_ + c - 2)
                    project(pe, 3 + c, (s + 1) % 3, c, v_full)

            def downs(D_, T_, b, s):
                pe.wait_ge(w_lo, b + 2)
                pe.wait_ge(hl, T_ + 1)
                down(pe, (s % 3, (s + 1) % 3), HH, HL, 24 * D_)

            t0 = FT * l
            tile(t0, w0, w0, True)
            tile(t0 + 1, w0 + 2, w0 + 2, False)
            with pe.Fori(1, FG) as g:
                b = w0 - 2 + 6 * g
                s = w0 + 4
                tile(2 * g + t0, b, s, False)
                downs(g + (d0 - 1), 2 * g + (t0 - 1), b + 2, s + 2)
                tile(2 * g + (t0 + 1), b + 4, s + 4, False)
            downs(d0 + FG - 1, t0 + FT - 1, w0 + 4 + 6 * (FG - 1), w0 + 4)

        def act_ffn(act, l):
            w0, d0, t0 = (W_F0, W_F1)[l], (DOWNS[1], DOWNS[3])[l], FT * l
            acts = ACTS[2 * l + 1]
            act.wait_ge(al_done, acts)
            for c in range(NC):
                act.wait_ge(h_out[c], 16 * (2 * l + 1))
            act.wait_ge(u0_set, l + 1)

            def bias(T_):
                for c in range(NC):
                    act.wait_ge(u_full, 3 * T_ + c + 1)
                    if c == 0 and not first_of_all(T_):
                        act.wait_ge(cn, T_)
                    n = CW if c < 2 else SEQ - 2 * CW
                    last = nc.scalar.activation(U[:, 2 + c * CW:2 + c * CW + n], PS[:, c, 0:n], ACT.Copy)
                    if c == 2:
                        last = nc.scalar.activation(U[:, UP:UW].rearrange("p (b s) -> p b s", s=2 + LS)[:, :, 2:2 + LS],
                                                    PS[:, 2, n:CW].rearrange("p (b s) -> p b s", s=LS), ACT.Copy)
                    last.then_inc(u_ev, 1)
                act.wait_ge(u_ev, 3 * T_ + 3)
                act.wait_ge(pre, T_ + 1)
                if not first_of_all(T_):
                    act.wait_ge(h_made, 3 * T_)
                nc.scalar.activation(C[:, 0:CV], U[:, 2:UW], ACT.Identity, bias=PC[:, 19:20], scale=PC[:, 18:19]).then_inc(cb, 1)

            def gelu(T_):
                act.wait_ge(cv2, T_ + 1)
                nc.scalar.activation(C[:, 0:CV], C[:, 0:CV], ACT.Gelu_apprx_tanh).then_inc(gl, 1)

            def hi(T_, t):
                act.wait_ge(h_made, 3 * T_ + 3)
                nc.scalar.activation(HH[:, t], HF[:], ACT.Copy).then_inc(hh, 1)

            def tile(T_, nxt):
                bias(T_)
                nxt(0)
                gelu(T_)
                act.wait_ge(v_full, 3 * T_ + 3)
                nxt(1)

            def rnd(b, third, s):
                w_round(act, b, third, s % 3)

            for t in range(2):
                tile(t0 + t, lambda x: rnd(w0 + 2 * t + x + 3, (w0 + 2 * t + x + 3) // 3, w0 + 2 * t + x))
                hi(t0 + t, t)
            with act.Fori(1, FG) as g:
                b = w0 - 2 + 6 * g
                s = w0 + 4

                def at(p):
                    rnd(b + p + 3, 2 * g + (s + p + 3) // 3 - 2, s + p)

                tile(2 * g + t0, at)
                act.wait_ge(dn_full, 24 * g + 24 * d0)
                at(2)
                at(3)
                hi(2 * g + t0, 0)
                tile(2 * g + (t0 + 1), lambda x: at(4 + x))
                hi(2 * g + (t0 + 1), 1)
            act.wait_ge(dn_full, 24 * (d0 + FG))
            for x in range(2):
                b = w0 + 4 + 6 * (FG - 1) + x + 3
                if b < W_END:
                    rnd(b, b // 3, b)

        def dve_ffn(dve, l):
            d0, t0 = (DOWNS[1], DOWNS[3])[l], FT * l
            for c in range(NC):
                dve.wait_ge(h_out[c], 16 * (2 * l + 1))
            dve.wait_ge(al_done, ACTS[2 * l + 1])
            nc.vector.memset(U[:, 0:2], 0.0).then_inc(u0_set, 1)
            dve.wait_ge(fp_in, 16 * (l + 1))

            def conv(T_, t):
                if not first_of_all(T_):
                    dve.wait_ge(cb, T_)
                    dve.wait_ge(cv2, T_)
                nc.vector.tensor_copy(PC[:], PAR[:, bass.ds(t, 1)].rearrange("p a n -> p (a n)")).then_inc(pc, 1)
                dve.wait_ge(pc, T_ + 1)
                if not first_of_all(T_):
                    dve.wait_ge(cn, T_)
                nc.vector.tensor_copy(U[:, UP:UW].rearrange("p (b s) -> p b s", s=2 + LS)[:, :, 0:2],
                                      PC[:, 0:16].rearrange("p (b s) -> p b s", s=2)).then_inc(pre, 1)
                dve.wait_ge(cb, T_ + 1)
                nc.vector.scalar_tensor_tensor(C[:, 0:CV], U[:, 1:1 + CV], PC[:, 17:18], C[:, 0:CV], ALU.mult, ALU.add).then_inc(cv1, 1)
                dve.wait_ge(cv1, T_ + 1)
                nc.vector.scalar_tensor_tensor(C[:, 0:CV], U[:, 0:CV], PC[:, 16:17], C[:, 0:CV], ALU.mult, ALU.add).then_inc(cv2, 1)
                nc.vector.tensor_copy(CN[:, bass.ds(t, 1), 0:2].rearrange("p a n -> p (a n)"), U[:, SEQ:SEQ + 2])
                nc.vector.tensor_copy(CN[:, bass.ds(t, 1), 2:18].rearrange("p a (b s) -> p (a b) s", s=2),
                                      U[:, UP:UW].rearrange("p (b s) -> p b s", s=2 + LS)[:, :, LS:LS + 2]).then_inc(cn, 1)

            def product(T_):
                dve.wait_ge(gl, T_ + 1)
                if not first_of_all(T_):
                    dve.wait_ge(hl, T_)
                for c in range(NC):
                    dve.wait_ge(v_full, 3 * T_ + c + 1)
                    n = CW if c < 2 else SEQ - 2 * CW
                    last = nc.vector.tensor_tensor(HF[:, c * CW:c * CW + n], C[:, c * CW:c * CW + n], PS[:, 3 + c, 0:n], ALU.mult)
                    if c == 2:
                        last = nc.vector.tensor_tensor(
                            HF[:, SEQ:T].rearrange("p (b s) -> p b s", s=LS),
                            C[:, UP:UW].rearrange("p (b s) -> p b s", s=2 + LS)[:, :, 0:LS],
                            PS[:, 5, n:CW].rearrange("p (b s) -> p b s", s=LS), ALU.mult)
                    last.then_inc(h_made, 1)

            def lo(T_, t):
                dve.wait_ge(hh, T_ + 1)
                nc.vector.tensor_tensor(HL[:, t], HF[:], HH[:, t].bitcast(fp32), ALU.subtract).then_inc(hl, 1)

            for t in range(2):
                conv(t0 + t, t)
                product(t0 + t)
                lo(t0 + t, t)
            dve.wait_ge(az_done, 2 * l + 2)
            with dve.Fori(1, FG) as g:
                conv(2 * g + t0, 2 * g)
                product(2 * g + t0)
                down_add(dve, 24 * g + 24 * (d0 - 1))
                lo(2 * g + t0, 0)
                conv(2 * g + (t0 + 1), 2 * g + 1)
                product(2 * g + (t0 + 1))
                lo(2 * g + (t0 + 1), 1)
            down_add(dve, 24 * (d0 + FG - 1))

        def sp_ffn(sp, l):
            w0 = (W_F0, W_F1)[l]
            sp.wait_ge(al_done, ACTS[2 * l + 1])
            for c in range(NC):
                sp.wait_ge(h_out[c], 16 * (2 * l + 1))
            if l:
                sp.wait_ge(cn_out, 16)
            sp.dma_start(PAR[:], ffnpar[l]).then_inc(fp_in, 16)
            w_loads(sp, w0 + 3, min(w0 + 3 * FT + 3, W_END))
            sp.wait_ge(cn, FT * (l + 1))
            sp.dma_start(conv_new[l], CN[:]).then_inc(cn_out, 16)

        def pe_attn(pe):
            pe.wait_ge(al_done, ACTS[2])
            pe.wait_ge(kt_ev, 1)
            with pe.Fori(0, NKV) as n:
                slot = [(W_M1 + p) % 3 for p in range(HW)]
                for j in range(2):
                    I = 2 * n + j
                    b = HW * n + W_M1 + 4 * j
                    pe.wait_ge(dn_add, 24 * I + 24 * DOWNS[2])
                    for t in range(2):
                        pe.wait_ge(w_lo, b + t + 1)
                        for c in range(NC):
                            project(pe, 3 * t + c, slot[4 * j + t], c, q_full)
                    pe.wait_ge(q_ev, 6 * I + 6)
                    if j == 0:
                        pe.wait_ge(kg_in, 112 * n + 112)

                    def scores(it):
                        t, i = divmod(it, NBLK)
                        if it >= 2:
                            pe.wait_ge(sa, 16 * I + it - 1)
                        for e in range(2):
                            x = slice(64 * e, 64 * e + 64)
                            q = Q1[x, t, i * WIN:(i + 1) * WIN]
                            bank = 2 * (it % 2) + e
                            if i:
                                last = nc.tensor.matmul(PS[:, bank, 0:2 * WIN], q, KG[x, (i - 1) * WIN:(i + 1) * WIN],
                                                        start=True, stop=True)
                            else:
                                last = nc.tensor.matmul(PS[:, bank, WIN:2 * WIN], q, KG[x, 0:WIN], start=True, stop=True)
                        last.then_inc(sf, 1)

                    def transposed(it):
                        i = it % NBLK
                        pe.wait_ge(es, 16 * I + it + 1)
                        if it >= 2:
                            pe.wait_ge(te, 16 * I + it - 1)
                        for e in range(2):
                            for k in range(0 if i else 1, 2):
                                m = 2 * e + k
                                last = nc.tensor.transpose(PS[:, 4 + it % 2, m * P:(m + 1) * P],
                                                           SS[:, it % 2, e, k * WIN:(k + 1) * WIN], ident[:])
                        last.then_inc(tf, 1)

                    def values(it):
                        i = it % NBLK
                        pe.wait_ge(te, 16 * I + it + 1)
                        if it:
                            pe.wait_ge(on, 16 * I + it)
                        for e in range(2):
                            for k in range(0 if i else 1, 2):
                                last = nc.tensor.matmul(PS[:, 6, 64 * e:64 * e + 64], PT[:, it % 2, 2 * e + k],
                                                        VG[:, i - 1 + k], start=(k == 0 or i == 0), stop=(k == 1))
                        last.then_inc(of, 1)

                    def turned(it):
                        pe.wait_ge(on, 16 * I + it + 1)
                        if it:
                            pe.wait_ge(xl, 16 * I + it)
                        nc.tensor.transpose(PS[:, 7, 0:P], OT[:, it % 2], ident[:]).then_inc(xf, 1)

                    for s in range(2 * NBLK + 2):
                        if s < 16:
                            scores(s)
                        if 1 <= s < 17:
                            transposed(s - 1)
                            values(s - 1)
                        if s >= 2:
                            turned(s - 2)

                    pe.wait_ge(one, 1)
                    pe.wait_ge(sa, 16 * I + 16)
                    pe.wait_ge(te, 16 * I + 16)
                    for e in range(2):
                        for t in range(2):
                            hh_ = 2 * t + e
                            x, y = slice(64 * e, 64 * e + 64), slice(32 * hh_, 32 * hh_ + 32)
                            q = Q1[x, t, SEQ:T]
                            for half in range(2):
                                nc.tensor.matmul(PS[y, 2 * e + half, :], q,
                                                 KCG[x, 4 * half:4 * half + 4].rearrange("p b k -> p (b k)"), start=True, stop=True)
                            last = nc.tensor.matmul(PS[y, 4 + e, 0:SAMP], q, KG[x, SEQ:T], start=True, stop=True)
                    last.then_inc(xsf, 1)
                    pe.wait_ge(xsc, I + 1)
                    for b_ in range(NB):
                        nc.tensor.transpose(PS[:, b_ // 4, (b_ % 4) * P:(b_ % 4 + 1) * P], SX[:, b_ * WIN:(b_ + 1) * WIN], ident[:])
                    nc.tensor.transpose(PS[0:SAMP, 2, 0:P], SX[:, SEQ:T], ident[:]).then_inc(xtf, 1)
                    pe.wait_ge(xte, I + 1)
                    for e in range(2):
                        y = slice(64 * e, 64 * e + 64)
                        out = PS[y, 4 + e, 0:2 * SAMP].rearrange("p (t m) -> p t m", t=2)
                        for b_ in range(NB):
                            nc.tensor.matmul(out, VCG[:, b_],
                                             PX[:, b_].rearrange("p (t e m) -> p e t m", t=2, e=2)[:, e],
                                             start=(b_ == 0), stop=False)
                        last = nc.tensor.matmul(out, VG[0:SAMP, 8],
                                                PXN[:].rearrange("p (t e m) -> p e t m", t=2, e=2)[:, e], start=False, stop=True)
                    last.then_inc(xof, 1)

                    pe.wait_ge(w_lo, b + 4)
                    pe.wait_ge(xol, 2 * I + 2)
                    pe.wait_ge(xl, 16 * I + 16)
                    down(pe, (slot[4 * j + 2], slot[4 * j + 3]), OH1, OL1, 24 * I + 24 * DOWNS[2])

        def dve_attn(dve):
            dve.wait_ge(a_c_in, 16 * 3)
            dve.wait_ge(az_done, 3)
            with dve.Fori(0, NKV) as n:
                for j in range(2):
                    I = 2 * n + j
                    nc.vector.tensor_copy(SKG[:, 0:4], SINK[:, bass.ds(8 * n + 4 * j, 4)])
                    nc.vector.tensor_copy(SKG[:, 4:5], SKS[:, bass.ds(2 * n + j, 1)]).then_inc(skg, 1)
                    dve.wait_ge(skg, I + 1)
                    dve.wait_ge(bi_in, 32 * 4 * I + 32 * 4)

                    def biased(it):
                        t, i = divmod(it, NBLK)
                        u = it % 2
                        x0 = 0 if i else WIN
                        dve.wait_ge(sf, 16 * I + it + 1)
                        if it >= 2:
                            dve.wait_ge(tf, 16 * I + it - 1)
                        nc.vector.tensor_tensor(SS[:, u, :, x0:], PS[:, 2 * u:2 * u + 2, x0:2 * WIN],
                                                BI[:, 2 * t:2 * t + 2, x0:], ALU.add).then_inc(sa, 1)
                        dve.wait_ge(sa, 16 * I + it + 1)
                        nc.vector.tensor_reduce(ST[:, u, 0:2], SS[:, u, :, x0:], AX.X, ALU.max).then_inc(mx, 1)
                        dve.wait_ge(mx, 16 * I + it + 1)
                        nc.vector.tensor_tensor(ST[:, u, 0:2], ST[:, u, 0:2], SKG[:, 2 * t:2 * t + 2], ALU.max).then_inc(mm_, 1)
                        dve.wait_ge(mm_, 16 * I + it + 1)
                        nc.vector.tensor_tensor(ST[:, u, 4:6], SKG[:, 2 * t:2 * t + 2], ST[:, u, 0:2], ALU.subtract)
                        nc.vector.tensor_scalar(ST[:, u, 2:4], ST[:, u, 0:2], -1.0, None, ALU.mult).then_inc(nm, 1)

                    def scaled(it):
                        u = it % 2
                        dve.wait_ge(es, 16 * I + it + 1)
                        nc.vector.tensor_tensor(ST[:, u, 6:8], ST[:, u, 6:8], ST[:, u, 8:10], ALU.add).then_inc(den, 1)
                        dve.wait_ge(den, 16 * I + it + 1)
                        nc.vector.reciprocal(ST[:, u, 10:12], ST[:, u, 6:8]).then_inc(rc, 1)
                        dve.wait_ge(rc, 16 * I + it + 1)
                        dve.wait_ge(of, 16 * I + it + 1)
                        if it >= 2:
                            dve.wait_ge(xf, 16 * I + it - 1)
                        nc.vector.tensor_tensor(OT[:, u].rearrange("p (e d) -> p e d", e=2),
                                                PS[:, 6, 0:P].rearrange("p (e d) -> p e d", e=2),
                                                bc(ST[:, u, 10:12], HD), ALU.mult).then_inc(on, 1)

                    def lo(it):
                        t, i = divmod(it, NBLK)
                        x = slice(i * WIN, (i + 1) * WIN)
                        dve.wait_ge(xh, 16 * I + it + 1)
                        nc.vector.tensor_tensor(OL1[:, t, x], PS[:, 7, 0:P], OH1[:, t, x].bitcast(fp32), ALU.subtract).then_inc(xl, 1)

                    for s in range(2 * NBLK + 2):
                        if s < 16:
                            biased(s)
                        if 1 <= s < 17:
                            scaled(s - 1)
                        if s >= 2:
                            lo(s - 2)

                    dve.wait_ge(xsf, I + 1)
                    for hh_ in range(4):
                        e = hh_ % 2
                        y = slice(32 * hh_, 32 * hh_ + 32)
                        nc.vector.tensor_tensor(SX[y, 0:SEQ].rearrange("p (b k) -> p b k", b=NB),
                                                PS[y, 2 * e:2 * e + 2].rearrange("p h (b k) -> p (h b) k", b=4),
                                                SBC[y, 0:WIN].unsqueeze(1).broadcast_to([SAMP, NB, WIN]), ALU.add)
                        last = nc.vector.tensor_tensor(SX[y, SEQ:T].rearrange("p (b k) -> p b k", b=NB),
                                                       PS[y, 4 + e, 0:SAMP].rearrange("p (b k) -> p b k", b=NB),
                                                       SBC[y, WIN:WIN + LS].unsqueeze(1).broadcast_to([SAMP, NB, LS]), ALU.add)
                    last.then_inc(xsa, 1)
                    dve.wait_ge(xsa, I + 1)
                    nc.vector.tensor_tensor(SX[:, 0:SEQ].rearrange("p (b k) -> p b k", b=NB),
                                            SX[:, 0:SEQ].rearrange("p (b k) -> p b k", b=NB), bc(BM4[:], WIN), ALU.add)
                    nc.vector.tensor_tensor(SX[:, SEQ:T], SX[:, SEQ:T], SM4[:], ALU.add).then_inc(xsb, 1)
                    dve.wait_ge(xsb, I + 1)
                    nc.vector.tensor_reduce(ST[:, 0, 12:13], SX[:], AX.X, ALU.max).then_inc(xmx, 1)
                    dve.wait_ge(xmx, 3 * I + 1)
                    nc.vector.tensor_tensor(ST[:, 0, 12:13], ST[:, 0, 12:13], SKG[:, 4:5], ALU.max).then_inc(xmx, 1)
                    dve.wait_ge(xmx, 3 * I + 2)
                    nc.vector.tensor_tensor(ST[:, 0, 14:15], SKG[:, 4:5], ST[:, 0, 12:13], ALU.subtract)
                    nc.vector.tensor_scalar(ST[:, 0, 13:14], ST[:, 0, 12:13], -1.0, None, ALU.mult).then_inc(xmx, 1)
                    dve.wait_ge(xex, I + 1)
                    nc.vector.tensor_tensor(ST[:, 1, 12:13], ST[:, 1, 12:13], ST[:, 1, 13:14], ALU.add).then_inc(xrc, 1)
                    dve.wait_ge(xrc, 2 * I + 1)
                    nc.vector.reciprocal(ST[:, 1, 14:15], ST[:, 1, 12:13]).then_inc(xrc, 1)
                    dve.wait_ge(xrc, 2 * I + 2)
                    nc.vector.tensor_scalar(SX[:], SX[:], ST[:, 1, 14:15], None, ALU.mult).then_inc(xsc, 1)
                    for e in range(2):
                        y = slice(64 * e, 64 * e + 64)
                        dve.wait_ge(xoh, 2 * I + 2)
                        nc.vector.tensor_tensor(OL1[y, :, SEQ:T], PS[y, 4 + e, 0:2 * SAMP].rearrange("p (t m) -> p t m", t=2),
                                                OH1[y, :, SEQ:T].bitcast(fp32), ALU.subtract).then_inc(xol, 1)
                    down_add(dve, 24 * I + 24 * DOWNS[2])

        def act_attn(act):
            act.wait_ge(kw_out, 16 * 20)
            act.wait_ge(kv_out, 16 * 3)
            for c in range(NC):
                act.wait_ge(h_out[c], 32)
            with act.Fori(0, NKV) as n:
                slot = [(W_M1 + p) % 3 for p in range(HW)]
                third = [(W_M1 + p) // 3 for p in range(HW + 3)]
                for j in range(2):
                    I = 2 * n + j

                    def round_next(p):
                        w_round(act, HW * n + W_M1 + p + 3, 3 * n + third[p + 3], slot[p])

                    for t in range(2):
                        for c in range(NC):
                            act.wait_ge(q_full, 6 * I + 3 * t + c + 1)
                            nc.scalar.activation(Q1[:, t, chunk(c)], PS[:, 3 * t + c, 0:CW], ACT.Copy,
                                                 scale=HD ** -0.5).then_inc(q_ev, 1)
                        round_next(4 * j + t)

                    def exps(it):
                        u, i = it % 2, it % NBLK
                        x0 = 0 if i else WIN
                        act.wait_ge(nm, 16 * I + it + 1)
                        if it >= 2:
                            act.wait_ge(rc, 16 * I + it - 1)
                        for e in range(2):
                            nc.scalar.activation(SS[:, u, e, x0:], SS[:, u, e, x0:], ACT.Exp, bias=ST[:, u, 2 + e:3 + e],
                                                 accum_out=ST[:, u, 6 + e:7 + e])
                        nc.scalar.activation(ST[:, u, 8:10], ST[:, u, 4:6], ACT.Exp).then_inc(es, 1)

                    def turn(it):
                        u, i = it % 2, it % NBLK
                        act.wait_ge(tf, 16 * I + it + 1)
                        if it >= 2:
                            act.wait_ge(of, 16 * I + it - 1)
                        if i:
                            nc.scalar.activation(PT[:, u].rearrange("p m q -> p (m q)"), PS[:, 4 + u], ACT.Copy).then_inc(te, 1)
                        else:
                            nc.scalar.activation(PT[:, u, 1:4:2], PS[:, 4 + u].rearrange("p (m q) -> p m q", q=P)[:, 1:4:2],
                                                 ACT.Copy).then_inc(te, 1)

                    def hi(it):
                        t, i = divmod(it, NBLK)
                        act.wait_ge(xf, 16 * I + it + 1)
                        nc.scalar.activation(OH1[:, t, i * WIN:(i + 1) * WIN], PS[:, 7, 0:P], ACT.Copy).then_inc(xh, 1)

                    for s in range(2 * NBLK + 2):
                        if s < 16:
                            exps(s)
                        if 1 <= s < 17:
                            turn(s - 1)
                        if s >= 2:
                            hi(s - 2)
                    act.wait_ge(xmx, 3 * I + 3)
                    nc.scalar.activation(SX[:], SX[:], ACT.Exp, bias=ST[:, 0, 13:14], accum_out=ST[:, 1, 12:13])
                    nc.scalar.activation(ST[:, 1, 13:14], ST[:, 0, 14:15], ACT.Exp).then_inc(xex, 1)
                    act.wait_ge(xtf, I + 1)
                    nc.scalar.activation(PX[:].rearrange("p (h b) n -> p h (b n)", h=2), PS[:, 0:2], ACT.Copy)
                    nc.scalar.activation(PXN[:], PS[0:SAMP, 2, 0:P], ACT.Copy).then_inc(xte, 1)
                    for e in range(2):
                        y = slice(64 * e, 64 * e + 64)
                        act.wait_ge(xof, I + 1)
                        nc.scalar.activation(OH1[y, :, SEQ:T], PS[y, 4 + e, 0:2 * SAMP].rearrange("p (t m) -> p t m", t=2),
                                             ACT.Copy).then_inc(xoh, 1)
                    act.wait_ge(dn_full, 24 * I + 24 * DOWNS[2] + 24)
                    round_next(4 * j + 2)
                    round_next(4 * j + 3)
                round_next(8)

        def sp_attn(sp):
            sp.wait_ge(kv_out, 16 * 3)
            sp.wait_ge(kw_out, 16 * 20)
            sp.wait_ge(al_done, ACTS[2])
            for c in range(NC):
                sp.wait_ge(h_out[c], 32)
            for dst, src in ((BM4, bmask4), (SM4, smask4), (SKS, sinks[1, :, 0:2 * NKV])):
                sp.dma_start(dst[:], src).then_inc(a_c_in, 16)
            with sp.Fori(0, NKV) as n:
                sp.wait_ge(dn_full, 48 * n + 24 * DOWNS[2])
                for e in range(2):
                    x = slice(64 * e, 64 * e + 64)
                    sp.dma_start(KG[x], kt_dram[bass.ds(64 * n, 64)]).then_inc(kg_in, 16)
                    sp.dma_start(KCG[x], kcT[bass.ds(64 * n, 64)]).then_inc(kg_in, 16)
                sp.dma_start(VG[:, 0:8], v_dram[0:SEQ].rearrange("(t p) d -> p t d", p=P)[:, :, bass.ds(64 * n, 64)]).then_inc(kg_in, 16)
                sp.dma_start(VG[0:SAMP, 8], v_dram[SEQ:T, bass.ds(64 * n, 64)]).then_inc(kg_in, 16)
                sp.dma_start(VCG[:], vc[:, :, bass.ds(64 * n, 64)]).then_inc(kg_in, 16)
                for j in range(2):
                    I = 2 * n + j
                    if j:
                        sp.wait_ge(xsb, I)
                    for x in range(4):
                        h0 = (8 * n + (4 * j + x)) * (P * RL)
                        sp.dma_start(BI[:, x], bass.AP(r_dram.tensor, h0 + (WIN - 1), [[RL - 1, P], [1, 2 * WIN]])).then_inc(bi_in, 16)
                        sp.dma_start(SBC[32 * x:32 * x + 32], bass.AP(r_dram.tensor, h0 + (WIN - 1), [[0, NB], [RL - 1, LS], [1, WIN + LS]])).then_inc(bi_in, 16)
                    for p in range(4):
                        w_load(sp, HW * n + W_M1 + 4 * j + p + 3, (W_M1 + 4 * j + p) % 3)
                w_load(sp, HW * n + W_M1 + 8 + 3, (W_M1 + 8) % 3)

        block = ctx.enter_context(nc.Block())

        @block.sync
        def _(sp):
            for dst, src in ((ident, ident_in), (GC, gains), (SINK, sinks[0])):
                sp.dma_start(dst[:], src).then_inc(c_in, 16)
            sp_boundary(sp, 0)
            for b in range(3):
                sp.dma_start(WR[:, b], wall[b]).then_inc(w_in[b], 16)
            sp.dma_start(OHR[:], onehot).then_inc(tb_in, 16)
            sp.wait_ge(tb_one, 1)
            sp.dma_start(TBL[0:32], table).then_inc(tb_in, 16)
            sp.wait_ge(rb_row, NQ)
            sp.dma_start(r_dram.rearrange("(h p m) -> p h m", p=P, m=RL), RB[:]).then_inc(rb_out, 16)
            sp_gla(sp)
            sp_boundary(sp, 1)
            sp_ffn(sp, 0)
            sp_boundary(sp, 2)
            w_loads(sp, W_KV + 3, W_M1 + 3)
            sp_kv(sp)
            sp_attn(sp)
            sp_boundary(sp, 3)
            sp_ffn(sp, 1)
            sp_boundary(sp, 4)
            for c in range(NC):
                sp.wait_ge(h_out[c], 64)
            sp.wait_ge(cn_out, 32)
            sp.wait_ge(gp_out, 16 * H)
            sp.wait_ge(st_out, 16 * H)
            sp.wait_ge(kw_out, 16 * 20)
            sp.wait_ge(kv_out, 16 * 3)
            sp.wait_ge(rb_out, 16)

        @block.gpsimd
        def _(pool):
            w_rests(pool, 0, 3)
            pool_boundary(pool, 0)
            w_rests(pool, 3, W_F0 + 3)
            pool_boundary(pool, 1)
            w_rests(pool, W_F0 + 3, W_KV + 3)
            pool_boundary(pool, 2)
            w_rests(pool, W_KV + 3, W_F1 + 3)
            pool_boundary(pool, 3)
            w_rests(pool, W_F1 + 3, W_END)
            pool_boundary(pool, 4)

        @block.vector
        def _(dve):
            nc.vector.memset(ones[:], 1.0).then_inc(one, 1)
            nc.vector.memset(TBL[:], 1.0).then_inc(tb_one, 1)
            dve.wait_ge(tb_in, 32)
            nc.vector.tensor_copy(TBB[:], bc(TBL[:], P)).then_inc(tb_cols, 1)
            for h in range(NQ):
                dve.wait_ge(rb_full, h + 1)
                nc.vector.tensor_copy(RB[:, h], PS[:, h % 6, 0:RL]).then_inc(rb_row, 1)
            dve.wait_ge(c_in, 48)
            dve_boundary(dve, 0)
            dve_gla(dve)
            dve_boundary(dve, 1)
            dve_ffn(dve, 0)
            dve_boundary(dve, 2)
            dve_attn(dve)
            dve_boundary(dve, 3)
            dve_ffn(dve, 1)
            dve_boundary(dve, 4)

        @block.scalar
        def _(act):
            for b in range(3):
                w_round(act, b, 0, b)
            act.wait_ge(rb_full, NQ)
            act_boundary(act, 0)
            act_gla(act)
            act_boundary(act, 1)
            act_ffn(act, 0)
            act_boundary(act, 2)
            act_kv(act)
            act_attn(act)
            act_boundary(act, 3)
            act_ffn(act, 1)
            act_boundary(act, 4)

        @block.tensor
        def _(pe):
            pe.wait_ge(tb_cols, 1)
            for h in range(NQ):
                if h >= 6:
                    pe.wait_ge(rb_row, h - 5)
                nc.tensor.matmul(PS[:, h % 6, 0:RL], TBB[:, h], OHR[:], start=True, stop=True).then_inc(rb_full, 1)
            pe.wait_ge(c_in, 48)
            pe.wait_ge(one, 1)
            pe.wait_ge(rb_row, NQ)
            pe_boundary(pe, 0)
            pe_gla(pe)
            pe_boundary(pe, 1)
            pe_ffn(pe, 0)
            pe_boundary(pe, 2)
            pe_kv_tokens(pe)
            pe_attn(pe)
            pe_boundary(pe, 3)
            pe_ffn(pe, 1)
            pe_boundary(pe, 4)


def _constants():
    one = np.zeros((33, RL), np.float32)
    for m in range(RL):
        n = 255 - m
        if 0 <= n < WIN:
            if n < 16:
                bucket = n
            else:
                large = 16 + int(np.float32(np.float32(np.log(np.float32(n / 16.0))) / np.float32(math.log(8.0)) * 16))
                bucket = min(large, 31)
            one[bucket, m] = 1.0
        else:
            one[32, m] = NEG
    j, i = np.arange(CH)[:, None], np.arange(CH)[None, :]
    masks = np.zeros((CH, 5, CH), np.float32)
    for n, L in enumerate(LEVELS):
        masks[:, n] = (j // (2 * L) == i // (2 * L)) & (j % (2 * L) < L) & (i % (2 * L) >= L)
    masks[:, 4] = (j // FINE == i // FINE) & (j <= i)
    j, i = np.arange(SAMP)[:, None], np.arange(SAMP)[None, :]
    same = (j // LS == i // LS)
    smask = (same & (j <= i)).astype(np.float32)
    bmask = (np.arange(SAMP)[:, None] // LS == np.arange(NB)[None, :]).astype(np.float32)
    scan = np.ones((2, T), np.float32)
    scan[0, 0:SEQ:CH] = 0
    scan[0, SEQ::LS] = 0
    scan[1, 0:SEQ:FINE] = 0
    scan[1, SEQ::LS] = 0
    bf = mybir.dt.np(bf16)
    b4 = np.where(np.tile(bmask, (4, 1)) > 0, 0.0, NEG).astype(np.float32)
    s4 = np.where(np.tile(same, (4, 1)), 0.0, NEG).astype(np.float32)
    return dict(onehot=one, masks=masks.astype(bf), smask=smask.astype(bf), bmask=bmask,
                scanm=np.ascontiguousarray(np.broadcast_to(scan, (P, 2, T))).astype(bf),
                ident_in=np.eye(P, dtype=np.float32), bmask4=b4, smask4=s4)


def _column_block(w, x):
    return w[:, x:x + P].reshape(KT, P, P).transpose(1, 0, 2).reshape(P, KT * P)


def _lay_out(i):
    w_in, w_up, w_down = i["w_in_a"][0], i["w_up"], i["w_down"]
    wall = np.zeros((W_END, P, KT * P), np.float32)
    wall[W_GLR].reshape(P, KT, P)[:, :, 0:RANK] = w_in[:, 3072:3088].reshape(KT, P, RANK).transpose(1, 0, 2)
    for h in range(H):
        b = W_M0 + HW * h
        for p, x in enumerate((h * P, 512 + h * P, 1024 + h * DV, 1024 + h * DV + P, 2048 + h * DV, 2048 + h * DV + P)):
            wall[b + p] = _column_block(w_in, x)
        for t in range(2):
            wall[b + 6 + t] = i["w_out_a"][0, h * DV + t * P:h * DV + (t + 1) * P]
    for l, w0 in enumerate((W_F0, W_F1)):
        for g in range(FG):
            b = w0 if g == 0 else w0 + 4 + 6 * (g - 1)
            for t in range(2):
                bt = b + 2 * t + (2 * t if g else 0)
                x = (2 * g + t) * P
                wall[bt] = _column_block(w_up[l], x)
                wall[bt + 1] = _column_block(w_up[l], FF + x)
                bd = w0 + 4 + 6 * g + 2 + t if g < FG - 1 else w0 + 4 + 6 * (FG - 1) + t
                wall[bd] = w_down[l, x:x + P]
    for x in range(2):
        wall[W_KV + x] = _column_block(i["w_kv"], x * P)
    for n in range(NKV):
        for j in range(2):
            for t in range(2):
                x = (4 * n + 2 * j + t) * P
                wall[W_M1 + HW * n + 4 * j + t] = _column_block(i["w_q_b"][0], x)
                wall[W_M1 + HW * n + 4 * j + 2 + t] = i["w_o_b"][0, x:x + P]
    x = np.concatenate([i["x_prompt"][0], i["x_sample"].reshape(SAMP, D)], 0)
    xT = x.reshape(NC, CW, KT, P).transpose(0, 3, 2, 1)
    rows = [i[n].reshape(-1, P) for n in ("g_mix_pre", "g_mix_post", "g_ffn_pre", "g_ffn_post", "g_kv", "g_gla_out")]
    par = np.zeros((2, P, FT, 20), np.float32)
    par[:, :, :, 0:16] = i["cache_conv"].reshape(2, 16, FT, P).transpose(0, 3, 2, 1)
    par[:, :, :, 16:19] = i["conv_w"].reshape(2, 3, FT, P).transpose(0, 3, 2, 1)
    par[:, :, :, 19] = i["conv_b"].reshape(2, FT, P).transpose(0, 2, 1)
    wg = np.concatenate([i["w_gate_up"][0], i["b_gate"][0][None]], 0).reshape(RANK + 1, H, P).transpose(1, 0, 2)
    s = i["sinks"][0]
    sinks = np.stack([np.broadcast_to(s, (P, NQ)), np.zeros((P, NQ), np.float32)])
    sinks[1, :, 0:4] = np.repeat(s.reshape(4, 4), 32, axis=1).T
    out = dict(wall=wall, xT=xT, gains=np.concatenate(rows, 0).T, ffnpar=par, wgate=wg,
               state=i["state_gla"][0].transpose(1, 2, 0, 3),
               kcT=i["cache_k_win"].transpose(2, 3, 0, 1).reshape(P, NB, WIN),
               vc=i["cache_v_win"].transpose(1, 0, 2, 3).reshape(WIN, NB, P),
               ck=i["cache_k_win"].reshape(NB, WIN, P), cv=i["cache_v_win"].reshape(NB, WIN, P),
               table=i["rel_bias"], sinks=sinks, **_constants())
    return {k: np.ascontiguousarray(v) for k, v in out.items()}


_OUTS = dict(yT=(NC, P, KT, CW), gla_p=(H, DK, DV), gla_s=(H, DK, NB, DV), conv_new=(2, P, FT, 18),
             kwin_p=(WIN, P), kwin_s=(NB, WIN, P), vwin_p=(WIN, P), vwin_s=(NB, WIN, P))


def kernel(**inputs):
    import concourse.bacc as bacc
    from concourse.bass_utils import run_bass_kernel_spmd

    arrays = _lay_out({k: np.asarray(v) for k, v in inputs.items()})
    nc = bacc.Bacc("TRN2", target_bir_lowering=False, num_devices=1)
    aps = {n: nc.dram_tensor(n, a.shape, mybir.dt.from_np(a.dtype), kind="ExternalInput").ap() for n, a in arrays.items()}
    for n, shape in _OUTS.items():
        aps[n] = nc.dram_tensor(n, shape, fp32, kind="ExternalOutput").ap()
    build(nc, **aps)
    r = run_bass_kernel_spmd(nc, [arrays], core_ids=[0]).results[0]
    y = np.asarray(r["yT"]).transpose(0, 3, 2, 1).reshape(T, D)
    conv = np.asarray(r["conv_new"]).transpose(0, 3, 2, 1).reshape(2, 18, FF)
    window = (NKV, HD)
    c = np.ascontiguousarray
    return (c(y[0:SEQ].reshape(1, SEQ, D)), c(y[SEQ:].reshape(NB, LS, D)),
            c(np.asarray(r["gla_p"]).reshape(1, 1, H, DK, DV)), c(np.asarray(r["gla_s"]).transpose(2, 0, 1, 3).reshape(1, NB, H, DK, DV)),
            c(conv[:, 0:2].reshape(2, 1, 2, FF)), c(conv[:, 2:18].reshape(2, NB, 2, FF)),
            c(np.asarray(r["kwin_p"]).reshape(1, WIN, *window)), c(np.asarray(r["kwin_s"]).reshape(NB, WIN, *window)),
            c(np.asarray(r["vwin_p"]).reshape(1, WIN, *window)), c(np.asarray(r["vwin_s"]).reshape(NB, WIN, *window)))
```

```python
import math
from contextlib import ExitStack

import numpy as np

import concourse.bass as bass
from concourse import mybir

fp32 = mybir.dt.float32
fp32r = mybir.dt.float32r
bf16 = mybir.dt.bfloat16
ALU = mybir.AluOpType
ACT = mybir.ActivationFunctionType
AX = mybir.AxisListType

P = 128
D = 1024
KT = D // P
SEQ, NB, LS = 1024, 8, 4
SAMP = NB * LS
T = SEQ + SAMP
NC, CW = 3, T // 3
H, DK, DV = 4, 128, 256
RANK = 16
CH = 128
NCHUNK = SEQ // CH
TAU = 16.0
LEVELS = (64, 32, 16, 8)
FINE = 8
GATE_FLOOR = -20.0 * TAU
HD, NQ, NKV = 64, 16, 2
WIN = 128
NBLK = SEQ // WIN
FF = 2816
FT = FF // P
FG = FT // 2
UP = 2 + SEQ
UW = UP + NB * (2 + LS)
CV = UW - 2
EPS = 1e-6
NEG = -1e30
RL = 383
HW = 9

G_MIX_PRE, G_MIX_POST, G_FFN_PRE, G_FFN_POST, G_KV, G_GLA = 0, 16, 32, 48, 64, 72
NGAIN = 74

W_GLR = 0
W_M0 = 1
W_F0 = W_M0 + H * HW
W_KV = W_F0 + FT * 3
W_M1 = W_KV + 3
W_F1 = W_M1 + NKV * HW
W_END = W_F1 + FT * 3 + 1


def build(nc, wall, xT, gains, ffnpar, wgate, state, kcT, vc, ck, cv, onehot, masks, smask, bmask,
          scanm, ident_in, bmask4, smask4, table, sinks,
          yT, gla_p, gla_s, conv_new, kwin_p, kwin_s, vwin_p, vwin_s):
    h_dram = nc.dram_tensor("h_scratch", [NC, P, KT, CW], fp32, kind="Internal").ap()
    r_dram = nc.dram_tensor("bias_scratch", [NQ * P * RL], fp32, kind="Internal").ap()
    kt_dram = nc.dram_tensor("kt_scratch", [P, T], fp32, kind="Internal").ap()
    v_dram = nc.dram_tensor("v_scratch", [T, P], fp32, kind="Internal").ap()

    ctx = ExitStack()
    with ctx:
        base = nc.sbuf_base
        at = [((base if isinstance(base, int) else base()) + 31) // 32 * 32]
        top = {"at": 0}

        def place(name, shape, dt=fp32, offset=None):
            size = math.prod(shape[1:]) * (2 if dt == bf16 else 4)
            size = (size + 31) // 32 * 32
            off = at[0] if offset is None else offset
            if offset is None:
                at[0] += size
            top["at"] = max(top["at"], off + size)
            return nc.alloc_sbuf_tensor_at(name, shape, dt, offset=off)

        def sem(name):
            return ctx.enter_context(nc.semaphore(name))

        AH_AT = at[0]
        AH = place("act_hi", [P, KT, T], fp32r)
        AL = place("act_lo", [P, KT, T], fp32r)
        AC_AT = at[0]
        ACC = place("acc", [P, NC, KT, CW])
        WR = place("w_raw", [P, 3, KT * P])
        WH = place("w_hi", [P, 3, KT * P], fp32r)
        WL = place("w_lo", [P, 3, KT * P], fp32r)
        ident = place("ident", [P, P])
        ones = place("ones", [P, P])
        EPSC = place("eps_col", [P, 1])
        GC = place("gain_cols", [P, NGAIN])
        SINK = place("sinks_b", [P, NQ])
        arena = at[0]

        HC_AT = arena + 4 * T * 4
        at[0] = HC_AT
        HC = place("h_chunk", [P, NC, KT, CW])
        RS_AT = at[0]
        RS = place("rstd", [P, NC, CW])
        SQ_AT = at[0]
        SQ = [place("squares0", [P, KT, CW], offset=arena), place("squares1", [P, KT, CW])]
        BEHIND = at[0]
        

        at[0] = arena
        Qb = at[0]
        Q = place("gq", [P, T])
        K = place("gk", [P, T])
        Z = place("gb", [P, T])
        B8 = place("gb8", [P, T])
        OH0 = place("go_hi", [P, 2, T], fp32r, offset=Qb)
        OL0 = place("go_lo", [P, 2, T], fp32r, offset=Qb + 2 * T * 4)
        KD = place("gkd", [P, NCHUNK, P], offset=Qb + T * 4)
        KDS = place("gkd_s", [SAMP, P], offset=Qb)
        S = place("gstate", [P, DV], offset=Qb + 2 * T * 4)
        KDM = place("gkd_masked", [SAMP, NB, P], offset=Qb + 3 * T * 4)
        Tb = at[0]
        T1 = place("gt1", [P, T])
        KTl = place("gkt", [P, T])
        SB = place("gstates", [P, NB, DV], offset=Tb)
        QTb = at[0]
        QT = place("gqt", [P, T])
        AT = place("gat", [P, T])
        SQ0 = place("gsq", [P, 2, T], offset=QTb)
        Vb = at[0]
        V = place("gv", [P, 9, DV])
        RS0 = place("grs", [P, T], offset=Vb)
        R = place("gr", [P, 2, T])
        O = place("go", [P, 2, T])
        GLR = place("glr", [RANK + 1, T])
        WG = place("wgate", [RANK + 1, P])
        EL = place("gel", [P, 16])
        MLEV = place("mlev", [P, 5, CH], bf16)
        SMASK = place("smask_t", [SAMP, SAMP], bf16)
        BMASK = place("bmask_t", [SAMP, NB])
        SCM = place("scan_masks", [P, 2, T], bf16)
        

        at[0] = arena
        HH = place("h_hi", [P, 2, T], fp32r)
        HL = place("h_lo", [P, 2, T], fp32r)
        at[0] = RS_AT
        U = place("u", [P, UW])
        C = place("c", [P, UW])
        HF = place("hf", [P, T])
        PAR = place("par", [P, FT, 20])
        PC = place("par_tile", [P, 20])
        at[0] = BEHIND
        CN = place("conv_new_t", [P, FT, 18])

        at[0] = BEHIND
        KTT = place("kT", [P, T])
        VTT = place("vT", [P, T], offset=arena + KT * CW * 4)
        KVTOK = place("kv_tok", [P, 11, P], offset=SQ_AT)
        at[0] = AC_AT
        TBB = place("table_cols", [33, NQ, P])
        RB = place("bias_rows", [P, NQ, RL])
        at[0] = AH_AT
        OHR = place("onehot_t", [33, RL])
        TBL = place("table_t", [33, NQ])
        at[0] = arena
        Q1_AT = at[0]
        Q1 = place("q1", [P, 4, T])
        KG = place("kg", [P, T])
        KCG = place("kcg", [P, NB, WIN])
        VG = place("vg", [P, 9, HD])
        VCG = place("vcg", [P, NB, HD])
        QS = place("q_sample", [P, 4, SAMP])
        BI = place("bias", [P, 8, 2 * WIN])
        SS = place("scores", [P, 3, 2, 2 * WIN])
        PT_AT = at[0]
        PT = place("probs_t", [P, 2, 4, P])
        PX = place("s_probs_t", [P, NB, P], offset=PT_AT)
        OT = place("o_tok", [P, 2, P])
        OH1 = place("o_hi", [P, 2, T], fp32r)
        OL1 = place("o_lo", [P, 2, T], fp32r)
        OH2 = place("o_hi2", [P, 2, T], fp32r, offset=Q1_AT)
        OL2 = place("o_lo2", [P, 2, T], fp32r, offset=Q1_AT + 2 * T * 4)
        ST = place("stats", [P, 8, 16])
        SST = place("s_stats", [P, 8])
        SX = place("s_scores", [P, T])
        PXN = place("s_probs_new_t", [SAMP, P])
        SBC = place("s_bias", [P, 2, WIN + LS])
        BM4 = place("s_mask", [P, NB])
        SM4 = place("s_mask_new", [P, SAMP])
        SKS = place("s_sinks", [P, NKV * 2])
        SKG = place("sinks_group", [P, 10])

        PS = ctx.enter_context(nc.psum_tensor("banks", [P, 8, 512], fp32))

        c_in = sem("constants_in")
        one = sem("ones_set")
        w_in = [sem(f"w_in{i}") for i in range(3)]
        w_hi, w_lo = sem("w_hi_done"), sem("w_lo_done")
        tb_one, tb_in, tb_cols = sem("table_ones"), sem("table_in"), sem("table_cols_done")
        rb_full, rb_row, rb_out = sem("bias_row_full"), sem("bias_row_copied"), sem("bias_rows_out")
        h_in = [sem(f"h_in{c}") for c in range(NC)]
        h_out = [sem(f"h_out{c}") for c in range(NC)]
        sq_done, ss_done, ms_done = sem("squares_done"), sem("square_sums_done"), sem("mean_squares_done")
        rs_done, po_done, ha_done = sem("rstd_done"), sem("post_norm_done"), sem("residual_done")
        nm_done, ah_done, al_done = sem("pre_norm_done"), sem("act_hi_done"), sem("act_lo_done")
        az_done = sem("acc_zeroed")
        dn_full, dn_add = sem("down_full"), sem("down_added")
        glr_full, glr_ev = sem("glr_full"), sem("glr_copied")
        m0c_in, wg_in = sem("m0_constants_in"), sem("wgate_in")
        m0_full, m0_ev = sem("gla_proj_full"), sem("gla_proj_copied")
        az, ln = sem("gate_abs"), sem("gate_log")
        gt = sem("gate_made")
        cs = sem("gate_summed")
        lv_d, lv_e, lv_qk, lv_pe, lv_m, lv_a = (sem(f"level_{x}") for x in ("diff", "exp", "qk", "scores", "masked", "added"))
        in_d, in_e, in_qk = sem("inter_diff"), sem("inter_exp"), sem("inter_qk")
        vt_full, vt_ev, kd_full, kd_ev, kdm = (sem(x) for x in ("v_tok_full", "v_tok_copied", "k_tok_full", "k_tok_copied", "k_masked"))
        st_in, st_out, gp_out = sem("states_in"), sem("states_out"), sem("gla_p_out")
        o_full, o_ev, s_full, s_upd = (sem(x) for x in ("o_full", "o_copied", "state_full", "state_updated"))
        os_full, os_ev, ss_full, ss_upd = (sem(x) for x in ("os_full", "os_copied", "sstate_full", "sstate_updated"))
        gq_sq, gq_ss, gq_ms, gq_rs, gq_si, gq_o, gq_h, gq_l = (sem("gn_" + x) for x in ("sq", "ss", "ms", "rs", "silu", "o", "hi", "lo"))
        fp_in, u0_set = sem("ffn_par_in"), sem("u_zeroed")
        pc, pre = sem("par_copied"), sem("prefix_copied")
        u_full, u_ev, v_full, h_made = sem("u_full"), sem("u_copied"), sem("val_full"), sem("h_made")
        cb, cv1, cv2, cn, gl, hh, hl = (sem("ffn_" + x) for x in ("bias", "conv1", "conv2", "cache", "gelu", "hi", "lo"))
        cn_out = sem("conv_new_out")
        kv_full, kv_ev, kt_full, kt_ev = sem("kv_full"), sem("kv_copied"), sem("kvt_full"), sem("kvt_copied")
        kw_out, kv_out = sem("windows_out"), sem("kv_out")
        kg_in, bi_in, a_c_in = sem("kv_head_in"), sem("bias_in"), sem("attn_constants_in")
        skg = sem("sinks_copied")
        q_full, q_ev = sem("q_full"), sem("q_copied")
        sf, sa, mx, mm_, nm, ex, es, den, rc = (sem("att_" + x) for x in ("scores", "biased", "max", "maxsink", "negmax", "exp", "expsink", "den", "rden"))
        tf, te, of, on, xf, xh, xl = (sem("att_" + x) for x in ("pt", "pt_copied", "o", "o_scaled", "ot", "hi", "lo"))
        xsf, xsa, xsb, xmx, xex, xrc, xsc, xtf, xte, xof, xoh, xol = (sem("samp_" + x) for x in ("scores", "biased", "masked", "max", "exp", "rden", "scaled", "pt", "pt_copied", "o", "hi", "lo"))

        def chunk(c):
            return slice(c * CW, (c + 1) * CW)

        def col(x):
            return GC[:, x:x + 1]

        def bc(ap, n):
            shape = list(ap.shape)
            return ap.unsqueeze(len(shape)).broadcast_to(shape + [n])

        steps = []
        n_stat = n_all = n_act = n_post = 0
        for B in range(5):
            here = {}
            for kind in {0: ["pre"], 1: ["post", "pre"], 2: ["post", "kv", "mix"], 3: ["post", "pre"], 4: ["post"]}[B]:
                for c in range(NC):
                    here[kind, c] = dict(B=B, kind=kind, c=c, at=len(here), buf=(len(here) + 1) % 2, stat=n_stat, k=n_all, act=n_act, post=n_post)
                    n_all += 1
                    n_stat += kind != "mix"
                    n_act += kind != "post"
                    n_post += kind == "post"
            steps.append(here)
        flat = [s for b in steps for s in b.values()]
        ACTS = [sum(s["kind"] != "post" for s in flat if s["B"] <= B) for B in range(5)]
        POSTS = [sum(s["kind"] == "post" for s in flat if s["B"] <= B) for B in range(5)]
        DOWNS = [0, H, H + FG, H + FG + 2 * NKV, H + 2 * FG + 2 * NKV]
        POST_G = {1: G_MIX_POST, 2: G_FFN_POST, 3: G_MIX_POST + 8, 4: G_FFN_POST + 8}
        PRE_G = {(0, "pre"): G_MIX_PRE, (1, "pre"): G_FFN_PRE, (2, "kv"): G_KV, (2, "mix"): G_MIX_PRE + 8,
                 (3, "pre"): G_FFN_PRE + 8}
        HALF = KT // 2
        HALVES = (slice(0, HALF), slice(HALF, KT))

        def free_squares(eng, s):
            if s["at"] >= 2:
                p = flat[s["k"] - 2]
                if p["kind"] == "post":
                    eng.wait_ge(ss_done, p["stat"] + 1)
                else:
                    eng.wait_ge(al_done, p["act"] + 1)
            elif s["at"] == 1 and s["B"]:
                eng.wait_ge(dn_full, 24 * DOWNS[s["B"]])

        def act_boundary(act, B):
            def square(kind, c):
                s = steps[B][kind, c]
                for n, half in enumerate(HALVES):
                    if kind == "post":
                        act.wait_ge(dn_add, 24 * DOWNS[B] - 24 + 8 * c + HALF * (n + 1))
                        src = ACC
                    elif B == 0:
                        act.wait_ge(h_in[c], 16)
                        src = HC
                    else:
                        act.wait_ge(ha_done, 2 * (POSTS[B - 1] + c) + n + 1)
                        src = HC
                    if n == 0:
                        free_squares(act, s)
                    nc.scalar.activation(SQ[s["buf"]][:, half], src[:, c, half], ACT.Square).then_inc(sq_done, 1)

            def rstd(kind, c):
                s = steps[B][kind, c]
                act.wait_ge(ss_done, s["stat"] + 1)
                nc.scalar.activation(RS[:, c], PS[:, 6 + s["stat"] % 2, 0:CW], ACT.Ln, bias=EPSC[:], scale=1.0 / D).then_inc(ms_done, 1)
                act.wait_ge(ms_done, s["stat"] + 1)
                nc.scalar.activation(RS[:, c], RS[:, c], ACT.Exp, scale=-0.5).then_inc(rs_done, 1)

            def hi(kind, c):
                s = steps[B][kind, c]
                if kind == "mix":
                    act.wait_ge(kv_full, 2 * c + 2)
                for n, half in enumerate(HALVES):
                    act.wait_ge(nm_done, 2 * s["act"] + n + 1)
                    nc.scalar.activation(AH[:, half, chunk(c)], SQ[s["buf"]][:, half], ACT.Copy).then_inc(ah_done, 1)

            if B:
                square("post", 0)
                square("post", 1)
                rstd("post", 0)
                square("post", 2)
                rstd("post", 1)
            if B == 4:
                rstd("post", 2)
                return
            pre = "kv" if B == 2 else "pre"
            square(pre, 0)
            if B:
                rstd("post", 2)
                rstd(pre, 0)
                square(pre, 1)
            else:
                square(pre, 1)
                rstd(pre, 0)
            hi(pre, 0)
            rstd(pre, 1)
            if B == 0:
                hi(pre, 1)
                square(pre, 2)
            else:
                square(pre, 2)
                hi(pre, 1)
            rstd(pre, 2)
            hi(pre, 2)
            if B == 2:
                for c in range(NC):
                    hi("mix", c)
                    act_kv_copies(act, c)

        def dve_boundary(dve, B):
            def post(c):
                s = steps[B]["post", c]
                dve.wait_ge(rs_done, s["stat"] + 1)
                for m, half in enumerate(HALVES):
                    for n in range(half.start, half.stop):
                        g = POST_G[B] + n
                        last = nc.vector.scalar_tensor_tensor(ACC[:, c, n], ACC[:, c, n], col(g), RS[:, c],
                                                              ALU.mult, ALU.mult)
                    last.then_inc(po_done, 1)
                    if m == 0 and B in (1, 3):
                        dve.wait_ge(h_in[c], 32 if B == 1 else 48)
                    dve.wait_ge(po_done, 2 * s["post"] + m + 1)
                    nc.vector.tensor_tensor(HC[:, c, half], HC[:, c, half], ACC[:, c, half], ALU.add).then_inc(ha_done, 1)

            def pre(kind, c):
                s = steps[B][kind, c]
                dve.wait_ge(rs_done, s["stat"] + 1 if kind != "mix" else steps[B]["kv", c]["stat"] + 1)
                if kind == "mix":
                    free_squares(dve, s)
                for half in HALVES:
                    for n in range(half.start, half.stop):
                        g = PRE_G[B, kind] + n
                        last = nc.vector.scalar_tensor_tensor(SQ[s["buf"]][:, n], HC[:, c, n], col(g), RS[:, c],
                                                              ALU.mult, ALU.mult)
                    last.then_inc(nm_done, 1)

            kind = "kv" if B == 2 else "pre"
            if B:
                post(0)
                post(1)
            if B < 4:
                pre(kind, 0)
            if B:
                post(2)
            if B < 4:
                pre(kind, 1)
                pre(kind, 2)
            if B == 2:
                for c in range(NC):
                    pre("mix", c)

        def pool_boundary(pool, B):
            for s in steps[B].values():
                if s["kind"] != "post":
                    for n, half in enumerate(HALVES):
                        pool.wait_ge(ah_done, 2 * s["act"] + n + 1)
                        last = nc.gpsimd.tensor_tensor(AL[:, half, chunk(s["c"])], SQ[s["buf"]][:, half],
                                                       AH[:, half, chunk(s["c"])].bitcast(fp32), ALU.subtract)
                    last.then_inc(al_done, 1)
            if B < 4:
                if B:
                    pool.wait_ge(ha_done, 2 * POSTS[B])
                else:
                    pool.wait_ge(rb_out, 16)
                nc.gpsimd.memset(ACC[:], 0.0).then_inc(az_done, 1)

        def pe_boundary(pe, B):
            if B:
                pe.wait_ge(dn_add, 24 * DOWNS[B])
            for s in steps[B].values():
                if s["kind"] != "mix":
                    st = s["stat"]
                    if st >= 2:
                        pe.wait_ge(ms_done, st - 1)
                    for m, half in enumerate(HALVES):
                        pe.wait_ge(sq_done, 2 * st + m + 1)
                        for n in range(half.start, half.stop):
                            last = nc.tensor.matmul(PS[:, 6 + st % 2, 0:CW], ones[:], SQ[s["buf"]][:, n],
                                                    start=(n == 0), stop=(n == KT - 1))
                    last.then_inc(ss_done, 1)
                if s["kind"] == "kv":
                    pe_kv(pe, s["c"], s["act"])

        def sp_boundary(sp, B):
            if B == 1:
                sp.wait_ge(st_out, 16 * H)
                sp.wait_ge(gp_out, 16 * H)
            if B in (1, 3):
                sp.wait_ge(dn_full, 24 * DOWNS[B] - 23)
            if B in (0, 1, 3):
                for c in range(NC):
                    if B == 3:
                        sp.wait_ge(h_out[c], 16)
                    sp.dma_start(HC[:, c], h_dram[c] if B == 3 else xT[c]).then_inc(h_in[c], 16)
            if B in (2, 4):
                for c in range(NC):
                    sp.wait_ge(ha_done, 2 * (POSTS[B - 1] + c) + 2)
                    sp.dma_start((h_dram if B == 2 else yT)[c], HC[:, c]).then_inc(h_out[c], 16)

        def w_load(sp, b, slot):
            sp.wait_ge(w_lo, b - 2)
            sp.dma_start(WR[:, slot], wall[bass.ds(b, 1)].rearrange("a p n -> p (a n)")).then_inc(w_in[slot], 16)

        def w_round(act, b, third, slot):
            act.wait_ge(w_in[slot], 16 * third + 16)
            nc.scalar.activation(WH[:, slot], WR[:, slot], ACT.Copy).then_inc(w_hi, 1)

        def w_rest(pool, b, slot):
            pool.wait_ge(w_hi, b + 1)
            nc.gpsimd.tensor_tensor(WL[:, slot], WR[:, slot], WH[:, slot].bitcast(fp32),
                                    ALU.subtract).then_inc(w_lo, 1)

        def w_rests(pool, first, end):
            b = first
            while b < end and b % 3:
                w_rest(pool, b, b % 3)
                b += 1
            whole = (end - b) // 3
            if whole > 0:
                with pool.Fori(0, whole) as i:
                    for s in range(3):
                        w_rest(pool, 3 * i + b + s, s)
            for x in range(b + 3 * max(whole, 0), end):
                w_rest(pool, x, x % 3)

        def w_loads(sp, first, end):
            b = first
            while b < end and b % 3:
                w_load(sp, b, b % 3)
                b += 1
            whole = (end - b) // 3
            if whole > 0:
                with sp.Fori(0, whole) as i:
                    for s in range(3):
                        w_load(sp, 3 * i + b + s, s)
            for x in range(b + 3 * max(whole, 0), end):
                w_load(sp, x, x % 3)

        def project(pe, bank, slot, c, full, hi=None, lo=None):
            for k in range(KT):
                wh, wl = WH[:, slot, k * P:(k + 1) * P], WL[:, slot, k * P:(k + 1) * P]
                for w, a, first in ((wl, AH, True), (wh, AL, False), (wh, AH, False)):
                    last = nc.tensor.matmul(PS[:, bank, 0:CW], w, a[:, k, chunk(c)],
                                            start=(k == 0 and first), stop=(k == KT - 1 and w is wh and a is AH))
            last.then_inc(full, 1)

        def down(pe, slots, hi, lo, n_before, idle=False, units=range(NC * KT)):
            for m in units:
                c, n = divmod(m, KT)
                if m >= 2 or not idle:
                    pe.wait_ge(dn_add, n_before + max(m - 1, 0))
                for t in range(2):
                    wh = WH[:, slots[t], n * P:(n + 1) * P]
                    wl = WL[:, slots[t], n * P:(n + 1) * P]
                    for x, (w, a) in enumerate(((wl, hi), (wh, lo), (wh, hi))):
                        last = nc.tensor.matmul(PS[:, 6 + m % 2, 0:CW], w, a[:, t, chunk(c)],
                                                start=(t == 0 and x == 0), stop=(t == 1 and x == 2))
                last.then_inc(dn_full, 1)

        def down_add(dve, n_before, units=range(NC * KT)):
            for m in units:
                dve.wait_ge(dn_full, n_before + m + 1)
                a = ACC[:, m // KT, m % KT]
                nc.vector.tensor_tensor(a, a, PS[:, 6 + m % 2, 0:CW], ALU.add).then_inc(dn_add, 1)

        def pe_gla(pe):
            pe.wait_ge(w_lo, W_GLR + 1)
            for c in range(NC):
                pe.wait_ge(al_done, c + 1)
                project(pe, c, W_GLR % 3, c, glr_full)
            pe.wait_ge(m0c_in, 16 * 4)
            pe.wait_ge(glr_ev, NC + 1)
            with pe.Fori(0, H) as h:
                b0 = HW * h + W_M0
                slot = [(W_M0 + p) % 3 for p in range(HW)]

                def level(n):
                    pe.wait_ge(lv_qk, 5 * h + n + 1)
                    if n:
                        pe.wait_ge(lv_m, 5 * h + n)
                    for c in range(NCHUNK):
                        x = slice(c * CH, (c + 1) * CH)
                        last = nc.tensor.matmul(PS[:, 6 + c // 4, (c % 4) * CH:(c % 4 + 1) * CH], KTl[:, x], QT[:, x],
                                                start=True, stop=True)
                    if n == 4:
                        x = slice(SEQ, T)
                        last = nc.tensor.matmul(PS[0:SAMP, 5, 0:SAMP], KTl[:, x], QT[:, x], start=True, stop=True)
                    last.then_inc(lv_pe, 1)

                pe.wait_ge(wg_in, 16 * h + 16)
                for c in range(NC):
                    nc.tensor.matmul(PS[:, 3 + c, 0:CW], WG[:], GLR[:, chunk(c)], start=True, stop=True).then_inc(m0_full, 1)
                for p in range(6):
                    pe.wait_ge(w_lo, b0 + p + 1)
                    for c in range(NC):
                        x = 3 + 3 * p + c
                        if p:
                            pe.wait_ge(m0_ev, 21 * h + x - 5)
                        project(pe, 3 * (p % 2) + c, slot[p], c, m0_full)
                    if p >= 2:
                        level(p - 2)
                pe.wait_ge(m0_ev, 21 * h + 21)
                for i in range(9):
                    n = CH if i < 8 else SAMP
                    for d in range(2):
                        last = nc.tensor.transpose(PS[0:n, i // 2, (i % 2) * DV + d * P:(i % 2) * DV + (d + 1) * P],
                                                   O[:, d, i * CH:i * CH + n], ident[:])
                last.then_inc(vt_full, 1)
                level(4)
                pe.wait_ge(in_qk, 2 * h + 1)
                pe.wait_ge(lv_a, 4 * h + 4)
                for c in range(NCHUNK):
                    nc.tensor.transpose(PS[:, 6 + c // 4, (c % 4) * CH:(c % 4 + 1) * CH], KTl[:, c * CH:(c + 1) * CH], ident[:])
                nc.tensor.transpose(PS[0:SAMP, 5, 0:P], KTl[:, SEQ:T], ident[:]).then_inc(kd_full, 1)
                pe.wait_ge(lv_a, 4 * h + 4)
                pe.wait_ge(in_qk, 2 * h + 2)
                pe.wait_ge(vt_ev, h + 1)
                pe.wait_ge(kd_ev, h + 1)
                for c in range(NCHUNK):
                    x = slice(c * CH, (c + 1) * CH)
                    if c >= 2:
                        pe.wait_ge(o_ev, 8 * h + c - 1)
                    if c:
                        pe.wait_ge(s_upd, 8 * h + c)
                    for d in range(2):
                        out = PS[:, c % 2, d * CH:(d + 1) * CH]
                        if c:
                            nc.tensor.matmul(out, S[:, d * P:(d + 1) * P], QT[:, x], start=True, stop=False)
                        last = nc.tensor.matmul(out, V[:, c, d * P:(d + 1) * P], AT[:, x], start=(c == 0), stop=True)
                    last.then_inc(o_full, 1)
                    nc.tensor.matmul(PS[:, 2 + c % 2, 0:DV], KD[:, c], V[:, c], start=True, stop=True).then_inc(s_full, 1)
                pe.wait_ge(st_in, 16 * h + 16)
                pe.wait_ge(vt_ev, h + 1)
                for d in range(2):
                    nc.tensor.matmul(PS[:, 4 + d, 0:SAMP], V[0:SAMP, 8, d * P:(d + 1) * P],
                                     AT[0:SAMP, SEQ:T], start=True, stop=False, skip_group_check=True)
                    for b in range(NB):
                        x = b * LS
                        last = nc.tensor.matmul(PS[:, 4 + d, x:x + LS], SB[:, b, d * P:(d + 1) * P],
                                                QT[:, SEQ + b * LS:SEQ + (b + 1) * LS], start=False, stop=(b == NB - 1),
                                                skip_group_check=True)
                last.then_inc(os_full, 1)
                pe.wait_ge(kdm, h + 1)
                for b in range(NB):
                    if b >= 2:
                        pe.wait_ge(ss_upd, 8 * h + b - 1)
                    nc.tensor.matmul(PS[:, 6 + b % 2, 0:DV], KDM[:, b], V[0:SAMP, 8, :],
                                     start=True, stop=True).then_inc(ss_full, 1)
                pe.wait_ge(gq_sq, h + 1)
                pe.wait_ge(s_upd, 8 * h + 8)
                for c in range(NC):
                    for d in range(2):
                        last = nc.tensor.matmul(PS[:, c, 0:CW], ones[:], SQ0[:, d, chunk(c)], start=(d == 0), stop=(d == 1))
                last.then_inc(gq_ss, 1)
                pe.wait_ge(gq_l, h + 1)
                pe.wait_ge(w_lo, b0 + 8)
                pe.wait_ge(ss_upd, 8 * h + 8)
                down(pe, (slot[6], slot[7]), OH0, OL0, 24 * h, idle=True)
                pe.wait_ge(dn_add, 24 * h + 24)

        def halves(buf, L):
            v = buf[:, 0:SEQ].rearrange("p (n s) -> p n s", s=2 * L)
            return v[:, :, 0:L], v[:, :, L:2 * L], v[:, :, L - 1:L]

        def dve_gla(dve):
            dve.wait_ge(al_done, ACTS[0])
            nc.vector.memset(GLR[:], 1.0).then_inc(glr_ev, 1)
            dve.wait_ge(m0c_in, 16 * 4)
            with dve.Fori(0, H) as h:
                dve.wait_ge(m0_ev, 21 * h + 3)
                nc.vector.scalar_tensor_tensor(T1[:], Z[:], -1.0, Z[:], ALU.mult, ALU.min).then_inc(az, 1)
                dve.wait_ge(ln, 2 * h + 2)
                nc.vector.scalar_tensor_tensor(Z[:], Z[:], 0.0, T1[:], ALU.min, ALU.subtract).then_inc(gt, 1)
                dve.wait_ge(gt, 2 * h + 1)
                nc.vector.tensor_scalar(B8[:], Z[:], GATE_FLOOR, None, ALU.max).then_inc(gt, 1)
                dve.wait_ge(gt, 2 * h + 2)
                nc.vector.tensor_tensor_scan(Z[:], SCM[:, 0], Z[:], 0.0, ALU.mult, ALU.add).then_inc(cs, 1)
                nc.vector.tensor_tensor_scan(B8[:], SCM[:, 1], B8[:], 0.0, ALU.mult, ALU.add).then_inc(cs, 1)
                dve.wait_ge(cs, 2 * h + 2)
                for n, L in enumerate(LEVELS):
                    left, right, ref = halves(Z, L)
                    tl, tr, _ = halves(T1, L)
                    shape = list(left.shape)
                    if n == 1:
                        dve.wait_ge(lv_m, 5 * h + 1)
                    if n >= 2:
                        dve.wait_ge(lv_a, 4 * h + n - 1)
                    nc.vector.tensor_tensor(tl, ref.broadcast_to(shape), left, ALU.subtract)
                    nc.vector.tensor_tensor(tr, right, ref.broadcast_to(shape), ALU.subtract).then_inc(lv_d, 1)
                    dve.wait_ge(lv_e, 5 * h + n + 1)
                    if n:
                        dve.wait_ge(lv_pe, 5 * h + n)
                    else:
                        dve.wait_ge(m0_ev, 21 * h + 9)
                    nc.vector.tensor_tensor(QT[:, 0:SEQ], Q[:, 0:SEQ], T1[:, 0:SEQ], ALU.mult)
                    nc.vector.tensor_tensor(KTl[:, 0:SEQ], K[:, 0:SEQ], T1[:, 0:SEQ], ALU.mult).then_inc(lv_qk, 1)
                    dve.wait_ge(lv_qk, 5 * h + n + 1)
                    mask_scores(dve, h, n)
                f = B8[:, 0:SEQ].rearrange("p (n s) -> p n s", s=FINE)
                o = T1[:, 0:SEQ].rearrange("p (n s) -> p n s", s=FINE)
                dve.wait_ge(lv_a, 4 * h + 3)
                nc.vector.tensor_tensor(o, f, f[:, :, FINE // 2 - 1:FINE // 2].broadcast_to(list(f.shape)), ALU.subtract)
                f = B8[:, SEQ:T].rearrange("p (n s) -> p n s", s=LS)
                o = T1[:, SEQ:T].rearrange("p (n s) -> p n s", s=LS)
                nc.vector.tensor_tensor(o, f, f[:, :, 1:2].broadcast_to(list(f.shape)), ALU.subtract).then_inc(lv_d, 1)
                dve.wait_ge(lv_e, 5 * h + 5)
                nc.vector.tensor_tensor(QT[:], Q[:], QT[:], ALU.mult)
                nc.vector.tensor_tensor(KTl[:], K[:], KTl[:], ALU.mult).then_inc(lv_qk, 1)
                mask_scores(dve, h, 4)
                f = Z[:, 0:SEQ].rearrange("p (n s) -> p n s", s=CH)
                o = T1[:, 0:SEQ].rearrange("p (n s) -> p n s", s=CH)
                dve.wait_ge(lv_a, 4 * h + 4)
                nc.vector.tensor_tensor(o, f[:, :, CH - 1:CH].broadcast_to(list(f.shape)), f, ALU.subtract)
                f = Z[:, SEQ:T].rearrange("p (n s) -> p n s", s=LS)
                o = T1[:, SEQ:T].rearrange("p (n s) -> p n s", s=LS)
                nc.vector.tensor_tensor(o, f[:, :, LS - 1:LS].broadcast_to(list(f.shape)), f, ALU.subtract).then_inc(in_d, 1)
                dve.wait_ge(in_e, h + 1)
                nc.vector.tensor_tensor(KTl[:], K[:], T1[:], ALU.mult).then_inc(in_qk, 1)
                nc.vector.tensor_tensor(QT[:], Q[:], QT[:], ALU.mult).then_inc(in_qk, 1)
                dve.wait_ge(kd_ev, h + 1)
                nc.vector.tensor_tensor(KDM[:], KDS[:].unsqueeze(1).broadcast_to([SAMP, NB, P]), bc(BMASK[:], P),
                                        ALU.mult).then_inc(kdm, 1)
                for c in range(NCHUNK):
                    dve.wait_ge(s_full, 8 * h + c + 1)
                    if c == 0:
                        nc.vector.tensor_copy(S[:], PS[:, 2, 0:DV]).then_inc(s_upd, 1)
                    else:
                        dve.wait_ge(s_upd, 8 * h + c)
                        nc.vector.scalar_tensor_tensor(S[:], S[:], EL[:, c:c + 1], PS[:, 2 + c % 2, 0:DV],
                                                       ALU.mult, ALU.add).then_inc(s_upd, 1)
                for b in range(NB):
                    dve.wait_ge(ss_full, 8 * h + b + 1)
                    nc.vector.scalar_tensor_tensor(SB[:, b], SB[:, b], EL[:, 8 + b:9 + b], PS[:, 6 + b % 2, 0:DV],
                                                   ALU.mult, ALU.add).then_inc(ss_upd, 1)
                dve.wait_ge(gq_rs, h + 1)
                for d in range(2):
                    nc.vector.scalar_tensor_tensor(O[:, d], O[:, d], col(G_GLA + d), RS0[:], ALU.mult, ALU.mult).then_inc(gq_o, 1)
                dve.wait_ge(gq_o, 3 * h + 2)
                dve.wait_ge(gq_si, h + 1)
                nc.vector.tensor_tensor(O[:], O[:], R[:], ALU.mult).then_inc(gq_o, 1)
                dve.wait_ge(gq_h, h + 1)
                dve.wait_ge(gp_out, 16 * h + 16)
                nc.vector.tensor_tensor(OL0[:], O[:], OH0[:].bitcast(fp32), ALU.subtract).then_inc(gq_l, 1)
                dve.wait_ge(az_done, 1)
                down_add(dve, 24 * h)
                dve.wait_ge(st_out, 16 * h + 16)

        def mask_scores(dve, h, n):
            dve.wait_ge(lv_pe, 5 * h + n + 1)
            dst = AT if n == 0 else T1
            nc.vector.tensor_tensor(dst[:, 0:SEQ].rearrange("p (c i) -> p c i", i=CH),
                                             PS[:, 6:8].rearrange("p b (c i) -> p (b c) i", i=CH),
                                             MLEV[:, n:n + 1].broadcast_to([P, NCHUNK, CH]), ALU.mult).then_inc(lv_m, 1)
            if n == 4:
                nc.vector.tensor_tensor(AT[0:SAMP, SEQ:T], PS[0:SAMP, 5, 0:SAMP], SMASK[:], ALU.mult)
            if n:
                dve.wait_ge(lv_m, 5 * h + n + 1)
                nc.vector.tensor_tensor(AT[:, 0:SEQ], AT[:, 0:SEQ], T1[:, 0:SEQ], ALU.add).then_inc(lv_a, 1)

        def act_gla(act):
            act.wait_ge(al_done, ACTS[0])
            for c in range(NC):
                act.wait_ge(glr_full, c + 1)
                act.wait_ge(glr_ev, 1)
                nc.scalar.activation(GLR[0:RANK, chunk(c)], PS[0:RANK, c, 0:CW], ACT.Copy).then_inc(glr_ev, 1)
            w_round(act, 3, 1, 0)
            with act.Fori(0, H) as h:
                slot = [(W_M0 + p) % 3 for p in range(HW)]
                third = [(W_M0 + p) // 3 for p in range(2 * HW)]

                def copy(dst, x0, **kw):
                    for c in range(NC):
                        x = x0 + c
                        act.wait_ge(m0_full, 21 * h + x + 1)
                        nc.scalar.activation(dst[:, chunk(c)], PS[:, (x + 3) % 6, 0:CW], ACT.Copy, **kw).then_inc(m0_ev, 1)

                def round_next(p):
                    w_round(act, HW * h + W_M0 + p + 3, 3 * h + third[p + 3], slot[p])

                copy(Z, 0)
                act.wait_ge(az, h + 1)
                nc.scalar.activation(T1[:], T1[:], ACT.Exp).then_inc(ln, 1)
                act.wait_ge(ln, 2 * h + 1)
                nc.scalar.activation(T1[:], T1[:], ACT.Ln, bias=1.0).then_inc(ln, 1)
                copy(Q, 3, scale=DK ** -0.5)
                round_next(0)
                copy(K, 6)
                round_next(1)

                def level(n):
                    act.wait_ge(lv_d, 5 * h + n + 1)
                    x = slice(0, SEQ)
                    if n < 4:
                        nc.scalar.activation(T1[:, x], T1[:, x], ACT.Exp, scale=1.0 / TAU).then_inc(lv_e, 1)
                    else:
                        act.wait_ge(lv_pe, 5 * h + 4)
                        nc.scalar.activation(QT[:], T1[:], ACT.Exp, scale=1.0 / TAU)
                        nc.scalar.activation(KTl[:], T1[:], ACT.Exp, scale=-1.0 / TAU).then_inc(lv_e, 1)

                level(0)
                copy(O[:, 0], 9)
                round_next(2)
                level(1)
                copy(O[:, 1], 12)
                round_next(3)
                level(2)
                copy(R[:, 0], 15)
                round_next(4)
                level(3)
                copy(R[:, 1], 18)
                round_next(5)
                act.wait_ge(vt_full, h + 1)
                for i in range(4):
                    nc.scalar.activation(V[:, 2 * i:2 * i + 2], PS[:, i].rearrange("p (a n) -> p a n", a=2), ACT.Copy)
                nc.scalar.activation(V[0:SAMP, 8], PS[0:SAMP, 4, 0:DV], ACT.Copy).then_inc(vt_ev, 1)
                level(4)
                act.wait_ge(in_d, h + 1)
                nc.scalar.activation(T1[:], T1[:], ACT.Exp, scale=1.0 / TAU)
                nc.scalar.activation(EL[:, 0:8], Z[:, CH - 1:SEQ:CH], ACT.Exp, scale=1.0 / TAU)
                nc.scalar.activation(EL[:, 8:16], Z[:, SEQ + LS - 1:T:LS], ACT.Exp, scale=1.0 / TAU)
                act.wait_ge(lv_pe, 5 * h + 5)
                nc.scalar.activation(QT[:], Z[:], ACT.Exp, scale=1.0 / TAU).then_inc(in_e, 1)
                act.wait_ge(kd_full, h + 1)
                act.wait_ge(in_qk, 2 * h + 2)
                nc.scalar.activation(KD[:].rearrange("p c n -> p (c n)").rearrange("p (b x) -> p b x", b=2), PS[:, 6:8], ACT.Copy)
                nc.scalar.activation(KDS[:], PS[0:SAMP, 5, 0:P], ACT.Copy).then_inc(kd_ev, 1)
                act.dma_start(SB[:], state[bass.ds(h, 1)].rearrange("a k b v -> k (a b) v")).then_inc(st_in, 16)
                for c in range(NCHUNK):
                    act.wait_ge(o_full, 8 * h + c + 1)
                    nc.scalar.activation(O[:, :, c * CH:(c + 1) * CH],
                                         PS[:, c % 2, 0:2 * CH].rearrange("p (d i) -> p d i", d=2), ACT.Copy).then_inc(o_ev, 1)
                act.wait_ge(os_full, h + 1)
                nc.scalar.activation(O[:, :, SEQ:T], PS[:, 4:6, 0:SAMP], ACT.Copy).then_inc(os_ev, 1)
                act.wait_ge(s_upd, 8 * h + 8)
                act.dma_start(gla_p[bass.ds(h, 1)].rearrange("a k v -> k (a v)"), S[:]).then_inc(gp_out, 16)
                act.wait_ge(o_ev, 8 * h + 8)
                act.wait_ge(os_ev, h + 1)
                nc.scalar.activation(SQ0[:], O[:], ACT.Square).then_inc(gq_sq, 1)
                nc.scalar.activation(R[:], R[:], ACT.Silu).then_inc(gq_si, 1)
                act.wait_ge(ss_upd, 8 * h + 8)
                act.dma_start(gla_s[bass.ds(h, 1)].rearrange("a k b v -> k (a b) v"), SB[:]).then_inc(st_out, 16)
                act.wait_ge(gq_ss, h + 1)
                nc.scalar.activation(RS0[:].rearrange("p (c n) -> p c n", c=NC), PS[:, 0:NC, 0:CW], ACT.Ln,
                                     bias=EPSC[:], scale=1.0 / DV).then_inc(gq_ms, 1)
                act.wait_ge(gq_ms, h + 1)
                nc.scalar.activation(RS0[:], RS0[:], ACT.Exp, scale=-0.5).then_inc(gq_rs, 1)
                act.wait_ge(gq_o, 3 * h + 3)
                nc.scalar.activation(OH0[:], O[:], ACT.Copy).then_inc(gq_h, 1)
                act.wait_ge(dn_full, 24 * h + 24)
                round_next(6)
                round_next(7)
                round_next(8)

        def sp_gla(sp):
            sp.wait_ge(al_done, ACTS[0])
            for dst, src in ((MLEV, masks), (SMASK, smask), (BMASK, bmask), (SCM, scanm)):
                sp.dma_start(dst[:], src).then_inc(m0c_in, 16)
            w_loads(sp, 3, 4)
            with sp.Fori(0, H) as h:
                sp.dma_start(WG[:], wgate[bass.ds(h, 1)].rearrange("a r n -> r (a n)")).then_inc(wg_in, 16)
                for p in range(HW):
                    if p == HW - 1:
                        sp.wait_ge(m0_ev, 21 * h + 21)
                    w_load(sp, HW * h + W_M0 + p + 3, (W_M0 + p) % 3)

        def pe_kv(pe, c, act):
            pe.wait_ge(al_done, act + 1)
            for x in range(2):
                if c == 0:
                    pe.wait_ge(w_lo, W_KV + x + 1)
                project(pe, 3 * x + c, (W_KV + x) % 3, c, kv_full)

        def act_kv_copies(act, c):
            if c == 0:
                act.wait_ge(cn_out, 16)
            for x, dst in ((0, KTT), (1, VTT)):
                act.wait_ge(kv_full, 2 * c + x + 1)
                nc.scalar.activation(dst[:, chunk(c)], PS[:, 3 * x + c, 0:CW], ACT.Copy).then_inc(kv_ev, 1)

        def act_kv(act):
            for x in range(3):
                w_round(act, W_KV + x + 3, (W_KV + x) // 3 + 1, (W_KV + x) % 3)
            act.wait_ge(kt_full, 1)
            act.wait_ge(al_done, ACTS[2])
            for i in range(3):
                n = 4 if i < 2 else 3
                last = nc.scalar.activation(KVTOK[:, 4 * i:4 * i + n].rearrange("p a n -> p (a n)"), PS[:, i, 0:n * P], ACT.Copy)
            last.then_inc(kt_ev, 1)

        def pe_kv_tokens(pe):
            pe.wait_ge(kv_ev, 2 * NC)
            tiles = [(VTT, i) for i in range(9)] + [(KTT, 7), (KTT, 8)]
            for x, (src, i) in enumerate(tiles):
                n = CH if i < 8 else SAMP
                last = nc.tensor.transpose(PS[0:n, x // 4, (x % 4) * P:(x % 4 + 1) * P], src[:, i * CH:i * CH + n], ident[:])
            last.then_inc(kt_full, 1)

        def sp_kv(sp):
            sp.wait_ge(kv_ev, 2 * NC)
            sp.dma_start(kt_dram, KTT[:]).then_inc(kv_out, 16)
            sp.wait_ge(kt_ev, 1)
            sp.dma_start(v_dram[0:SEQ].rearrange("(t p) d -> p t d", p=P), KVTOK[:, 0:8]).then_inc(kv_out, 16)
            sp.dma_start(v_dram[SEQ:T], KVTOK[0:SAMP, 8]).then_inc(kv_out, 16)
            sp.dma_start(vwin_p, KVTOK[:, 7]).then_inc(kw_out, 16)
            sp.dma_start(kwin_p, KVTOK[:, 9]).then_inc(kw_out, 16)
            for dst, tile, old in ((vwin_s, 8, cv), (kwin_s, 10, ck)):
                for b in range(NB):
                    sp.dma_start(dst[b, WIN - LS:WIN], KVTOK[b * LS:(b + 1) * LS, tile]).then_inc(kw_out, 16)
                sp.dma_start(dst[:, 0:WIN - LS], old[:, LS:WIN]).then_inc(kw_out, 16)

        def first_of_all(T_):
            return isinstance(T_, int) and T_ == 0

        def pe_ffn(pe, l):
            w0, d0, acts = (W_F0, W_F1)[l], (DOWNS[1], DOWNS[3])[l], (ACTS[1], ACTS[3])[l]

            def tile(T_, b, s, first):
                pe.wait_ge(w_lo, b + 1)
                if first:
                    pe.wait_ge(w_lo, b + 2)
                    for c in range(NC):
                        pe.wait_ge(al_done, acts - NC + c + 1)
                        if not first_of_all(T_):
                            pe.wait_ge(u_ev, 3 * T_ + c - 2)
                            pe.wait_ge(h_made, 3 * T_ + c - 2)
                        project(pe, c, s % 3, c, u_full)
                        project(pe, 3 + c, (s + 1) % 3, c, v_full)
                    return
                for c in range(NC):
                    if not first_of_all(T_):
                        pe.wait_ge(u_ev, 3 * T_ + c - 2)
                    project(pe, c, s % 3, c, u_full)
                pe.wait_ge(w_lo, b + 2)
                for c in range(NC):
                    if not first_of_all(T_):
                        pe.wait_ge(h_made, 3 * T_ + c - 2)
                    project(pe, 3 + c, (s + 1) % 3, c, v_full)

            def downs(D_, T_, b, s):
                pe.wait_ge(w_lo, b + 2)
                pe.wait_ge(hl, T_ + 1)
                down(pe, (s % 3, (s + 1) % 3), HH, HL, 24 * D_)

            t0 = FT * l
            tile(t0, w0, w0, True)
            tile(t0 + 1, w0 + 2, w0 + 2, False)
            with pe.Fori(1, FG) as g:
                b = w0 - 2 + 6 * g
                s = w0 + 4
                tile(2 * g + t0, b, s, False)
                downs(g + (d0 - 1), 2 * g + (t0 - 1), b + 2, s + 2)
                tile(2 * g + (t0 + 1), b + 4, s + 4, False)
            downs(d0 + FG - 1, t0 + FT - 1, w0 + 4 + 6 * (FG - 1), w0 + 4)

        def act_ffn(act, l):
            w0, d0, t0 = (W_F0, W_F1)[l], (DOWNS[1], DOWNS[3])[l], FT * l
            acts = ACTS[2 * l + 1]
            act.wait_ge(al_done, acts)
            act.wait_ge(u0_set, l + 1)

            def bias(T_):
                for c in range(NC):
                    act.wait_ge(u_full, 3 * T_ + c + 1)
                    if c == 0 and not first_of_all(T_):
                        act.wait_ge(cn, T_)
                    n = CW if c < 2 else SEQ - 2 * CW
                    last = nc.scalar.activation(U[:, 2 + c * CW:2 + c * CW + n], PS[:, c, 0:n], ACT.Copy)
                    if c == 2:
                        last = nc.scalar.activation(U[:, UP:UW].rearrange("p (b s) -> p b s", s=2 + LS)[:, :, 2:2 + LS],
                                                    PS[:, 2, n:CW].rearrange("p (b s) -> p b s", s=LS), ACT.Copy)
                    last.then_inc(u_ev, 1)
                act.wait_ge(u_ev, 3 * T_ + 3)
                act.wait_ge(pre, T_ + 1)
                if not first_of_all(T_):
                    act.wait_ge(h_made, 3 * T_)
                nc.scalar.activation(C[:, 0:CV], U[:, 2:UW], ACT.Identity, bias=PC[:, 19:20], scale=PC[:, 18:19]).then_inc(cb, 1)

            def gelu(T_):
                act.wait_ge(cv2, T_ + 1)
                nc.scalar.activation(C[:, 0:CV], C[:, 0:CV], ACT.Gelu_apprx_tanh).then_inc(gl, 1)

            def hi(T_, t):
                act.wait_ge(h_made, 3 * T_ + 3)
                nc.scalar.activation(HH[:, t], HF[:], ACT.Copy).then_inc(hh, 1)

            def tile(T_, nxt):
                bias(T_)
                nxt(0)
                gelu(T_)
                act.wait_ge(v_full, 3 * T_ + 3)
                nxt(1)

            def rnd(b, third, s):
                w_round(act, b, third, s % 3)

            for t in range(2):
                tile(t0 + t, lambda x: rnd(w0 + 2 * t + x + 3, (w0 + 2 * t + x + 3) // 3, w0 + 2 * t + x))
                hi(t0 + t, t)
            with act.Fori(1, FG) as g:
                b = w0 - 2 + 6 * g
                s = w0 + 4

                def at(p):
                    rnd(b + p + 3, 2 * g + (s + p + 3) // 3 - 2, s + p)

                tile(2 * g + t0, at)
                act.wait_ge(dn_full, 24 * g + 24 * d0)
                at(2)
                at(3)
                hi(2 * g + t0, 0)
                tile(2 * g + (t0 + 1), lambda x: at(4 + x))
                hi(2 * g + (t0 + 1), 1)
            act.wait_ge(dn_full, 24 * (d0 + FG))
            for x in range(2):
                b = w0 + 4 + 6 * (FG - 1) + x + 3
                if b < W_END:
                    rnd(b, b // 3, b)

        def dve_ffn(dve, l):
            d0, t0 = (DOWNS[1], DOWNS[3])[l], FT * l
            dve.wait_ge(al_done, ACTS[2 * l + 1])
            nc.vector.memset(U[:, 0:2], 0.0).then_inc(u0_set, 1)
            dve.wait_ge(fp_in, 16 * (l + 1))

            def conv(T_, t):
                if not first_of_all(T_):
                    dve.wait_ge(cb, T_)
                    dve.wait_ge(cv2, T_)
                nc.vector.tensor_copy(PC[:], PAR[:, bass.ds(t, 1)].rearrange("p a n -> p (a n)")).then_inc(pc, 1)
                dve.wait_ge(pc, T_ + 1)
                if not first_of_all(T_):
                    dve.wait_ge(cn, T_)
                nc.vector.tensor_copy(U[:, UP:UW].rearrange("p (b s) -> p b s", s=2 + LS)[:, :, 0:2],
                                      PC[:, 0:16].rearrange("p (b s) -> p b s", s=2)).then_inc(pre, 1)
                dve.wait_ge(cb, T_ + 1)
                nc.vector.scalar_tensor_tensor(C[:, 0:CV], U[:, 1:1 + CV], PC[:, 17:18], C[:, 0:CV], ALU.mult, ALU.add).then_inc(cv1, 1)
                dve.wait_ge(cv1, T_ + 1)
                nc.vector.scalar_tensor_tensor(C[:, 0:CV], U[:, 0:CV], PC[:, 16:17], C[:, 0:CV], ALU.mult, ALU.add).then_inc(cv2, 1)
                nc.vector.tensor_copy(CN[:, bass.ds(t, 1), 0:2].rearrange("p a n -> p (a n)"), U[:, SEQ:SEQ + 2])
                nc.vector.tensor_copy(CN[:, bass.ds(t, 1), 2:18].rearrange("p a (b s) -> p (a b) s", s=2),
                                      U[:, UP:UW].rearrange("p (b s) -> p b s", s=2 + LS)[:, :, LS:LS + 2]).then_inc(cn, 1)

            def product(T_):
                dve.wait_ge(gl, T_ + 1)
                if not first_of_all(T_):
                    dve.wait_ge(hl, T_)
                for c in range(NC):
                    dve.wait_ge(v_full, 3 * T_ + c + 1)
                    n = CW if c < 2 else SEQ - 2 * CW
                    last = nc.vector.tensor_tensor(HF[:, c * CW:c * CW + n], C[:, c * CW:c * CW + n], PS[:, 3 + c, 0:n], ALU.mult)
                    if c == 2:
                        last = nc.vector.tensor_tensor(
                            HF[:, SEQ:T].rearrange("p (b s) -> p b s", s=LS),
                            C[:, UP:UW].rearrange("p (b s) -> p b s", s=2 + LS)[:, :, 0:LS],
                            PS[:, 5, n:CW].rearrange("p (b s) -> p b s", s=LS), ALU.mult)
                    last.then_inc(h_made, 1)

            def lo(T_, t):
                dve.wait_ge(hh, T_ + 1)
                nc.vector.tensor_tensor(HL[:, t], HF[:], HH[:, t].bitcast(fp32), ALU.subtract).then_inc(hl, 1)

            for t in range(2):
                conv(t0 + t, t)
                product(t0 + t)
                lo(t0 + t, t)
            dve.wait_ge(az_done, 2 * l + 2)
            with dve.Fori(1, FG) as g:
                conv(2 * g + t0, 2 * g)
                product(2 * g + t0)
                down_add(dve, 24 * g + 24 * (d0 - 1))
                lo(2 * g + t0, 0)
                conv(2 * g + (t0 + 1), 2 * g + 1)
                product(2 * g + (t0 + 1))
                lo(2 * g + (t0 + 1), 1)
            down_add(dve, 24 * (d0 + FG - 1))

        def sp_ffn(sp, l):
            w0 = (W_F0, W_F1)[l]
            sp.wait_ge(al_done, ACTS[2 * l + 1])
            if l:
                sp.wait_ge(cn_out, 16)
            sp.dma_start(PAR[:], ffnpar[l]).then_inc(fp_in, 16)
            w_loads(sp, w0 + 3, min(w0 + 3 * FT + 3, W_END))
            sp.wait_ge(cn, FT * (l + 1))
            sp.dma_start(conv_new[l], CN[:]).then_inc(cn_out, 16)

        NIT = 4 * NBLK
        UT = (T - SEQ) * 2

        def pe_attn(pe):
            pe.wait_ge(al_done, ACTS[2])
            pe.wait_ge(kt_ev, 1)
            pe.wait_ge(one, 1)
            with pe.Fori(0, NKV) as n:
                slot = [(W_M1 + p) % 3 for p in range(HW)]
                b = HW * n + W_M1
                pe.wait_ge(dn_add, 48 * n + 24 * DOWNS[2])

                def query(x):
                    t, c = divmod(x, NC)
                    if c == 0:
                        pe.wait_ge(w_lo, b + t + 1)
                    if x >= 8:
                        pe.wait_ge(q_ev, 12 * n + x - 1)
                    project(pe, x if x < 6 else 6 + x % 2, slot[t], c, q_full)

                def scores(it):
                    t, i = divmod(it, NBLK)
                    if it >= 2:
                        pe.wait_ge(sa, NIT * n + it - 1)
                    for e in range(2):
                        x = slice(64 * e, 64 * e + 64)
                        q = Q1[x, t, i * WIN:(i + 1) * WIN]
                        bank = 2 * (it % 2) + e
                        if i:
                            last = nc.tensor.matmul(PS[:, bank, 0:2 * WIN], q, KG[x, (i - 1) * WIN:(i + 1) * WIN],
                                                    start=True, stop=True)
                        else:
                            last = nc.tensor.matmul(PS[:, bank, WIN:2 * WIN], q, KG[x, 0:WIN], start=True, stop=True)
                    last.then_inc(sf, 1)

                def transposed(it):
                    i = it % NBLK
                    pe.wait_ge(es, NIT * n + it + 1)
                    if it >= 2:
                        pe.wait_ge(te, NIT * n + it - 1)
                    else:
                        pe.wait_ge(xol, 4 * n + 2)
                    for e in range(2):
                        for k in range(0 if i else 1, 2):
                            m = 2 * e + k
                            last = nc.tensor.transpose(PS[:, 4 + it % 2, m * P:(m + 1) * P],
                                                       SS[:, it % 3, e, k * WIN:(k + 1) * WIN], ident[:])
                    last.then_inc(tf, 1)

                def values(it):
                    i = it % NBLK
                    pe.wait_ge(te, NIT * n + it + 1)
                    if it:
                        pe.wait_ge(on, NIT * n + it)
                    for e in range(2):
                        for k in range(0 if i else 1, 2):
                            last = nc.tensor.matmul(PS[:, 6, 64 * e:64 * e + 64], PT[:, it % 2, 2 * e + k],
                                                    VG[:, i - 1 + k], start=(k == 0 or i == 0), stop=(k == 1))
                    last.then_inc(of, 1)

                def turned(it):
                    pe.wait_ge(on, NIT * n + it + 1)
                    if it:
                        pe.wait_ge(xl, NIT * n + it)
                    nc.tensor.transpose(PS[:, 7, 0:P], OT[:, it % 2], ident[:]).then_inc(xf, 1)

                def s_scores(j):
                    for e in range(2):
                        x = slice(64 * e, 64 * e + 64)
                        q = QS[x, 2 * j:2 * j + 2].rearrange("p t m -> p (t m)")
                        for half in range(2):
                            nc.tensor.matmul(PS[x, 2 * e + half, :], q,
                                             KCG[x, 4 * half:4 * half + 4].rearrange("p b k -> p (b k)"), start=True, stop=True)
                        last = nc.tensor.matmul(PS[x, 4 + e, 0:SAMP], q, KG[x, SEQ:T], start=True, stop=True)
                    last.then_inc(xsf, 1)

                def s_transposed(j):
                    pe.wait_ge(xsc, 2 * n + j + 1)
                    for b_ in range(NB):
                        nc.tensor.transpose(PS[:, b_ // 4, (b_ % 4) * P:(b_ % 4 + 1) * P], SX[:, b_ * WIN:(b_ + 1) * WIN], ident[:])
                    nc.tensor.transpose(PS[0:SAMP, 2, 0:P], SX[:, SEQ:T], ident[:]).then_inc(xtf, 1)

                def s_values(j):
                    pe.wait_ge(xte, 2 * n + j + 1)
                    for e in range(2):
                        y = slice(64 * e, 64 * e + 64)
                        for b_ in range(NB):
                            nc.tensor.matmul(PS[y, 4 + e, 0:UT], VCG[:, b_], PX[:, b_, y], start=(b_ == 0), stop=False)
                        last = nc.tensor.matmul(PS[y, 4 + e, 0:UT], VG[0:SAMP, 8], PXN[:, y], start=False, stop=True)
                    last.then_inc(xof, 1)

                for x in range(7):
                    query(x)
                pe.wait_ge(kg_in, 112 * n + 112)
                pe.wait_ge(q_ev, 12 * n + 6)
                query(7)
                s_scores(0)
                query(8)
                query(9)
                query(10)
                s_transposed(0)
                query(11)
                s_values(0)
                pe.wait_ge(q_ev, 12 * n + 12)
                for s in range(NIT + 7):
                    if s < NIT:
                        scores(s)
                    if 3 <= s < NIT + 3:
                        transposed(s - 3)
                    if 5 <= s < NIT + 5:
                        values(s - 5)
                    if s == NIT + 4:
                        s_scores(1)
                    if s >= 7:
                        turned(s - 7)

                pe.wait_ge(w_lo, b + 6)
                pe.wait_ge(xl, NIT * n + NIT)
                pe.wait_ge(xol, 4 * n + 2)
                before = 48 * n + 24 * DOWNS[2]
                down(pe, (slot[4], slot[5]), OH1, OL1, before, idle=True, units=range(0, 14))
                s_transposed(1)
                down(pe, (slot[4], slot[5]), OH1, OL1, before, units=range(14, 18))
                s_values(1)
                down(pe, (slot[4], slot[5]), OH1, OL1, before, units=range(18, 24))
                pe.wait_ge(w_lo, b + 8)
                pe.wait_ge(xol, 4 * n + 4)
                down(pe, (slot[6], slot[7]), OH2, OL2, before + 24)

        def dve_attn(dve):
            dve.wait_ge(a_c_in, 16 * 3)
            dve.wait_ge(az_done, 3)
            with dve.Fori(0, NKV) as n:
                nc.vector.tensor_copy(SKG[:, 0:8], SINK[:, bass.ds(8 * n, 8)])
                nc.vector.tensor_copy(SKG[:, 8:10], SKS[:, bass.ds(2 * n, 2)]).then_inc(skg, 1)
                dve.wait_ge(skg, n + 1)
                dve.wait_ge(bi_in, 256 * n + 256)

                def biased(it):
                    t, i = divmod(it, NBLK)
                    u, r = it % 3, it % 8
                    x0 = 0 if i else WIN
                    dve.wait_ge(sf, NIT * n + it + 1)
                    if it >= 3:
                        dve.wait_ge(tf, NIT * n + it - 2)
                    bank = 2 * (it % 2)
                    nc.vector.tensor_tensor(SS[:, u, :, x0:], PS[:, bank:bank + 2, x0:2 * WIN],
                                            BI[:, 2 * t:2 * t + 2, x0:], ALU.add).then_inc(sa, 1)
                    dve.wait_ge(sa, NIT * n + it + 1)
                    nc.vector.tensor_reduce(ST[:, r, 0:2], SS[:, u, :, x0:], AX.X, ALU.max).then_inc(mx, 1)
                    if it >= 7:
                        lo(it - 7)
                    dve.wait_ge(mx, NIT * n + it + 1)
                    nc.vector.tensor_tensor(ST[:, r, 0:2], ST[:, r, 0:2], SKG[:, 2 * t:2 * t + 2], ALU.max).then_inc(mm_, 1)
                    dve.wait_ge(mm_, NIT * n + it + 1)
                    nc.vector.tensor_tensor(ST[:, r, 4:6], SKG[:, 2 * t:2 * t + 2], ST[:, r, 0:2], ALU.subtract)
                    nc.vector.tensor_scalar(ST[:, r, 2:4], ST[:, r, 0:2], -1.0, None, ALU.mult).then_inc(nm, 1)

                def scaled(it):
                    r = it % 8
                    dve.wait_ge(es, NIT * n + it + 1)
                    nc.vector.tensor_tensor(ST[:, r, 6:8], ST[:, r, 6:8], ST[:, r, 8:10], ALU.add).then_inc(den, 1)
                    dve.wait_ge(den, NIT * n + it + 1)
                    nc.vector.reciprocal(ST[:, r, 10:12], ST[:, r, 6:8]).then_inc(rc, 1)
                    dve.wait_ge(rc, NIT * n + it + 1)
                    dve.wait_ge(of, NIT * n + it + 1)
                    if it >= 2:
                        dve.wait_ge(xf, NIT * n + it - 1)
                    nc.vector.tensor_tensor(OT[:, it % 2].rearrange("p (e d) -> p e d", e=2),
                                            PS[:, 6, 0:P].rearrange("p (e d) -> p e d", e=2),
                                            bc(ST[:, r, 10:12], HD), ALU.mult).then_inc(on, 1)

                def lo(it):
                    t, i = divmod(it, NBLK)
                    x = slice(i * WIN, (i + 1) * WIN)
                    oh, ol = (OH1, OL1) if t < 2 else (OH2, OL2)
                    dve.wait_ge(xh, NIT * n + it + 1)
                    nc.vector.tensor_tensor(ol[:, t % 2, x], PS[:, 7, 0:P], oh[:, t % 2, x].bitcast(fp32), ALU.subtract).then_inc(xl, 1)

                def s_max(j):
                    I = 2 * n + j
                    dve.wait_ge(xsb, I + 1)
                    nc.vector.tensor_reduce(SST[:, 0:1], SX[:], AX.X, ALU.max).then_inc(xmx, 1)
                    dve.wait_ge(xmx, 3 * I + 1)
                    nc.vector.tensor_tensor(SST[:, 0:1], SST[:, 0:1], SKG[:, 8 + j:9 + j], ALU.max).then_inc(xmx, 1)
                    dve.wait_ge(xmx, 3 * I + 2)
                    nc.vector.tensor_tensor(SST[:, 2:3], SKG[:, 8 + j:9 + j], SST[:, 0:1], ALU.subtract)
                    nc.vector.tensor_scalar(SST[:, 1:2], SST[:, 0:1], -1.0, None, ALU.mult).then_inc(xmx, 1)

                def s_scaled(j):
                    I = 2 * n + j
                    dve.wait_ge(xex, I + 1)
                    nc.vector.tensor_tensor(SST[:, 4:5], SST[:, 4:5], SST[:, 5:6], ALU.add).then_inc(xrc, 1)
                    dve.wait_ge(xrc, 2 * I + 1)
                    nc.vector.reciprocal(SST[:, 6:7], SST[:, 4:5]).then_inc(xrc, 1)
                    dve.wait_ge(xrc, 2 * I + 2)
                    nc.vector.tensor_scalar(SX[:], SX[:], SST[:, 6:7], None, ALU.mult).then_inc(xsc, 1)

                def s_lo(j):
                    oh, ol = (OH1, OL1) if j == 0 else (OH2, OL2)
                    for e in range(2):
                        y = slice(64 * e, 64 * e + 64)
                        dve.wait_ge(xoh, 2 * (2 * n + j) + 2)
                        nc.vector.tensor_tensor(ol[y, :, SEQ:T], PS[y, 4 + e, 0:UT].rearrange("p (t m) -> p t m", t=2),
                                                oh[y, :, SEQ:T].bitcast(fp32), ALU.subtract).then_inc(xol, 1)

                for e in range(2):
                    s_add(dve, n, 0, e)
                s_masked(dve, n, 0)
                s_max(0)
                s_scaled(0)
                s_lo(0)
                for s in range(1, NIT + 8):
                    if s >= 6 and s - 6 < NIT:
                        scaled(s - 6)
                    if s <= NIT:
                        biased(s - 1)
                    elif s >= 8:
                        lo(s - 8)
                before = 48 * n + 24 * DOWNS[2]
                for m in range(NC * KT):
                    down_add(dve, before, units=[m])
                    if m < 2:
                        s_add(dve, n, 1, m)
                    elif m == 2:
                        s_masked(dve, n, 1)
                    elif m == 4:
                        s_max(1)
                    elif m == 8:
                        s_scaled(1)
                    elif m == 21:
                        s_lo(1)
                down_add(dve, before + 24)

        def s_add(dve, n, j, e):
            y = slice(64 * e, 64 * e + 64)
            dve.wait_ge(xsf, 2 * n + j + 1)
            nc.vector.tensor_tensor(SX[y, 0:SEQ].rearrange("p (b k) -> p b k", b=NB),
                                    PS[y, 2 * e:2 * e + 2].rearrange("p h (b k) -> p (h b) k", b=4),
                                    SBC[y, j, 0:WIN].unsqueeze(1).broadcast_to([64, NB, WIN]), ALU.add)
            nc.vector.tensor_tensor(SX[y, SEQ:T].rearrange("p (b k) -> p b k", b=NB),
                                    PS[y, 4 + e, 0:SAMP].rearrange("p (b k) -> p b k", b=NB),
                                    SBC[y, j, WIN:WIN + LS].unsqueeze(1).broadcast_to([64, NB, LS]), ALU.add).then_inc(xsa, 1)

        def s_masked(dve, n, j):
            dve.wait_ge(xsa, 2 * (2 * n + j) + 2)
            nc.vector.tensor_tensor(SX[:, 0:SEQ].rearrange("p (b k) -> p b k", b=NB),
                                    SX[:, 0:SEQ].rearrange("p (b k) -> p b k", b=NB), bc(BM4[:], WIN), ALU.add)
            nc.vector.tensor_tensor(SX[:, SEQ:T], SX[:, SEQ:T], SM4[:], ALU.add).then_inc(xsb, 1)

        def act_attn(act):
            act.wait_ge(kw_out, 16 * 20)
            act.wait_ge(kv_out, 16 * 3)
            for c in range(NC):
                act.wait_ge(h_out[c], 16)
            with act.Fori(0, NKV) as n:
                slot = [(W_M1 + p) % 3 for p in range(HW)]
                third = [(W_M1 + p) // 3 for p in range(HW + 3)]

                def round_next(p):
                    w_round(act, HW * n + W_M1 + p + 3, 3 * n + third[p + 3], slot[p])

                def query(x):
                    t, c = divmod(x, NC)
                    act.wait_ge(q_full, 12 * n + x + 1)
                    bank = x if x < 6 else 6 + x % 2
                    if c == 2:
                        nc.scalar.activation(QS[:, t], PS[:, bank, CW - SAMP:CW], ACT.Copy, scale=HD ** -0.5)
                    nc.scalar.activation(Q1[:, t, chunk(c)], PS[:, bank, 0:CW], ACT.Copy, scale=HD ** -0.5).then_inc(q_ev, 1)
                    if c == 2:
                        round_next(t)

                def exps(it):
                    u, r, i = it % 3, it % 8, it % NBLK
                    x0 = 0 if i else WIN
                    act.wait_ge(nm, NIT * n + it + 1)
                    for e in range(2):
                        nc.scalar.activation(SS[:, u, e, x0:], SS[:, u, e, x0:], ACT.Exp, bias=ST[:, r, 2 + e:3 + e],
                                             accum_out=ST[:, r, 6 + e:7 + e])
                    nc.scalar.activation(ST[:, r, 8:10], ST[:, r, 4:6], ACT.Exp).then_inc(es, 1)

                def turn(it):
                    u, i = it % 2, it % NBLK
                    act.wait_ge(tf, NIT * n + it + 1)
                    if it >= 2:
                        act.wait_ge(of, NIT * n + it - 1)
                    if i:
                        nc.scalar.activation(PT[:, u].rearrange("p m q -> p (m q)"), PS[:, 4 + u], ACT.Copy).then_inc(te, 1)
                    else:
                        nc.scalar.activation(PT[:, u, 1:4:2], PS[:, 4 + u].rearrange("p (m q) -> p m q", q=P)[:, 1:4:2],
                                             ACT.Copy).then_inc(te, 1)

                def hi(it):
                    t, i = divmod(it, NBLK)
                    oh = OH1 if t < 2 else OH2
                    act.wait_ge(xf, NIT * n + it + 1)
                    nc.scalar.activation(oh[:, t % 2, i * WIN:(i + 1) * WIN], PS[:, 7, 0:P], ACT.Copy).then_inc(xh, 1)

                def s_exps(j):
                    act.wait_ge(xmx, 3 * (2 * n + j) + 3)
                    nc.scalar.activation(SX[:], SX[:], ACT.Exp, bias=SST[:, 1:2], accum_out=SST[:, 4:5])
                    nc.scalar.activation(SST[:, 5:6], SST[:, 2:3], ACT.Exp).then_inc(xex, 1)

                def s_turn(j):
                    act.wait_ge(xtf, 2 * n + j + 1)
                    nc.scalar.activation(PX[:].rearrange("p (h b) n -> p h (b n)", h=2), PS[:, 0:2], ACT.Copy)
                    nc.scalar.activation(PXN[:], PS[0:SAMP, 2, 0:P], ACT.Copy).then_inc(xte, 1)

                def s_hi(j):
                    oh = OH1 if j == 0 else OH2
                    for e in range(2):
                        y = slice(64 * e, 64 * e + 64)
                        act.wait_ge(xof, 2 * n + j + 1)
                        nc.scalar.activation(oh[y, :, SEQ:T], PS[y, 4 + e, 0:UT].rearrange("p (t m) -> p t m", t=2),
                                             ACT.Copy).then_inc(xoh, 1)

                for x in range(10):
                    query(x)
                s_exps(0)
                query(10)
                s_turn(0)
                query(11)
                s_hi(0)
                for s in range(2, NIT + 8):
                    if s >= 8:
                        hi(s - 8)
                    if 4 <= s < NIT + 4:
                        turn(s - 4)
                    if s < NIT + 2:
                        exps(s - 2)
                s_exps(1)
                s_turn(1)
                s_hi(1)
                act.wait_ge(dn_full, 48 * n + 24 * DOWNS[2] + 24)
                round_next(4)
                round_next(5)
                act.wait_ge(dn_full, 48 * n + 24 * DOWNS[2] + 48)
                for p in range(6, HW):
                    round_next(p)

        def sp_attn(sp):
            sp.wait_ge(kv_out, 16 * 3)
            sp.wait_ge(kw_out, 16 * 20)
            sp.wait_ge(al_done, ACTS[2])
            for c in range(NC):
                sp.wait_ge(h_out[c], 16)
            for dst, src in ((BM4, bmask4), (SM4, smask4), (SKS, sinks[1, :, 0:2 * NKV])):
                sp.dma_start(dst[:], src).then_inc(a_c_in, 16)
            with sp.Fori(0, NKV) as n:
                sp.wait_ge(dn_full, 48 * n + 24 * DOWNS[2])
                for e in range(2):
                    x = slice(64 * e, 64 * e + 64)
                    sp.dma_start(KG[x], kt_dram[bass.ds(64 * n, 64)]).then_inc(kg_in, 16)
                    sp.dma_start(KCG[x], kcT[bass.ds(64 * n, 64)]).then_inc(kg_in, 16)
                sp.dma_start(VG[:, 0:8], v_dram[0:SEQ].rearrange("(t p) d -> p t d", p=P)[:, :, bass.ds(64 * n, 64)]).then_inc(kg_in, 16)
                sp.dma_start(VG[0:SAMP, 8], v_dram[SEQ:T, bass.ds(64 * n, 64)]).then_inc(kg_in, 16)
                sp.dma_start(VCG[:], vc[:, :, bass.ds(64 * n, 64)]).then_inc(kg_in, 16)
                for x in range(8):
                    h0 = (8 * n + x) * (P * RL)
                    sp.dma_start(BI[:, x], bass.AP(r_dram.tensor, h0 + (WIN - 1), [[RL - 1, P], [1, 2 * WIN]])).then_inc(bi_in, 16)
                    j, t, e = x // 4, x // 2 % 2, x % 2
                    y = 64 * e + 32 * t
                    sp.dma_start(SBC[y:y + 32, j], bass.AP(r_dram.tensor, h0 + (WIN - 1), [[0, NB], [RL - 1, LS], [1, WIN + LS]])).then_inc(bi_in, 16)
                for p in range(HW):
                    w_load(sp, HW * n + W_M1 + p + 3, (W_M1 + p) % 3)

        block = ctx.enter_context(nc.Block())

        @block.sync
        def _(sp):
            for dst, src in ((ident, ident_in), (GC, gains), (SINK, sinks[0])):
                sp.dma_start(dst[:], src).then_inc(c_in, 16)
            sp_boundary(sp, 0)
            for b in range(3):
                sp.dma_start(WR[:, b], wall[b]).then_inc(w_in[b], 16)
            sp.dma_start(OHR[:], onehot).then_inc(tb_in, 16)
            sp.wait_ge(tb_one, 1)
            sp.dma_start(TBL[0:32], table).then_inc(tb_in, 16)
            sp.wait_ge(rb_row, NQ)
            sp.dma_start(r_dram.rearrange("(h p m) -> p h m", p=P, m=RL), RB[:]).then_inc(rb_out, 16)
            sp_gla(sp)
            sp_boundary(sp, 1)
            sp_ffn(sp, 0)
            sp_boundary(sp, 2)
            w_loads(sp, W_KV + 3, W_M1 + 3)
            sp_kv(sp)
            sp_attn(sp)
            sp_boundary(sp, 3)
            sp_ffn(sp, 1)
            sp_boundary(sp, 4)
            for c in range(NC):
                sp.wait_ge(h_out[c], 32)
            sp.wait_ge(cn_out, 32)
            sp.wait_ge(gp_out, 16 * H)
            sp.wait_ge(st_out, 16 * H)
            sp.wait_ge(kw_out, 16 * 20)
            sp.wait_ge(kv_out, 16 * 3)
            sp.wait_ge(rb_out, 16)

        @block.gpsimd
        def _(pool):
            w_rests(pool, 0, 3)
            pool_boundary(pool, 0)
            w_rests(pool, 3, W_F0 + 3)
            pool_boundary(pool, 1)
            w_rests(pool, W_F0 + 3, W_KV + 3)
            pool_boundary(pool, 2)
            w_rests(pool, W_KV + 3, W_F1 + 3)
            pool_boundary(pool, 3)
            w_rests(pool, W_F1 + 3, W_END)
            pool_boundary(pool, 4)

        @block.vector
        def _(dve):
            nc.vector.memset(EPSC[:], EPS)
            nc.vector.memset(ones[:], 1.0).then_inc(one, 1)
            nc.vector.memset(TBL[:], 1.0).then_inc(tb_one, 1)
            dve.wait_ge(tb_in, 32)
            nc.vector.tensor_copy(TBB[:], bc(TBL[:], P)).then_inc(tb_cols, 1)
            for h in range(NQ):
                dve.wait_ge(rb_full, h + 1)
                nc.vector.tensor_copy(RB[:, h], PS[:, h % 6, 0:RL]).then_inc(rb_row, 1)
            dve.wait_ge(c_in, 48)
            dve_boundary(dve, 0)
            dve_gla(dve)
            dve_boundary(dve, 1)
            dve_ffn(dve, 0)
            dve_boundary(dve, 2)
            dve_attn(dve)
            dve_boundary(dve, 3)
            dve_ffn(dve, 1)
            dve_boundary(dve, 4)

        @block.scalar
        def _(act):
            for b in range(3):
                w_round(act, b, 0, b)
            act.wait_ge(rb_full, NQ)
            act.wait_ge(one, 1)
            act_boundary(act, 0)
            act_gla(act)
            act_boundary(act, 1)
            act_ffn(act, 0)
            act_boundary(act, 2)
            act_kv(act)
            act_attn(act)
            act_boundary(act, 3)
            act_ffn(act, 1)
            act_boundary(act, 4)

        @block.tensor
        def _(pe):
            pe.wait_ge(tb_cols, 1)
            for h in range(NQ):
                if h >= 6:
                    pe.wait_ge(rb_row, h - 5)
                nc.tensor.matmul(PS[:, h % 6, 0:RL], TBB[:, h], OHR[:], start=True, stop=True).then_inc(rb_full, 1)
            pe.wait_ge(c_in, 48)
            pe.wait_ge(one, 1)
            pe.wait_ge(rb_row, NQ)
            pe_boundary(pe, 0)
            pe_gla(pe)
            pe_boundary(pe, 1)
            pe_ffn(pe, 0)
            pe_boundary(pe, 2)
            pe_kv_tokens(pe)
            pe_attn(pe)
            pe_boundary(pe, 3)
            pe_ffn(pe, 1)
            pe_boundary(pe, 4)


def _constants():
    one = np.zeros((33, RL), np.float32)
    for m in range(RL):
        n = 255 - m
        if 0 <= n < WIN:
            if n < 16:
                bucket = n
            else:
                large = 16 + int(np.float32(np.float32(np.log(np.float32(n / 16.0))) / np.float32(math.log(8.0)) * 16))
                bucket = min(large, 31)
            one[bucket, m] = 1.0
        else:
            one[32, m] = NEG
    j, i = np.arange(CH)[:, None], np.arange(CH)[None, :]
    masks = np.zeros((CH, 5, CH), np.float32)
    for n, L in enumerate(LEVELS):
        masks[:, n] = (j // (2 * L) == i // (2 * L)) & (j % (2 * L) < L) & (i % (2 * L) >= L)
    masks[:, 4] = (j // FINE == i // FINE) & (j <= i)
    j, i = np.arange(SAMP)[:, None], np.arange(SAMP)[None, :]
    same = (j // LS == i // LS)
    smask = (same & (j <= i)).astype(np.float32)
    bmask = (np.arange(SAMP)[:, None] // LS == np.arange(NB)[None, :]).astype(np.float32)
    scan = np.ones((2, T), np.float32)
    scan[0, 0:SEQ:CH] = 0
    scan[0, SEQ::LS] = 0
    scan[1, 0:SEQ:FINE] = 0
    scan[1, SEQ::LS] = 0
    bf = mybir.dt.np(bf16)
    b4 = np.where(np.tile(bmask, (4, 1)) > 0, 0.0, NEG).astype(np.float32)
    s4 = np.where(np.tile(same, (4, 1)), 0.0, NEG).astype(np.float32)
    return dict(onehot=one, masks=masks.astype(bf), smask=smask.astype(bf), bmask=bmask,
                scanm=np.ascontiguousarray(np.broadcast_to(scan, (P, 2, T))).astype(bf),
                ident_in=np.eye(P, dtype=np.float32), bmask4=b4, smask4=s4)


def _column_block(w, x):
    return w[:, x:x + P].reshape(KT, P, P).transpose(1, 0, 2).reshape(P, KT * P)


def _lay_out(i):
    w_in, w_up, w_down = i["w_in_a"][0], i["w_up"], i["w_down"]
    wall = np.zeros((W_END, P, KT * P), np.float32)
    wall[W_GLR].reshape(P, KT, P)[:, :, 0:RANK] = w_in[:, 3072:3088].reshape(KT, P, RANK).transpose(1, 0, 2)
    for h in range(H):
        b = W_M0 + HW * h
        for p, x in enumerate((h * P, 512 + h * P, 1024 + h * DV, 1024 + h * DV + P, 2048 + h * DV, 2048 + h * DV + P)):
            wall[b + p] = _column_block(w_in, x)
        for t in range(2):
            wall[b + 6 + t] = i["w_out_a"][0, h * DV + t * P:h * DV + (t + 1) * P]
    for l, w0 in enumerate((W_F0, W_F1)):
        for g in range(FG):
            b = w0 if g == 0 else w0 + 4 + 6 * (g - 1)
            for t in range(2):
                bt = b + 2 * t + (2 * t if g else 0)
                x = (2 * g + t) * P
                wall[bt] = _column_block(w_up[l], x)
                wall[bt + 1] = _column_block(w_up[l], FF + x)
                bd = w0 + 4 + 6 * g + 2 + t if g < FG - 1 else w0 + 4 + 6 * (FG - 1) + t
                wall[bd] = w_down[l, x:x + P]
    for x in range(2):
        wall[W_KV + x] = _column_block(i["w_kv"], x * P)
    for n in range(NKV):
        for j in range(2):
            for t in range(2):
                x = (4 * n + 2 * j + t) * P
                wall[W_M1 + HW * n + 2 * j + t] = _column_block(i["w_q_b"][0], x)
                wall[W_M1 + HW * n + 4 + 2 * j + t] = i["w_o_b"][0, x:x + P]
    x = np.concatenate([i["x_prompt"][0], i["x_sample"].reshape(SAMP, D)], 0)
    xT = x.reshape(NC, CW, KT, P).transpose(0, 3, 2, 1)
    rows = [i[n].reshape(-1, P) for n in ("g_mix_pre", "g_mix_post", "g_ffn_pre", "g_ffn_post", "g_kv", "g_gla_out")]
    par = np.zeros((2, P, FT, 20), np.float32)
    par[:, :, :, 0:16] = i["cache_conv"].reshape(2, 16, FT, P).transpose(0, 3, 2, 1)
    par[:, :, :, 16:19] = i["conv_w"].reshape(2, 3, FT, P).transpose(0, 3, 2, 1)
    par[:, :, :, 19] = i["conv_b"].reshape(2, FT, P).transpose(0, 2, 1)
    wg = np.concatenate([i["w_gate_up"][0], i["b_gate"][0][None]], 0).reshape(RANK + 1, H, P).transpose(1, 0, 2)
    s = i["sinks"][0]
    sinks = np.stack([np.broadcast_to(s, (P, NQ)), np.zeros((P, NQ), np.float32)])
    sinks[1, :, 0:4] = np.repeat(s.reshape(4, 2, 2).transpose(0, 2, 1).reshape(4, 4), 32, axis=1).T
    out = dict(wall=wall, xT=xT, gains=np.concatenate(rows, 0).T, ffnpar=par, wgate=wg,
               state=i["state_gla"][0].transpose(1, 2, 0, 3),
               kcT=i["cache_k_win"].transpose(2, 3, 0, 1).reshape(P, NB, WIN),
               vc=i["cache_v_win"].transpose(1, 0, 2, 3).reshape(WIN, NB, P),
               ck=i["cache_k_win"].reshape(NB, WIN, P), cv=i["cache_v_win"].reshape(NB, WIN, P),
               table=i["rel_bias"], sinks=sinks, **_constants())
    return {k: np.ascontiguousarray(v) for k, v in out.items()}


_OUTS = dict(yT=(NC, P, KT, CW), gla_p=(H, DK, DV), gla_s=(H, DK, NB, DV), conv_new=(2, P, FT, 18),
             kwin_p=(WIN, P), kwin_s=(NB, WIN, P), vwin_p=(WIN, P), vwin_s=(NB, WIN, P))


def kernel(**inputs):
    import concourse.bacc as bacc
    from concourse.bass_utils import run_bass_kernel_spmd

    arrays = _lay_out({k: np.asarray(v) for k, v in inputs.items()})
    nc = bacc.Bacc("TRN2", target_bir_lowering=False, num_devices=1)
    aps = {n: nc.dram_tensor(n, a.shape, mybir.dt.from_np(a.dtype), kind="ExternalInput").ap() for n, a in arrays.items()}
    for n, shape in _OUTS.items():
        aps[n] = nc.dram_tensor(n, shape, fp32, kind="ExternalOutput").ap()
    build(nc, **aps)
    r = run_bass_kernel_spmd(nc, [arrays], core_ids=[0]).results[0]
    y = np.asarray(r["yT"]).transpose(0, 3, 2, 1).reshape(T, D)
    conv = np.asarray(r["conv_new"]).transpose(0, 3, 2, 1).reshape(2, 18, FF)
    window = (NKV, HD)
    c = np.ascontiguousarray
    return (c(y[0:SEQ].reshape(1, SEQ, D)), c(y[SEQ:].reshape(NB, LS, D)),
            c(np.asarray(r["gla_p"]).reshape(1, 1, H, DK, DV)), c(np.asarray(r["gla_s"]).transpose(2, 0, 1, 3).reshape(1, NB, H, DK, DV)),
            c(conv[:, 0:2].reshape(2, 1, 2, FF)), c(conv[:, 2:18].reshape(2, NB, 2, FF)),
            c(np.asarray(r["kwin_p"]).reshape(1, WIN, *window)), c(np.asarray(r["kwin_s"]).reshape(NB, WIN, *window)),
            c(np.asarray(r["vwin_p"]).reshape(1, WIN, *window)), c(np.asarray(r["vwin_s"]).reshape(NB, WIN, *window)))
```

```python
import math
from contextlib import ExitStack

import numpy as np

import concourse.bass as bass
from concourse import mybir

fp32 = mybir.dt.float32
fp32r = mybir.dt.float32r
bf16 = mybir.dt.bfloat16
ALU = mybir.AluOpType
ACT = mybir.ActivationFunctionType
AX = mybir.AxisListType

P = 128
D = 1024
KT = D // P
SEQ, NB, LS = 1024, 8, 4
SAMP = NB * LS
T = SEQ + SAMP
NC, CW = 3, T // 3
H, DK, DV = 4, 128, 256
RANK = 16
CH = 128
NCHUNK = SEQ // CH
TAU = 16.0
LEVELS = (64, 32, 16, 8)
FINE = 8
GATE_FLOOR = -20.0 * TAU
HD, NQ, NKV = 64, 16, 2
WIN = 128
NBLK = SEQ // WIN
FF = 2816
FT = FF // P
FG = FT // 2
UP = 2 + SEQ
UW = UP + NB * (2 + LS)
CV = UW - 2
EPS = 1e-6
NEG = -1e30
RL = 383
HW = 9

G_MIX_PRE, G_MIX_POST, G_FFN_PRE, G_FFN_POST, G_KV, G_GLA = 0, 16, 32, 48, 64, 72
NGAIN = 74

W_GLR = 0
W_M0 = 1
W_F0 = W_M0 + H * HW - 1
W_KV = W_F0 + FT * 3
W_M1 = W_KV + 3
W_F1 = W_M1 + NKV * HW
W_END = W_F1 + FT * 3 + 1


def build(nc, wall, xT, gains, ffnpar, wgate, state, kcT, vc, ck, cv, onehot, masks, smask, bmask,
          scanm, ident_in, bmask4, smask4, table, sinks,
          yT, gla_p, gla_s, conv_new, kwin_p, kwin_s, vwin_p, vwin_s):
    h_dram = nc.dram_tensor("h_scratch", [NC, P, KT, CW], fp32, kind="Internal").ap()
    r_dram = nc.dram_tensor("bias_scratch", [NQ * P * RL], fp32, kind="Internal").ap()
    kt_dram = nc.dram_tensor("kt_scratch", [P, T], fp32, kind="Internal").ap()
    v_dram = nc.dram_tensor("v_scratch", [T, P], fp32, kind="Internal").ap()

    ctx = ExitStack()
    with ctx:
        base = nc.sbuf_base
        at = [((base if isinstance(base, int) else base()) + 31) // 32 * 32]
        top = {"at": 0}

        def place(name, shape, dt=fp32, offset=None):
            size = math.prod(shape[1:]) * (2 if dt == bf16 else 4)
            size = (size + 31) // 32 * 32
            off = at[0] if offset is None else offset
            if offset is None:
                at[0] += size
            top["at"] = max(top["at"], off + size)
            return nc.alloc_sbuf_tensor_at(name, shape, dt, offset=off)

        def sem(name):
            return ctx.enter_context(nc.semaphore(name))

        AH_AT = at[0]
        AH = place("act_hi", [P, KT, T], fp32r)
        AL = place("act_lo", [P, KT, T], fp32r)
        AC_AT = at[0]
        ACC = place("acc", [P, NC, KT, CW])
        WR = place("w_raw", [P, 3, KT * P])
        WH = place("w_hi", [P, 3, KT * P], fp32r)
        WL = place("w_lo", [P, 3, KT * P], fp32r)
        ident = place("ident", [P, P])
        ones = place("ones", [P, P])
        EPSC = place("eps_col", [P, 1])
        GC = place("gain_cols", [P, NGAIN])
        SINK = place("sinks_b", [P, NQ])
        arena = at[0]

        HC_AT = arena + 4 * T * 4
        at[0] = HC_AT
        HC = place("h_chunk", [P, NC, KT, CW])
        RS_AT = at[0]
        RS = place("rstd", [P, NC, CW])
        SQ_AT = at[0]
        SQ = [place("squares0", [P, KT, CW], offset=arena), place("squares1", [P, KT, CW])]
        BEHIND = at[0]
        

        at[0] = arena
        Qb = at[0]
        Q = place("gq", [P, T])
        K = place("gk", [P, T])
        Z = place("gb", [P, T])
        B8 = place("gb8", [P, T])
        OHE = place("go_hi_end", [P, 2, T], fp32r, offset=Qb)
        OLE = place("go_lo_end", [P, 2, T], fp32r, offset=Qb + 2 * T * 4)
        KD = place("gkd", [P, NCHUNK, P], offset=Qb + T * 4)
        KDS = place("gkd_s", [SAMP, P], offset=Qb)
        S = place("gstate", [P, DV], offset=Qb + 2 * T * 4)
        KDM = place("gkd_masked", [SAMP, NB, P], offset=Qb + 3 * T * 4)
        Tb = at[0]
        T1 = place("gt1", [P, T])
        KTl = place("gkt", [P, T])
        SB = place("gstates", [P, NB, DV], offset=Tb)
        QTb = at[0]
        QT = place("gqt", [P, T])
        AT = place("gat", [P, T])
        SQ0 = place("gsq", [P, 2, T], offset=QTb)
        OL0 = place("go_lo", [P, 2, T], fp32r, offset=QTb)
        Vb = at[0]
        OH0 = place("go_hi", [P, 2, T], fp32r, offset=Vb)
        V = place("gv", [P, 9, DV])
        RS0 = place("grs", [P, T], offset=Vb)
        R = place("gr", [P, 2, T])
        O = place("go", [P, 2, T])
        GLR = place("glr", [RANK + 1, T])
        WG = place("wgate", [RANK + 1, P])
        EL = place("gel", [P, 16])
        MLEV = place("mlev", [P, 5, CH], bf16)
        SMASK = place("smask_t", [SAMP, SAMP], bf16)
        BMASK = place("bmask_t", [SAMP, NB])
        SCM = place("scan_masks", [P, 2, T], bf16)
        

        at[0] = arena
        HH = place("h_hi", [P, 2, T], fp32r)
        HL = place("h_lo", [P, 2, T], fp32r)
        at[0] = RS_AT
        U = place("u", [P, UW])
        C = place("c", [P, UW])
        HF = place("hf", [P, T])
        PAR = place("par", [P, FT, 20])
        PC = place("par_tile", [P, 20])
        at[0] = BEHIND
        CN = place("conv_new_t", [P, FT, 18])

        at[0] = BEHIND
        KTT = place("kT", [P, T])
        VTT = place("vT", [P, T], offset=arena + KT * CW * 4)
        KVTOK = place("kv_tok", [P, 11, P], offset=SQ_AT)
        at[0] = AC_AT
        TBB = place("table_cols", [33, NQ, P])
        RB = place("bias_rows", [P, NQ, RL])
        at[0] = BEHIND
        OHR = place("onehot_t", [33, RL])
        TBL = place("table_t", [33, NQ])
        at[0] = arena
        Q1_AT = at[0]
        Q1 = place("q1", [P, 4, T])
        KG = place("kg", [P, T])
        KCG = place("kcg", [P, NB, WIN])
        VG = place("vg", [P, 9, HD])
        VCG = place("vcg", [P, NB, HD])
        QS = place("q_sample", [P, 4, SAMP])
        BI = place("bias", [P, 8, 2 * WIN])
        SS = place("scores", [P, 3, 2, 2 * WIN])
        PT_AT = at[0]
        PT = place("probs_t", [P, 2, 4, P])
        PX = place("s_probs_t", [P, NB, P], offset=PT_AT)
        OT = place("o_tok", [P, 2, P])
        OH1 = place("o_hi", [P, 2, T], fp32r)
        OL1_AT = at[0]
        OL1 = place("o_lo", [P, 2, T], fp32r)
        OW1 = place("o_whole", [P, 2, T], offset=OL1_AT)
        OH2 = place("o_hi2", [P, 2, T], fp32r, offset=Q1_AT)
        OL2 = place("o_lo2", [P, 2, T], fp32r, offset=Q1_AT + 2 * T * 4)
        OW2 = place("o_whole2", [P, 2, T], offset=Q1_AT + 2 * T * 4)
        ST = place("stats", [P, 8, 16])
        SST = place("s_stats", [P, 8])
        SX = place("s_scores", [P, T])
        PXN = place("s_probs_new_t", [SAMP, P])
        SBC = place("s_bias", [P, 2, WIN + LS])
        BM4 = place("s_mask", [P, NB])
        SM4 = place("s_mask_new", [P, SAMP])
        SKS = place("s_sinks", [P, NKV * 2])
        SKG = place("sinks_group", [P, 10])
        SKN = place("sinks_negated", [P, 8])

        PS = ctx.enter_context(nc.psum_tensor("banks", [P, 8, 512], fp32))

        c_in = sem("constants_in")
        one = sem("ones_set")
        w_in = [sem(f"w_in{i}") for i in range(3)]
        w_hi, w_lo = sem("w_hi_done"), sem("w_lo_done")
        tb_one, tb_in, tb_cols = sem("table_ones"), sem("table_in"), sem("table_cols_done")
        rb_full, rb_row, rb_out = sem("bias_row_full"), sem("bias_row_copied"), sem("bias_rows_out")
        h_in = [sem(f"h_in{c}") for c in range(NC)]
        h_out = [sem(f"h_out{c}") for c in range(NC)]
        sq_done, ss_done, ms_done = sem("squares_done"), sem("square_sums_done"), sem("mean_squares_done")
        rs_done, po_done, ha_done = sem("rstd_done"), sem("post_norm_done"), sem("residual_done")
        nm_done, ah_done, al_done = sem("pre_norm_done"), sem("act_hi_done"), sem("act_lo_done")
        az_done, lo_half = sem("acc_zeroed"), sem("act_lo_half")
        dn_full, dn_add = sem("down_full"), sem("down_added")
        glr_full, glr_ev = sem("glr_full"), sem("glr_copied")
        m0c_in, wg_in = sem("m0_constants_in"), sem("wgate_in")
        m0_full, m0_ev = sem("gla_proj_full"), sem("gla_proj_copied")
        az, ln = sem("gate_abs"), sem("gate_log")
        gt = sem("gate_made")
        cs = sem("gate_summed")
        lv_d, lv_e, lv_qk, lv_pe, lv_m, lv_a = (sem(f"level_{x}") for x in ("diff", "exp", "qk", "scores", "masked", "added"))
        in_d, in_e, in_qk = sem("inter_diff"), sem("inter_exp"), sem("inter_qk")
        vt_full, vt_ev, kd_full, kd_ev, kdm = (sem(x) for x in ("v_tok_full", "v_tok_copied", "k_tok_full", "k_tok_copied", "k_masked"))
        st_in, st_out, gp_out = sem("states_in"), sem("states_out"), sem("gla_p_out")
        o_full, o_ev, s_full, s_upd = (sem(x) for x in ("o_full", "o_copied", "state_full", "state_updated"))
        os_full, os_ev, ss_full, ss_upd = (sem(x) for x in ("os_full", "os_copied", "sstate_full", "sstate_updated"))
        gq_sq, gq_ss, gq_ms, gq_rs, gq_si, gq_o, gq_h, gq_l = (sem("gn_" + x) for x in ("sq", "ss", "ms", "rs", "silu", "o", "hi", "lo"))
        fp_in, u0_set = sem("ffn_par_in"), sem("u_zeroed")
        pc, pre = sem("par_copied"), sem("prefix_copied")
        u_full, u_ev, v_full, h_made = sem("u_full"), sem("u_copied"), sem("val_full"), sem("h_made")
        cb, cv1, cv2, cn, gl, hh, hl = (sem("ffn_" + x) for x in ("bias", "conv1", "conv2", "cache", "gelu", "hi", "lo"))
        cn_out = sem("conv_new_out")
        kv_full, kv_ev, kt_full, kt_ev = sem("kv_full"), sem("kv_copied"), sem("kvt_full"), sem("kvt_copied")
        kw_out, kv_out = sem("windows_out"), sem("kv_out")
        kg_in, bi_in, a_c_in = sem("kv_head_in"), sem("bias_in"), sem("attn_constants_in")
        skg = sem("sinks_copied")
        q_full, q_ev = sem("q_full"), sem("q_copied")
        xt = sem("att_tile_hi")
        sf, sa, mx, mm_, nm, ex, es, den, rc = (sem("att_" + x) for x in ("scores", "biased", "max", "maxsink", "negmax", "exp", "expsink", "den", "rden"))
        tf, te, of, on, xf, xh, xl = (sem("att_" + x) for x in ("pt", "pt_copied", "o", "o_scaled", "ot", "hi", "lo"))
        xsf, xsa, xsb, xmx, xex, xrc, xsc, xtf, xte, xof, xoh, xol = (sem("samp_" + x) for x in ("scores", "biased", "masked", "max", "exp", "rden", "scaled", "pt", "pt_copied", "o", "hi", "lo"))

        def chunk(c):
            return slice(c * CW, (c + 1) * CW)

        def col(x):
            return GC[:, x:x + 1]

        def bc(ap, n):
            shape = list(ap.shape)
            return ap.unsqueeze(len(shape)).broadcast_to(shape + [n])

        steps = []
        n_stat = n_all = n_act = n_post = 0
        for B in range(5):
            here = {}
            for kind in {0: ["pre"], 1: ["post", "pre"], 2: ["post", "kv", "mix"], 3: ["post", "pre"], 4: ["post"]}[B]:
                for c in range(NC):
                    here[kind, c] = dict(B=B, kind=kind, c=c, at=len(here), buf=(len(here) + 1) % 2, stat=n_stat, k=n_all, act=n_act, post=n_post)
                    n_all += 1
                    n_stat += kind != "mix"
                    n_act += kind != "post"
                    n_post += kind == "post"
            steps.append(here)
        flat = [s for b in steps for s in b.values()]
        ACTS = [sum(s["kind"] != "post" for s in flat if s["B"] <= B) for B in range(5)]
        POSTS = [sum(s["kind"] == "post" for s in flat if s["B"] <= B) for B in range(5)]
        DOWNS = [0, H, H + FG, H + FG + 2 * NKV, H + 2 * FG + 2 * NKV]
        POST_G = {1: G_MIX_POST, 2: G_FFN_POST, 3: G_MIX_POST + 8, 4: G_FFN_POST + 8}
        PRE_G = {(0, "pre"): G_MIX_PRE, (1, "pre"): G_FFN_PRE, (2, "kv"): G_KV, (2, "mix"): G_MIX_PRE + 8,
                 (3, "pre"): G_FFN_PRE + 8}
        for s in flat:
            s["bank"] = (4 if s["kind"] == "post" else 6) + s["stat"] % 2
        HALF = KT // 2
        HALVES = (slice(0, HALF), slice(HALF, KT))

        def free_squares(eng, s):
            if s["at"] >= 2:
                p = flat[s["k"] - 2]
                if p["kind"] == "post":
                    eng.wait_ge(ss_done, p["stat"] + 1)
                else:
                    eng.wait_ge(al_done, p["act"] + 1)
            elif s["at"] == 1 and s["B"]:
                eng.wait_ge(dn_full, 24 * DOWNS[s["B"]])

        def act_square(act, B, kind, c):
            s = steps[B][kind, c]
            for n, half in enumerate(HALVES):
                if kind == "post":
                    act.wait_ge(dn_add, 24 * DOWNS[B] - 24 + 8 * c + HALF * (n + 1))
                    src = ACC
                elif B == 0:
                    act.wait_ge(h_in[c], 16)
                    src = HC
                else:
                    act.wait_ge(ha_done, 2 * (POSTS[B - 1] + c) + n + 1)
                    src = HC
                if n == 0:
                    free_squares(act, s)
                nc.scalar.activation(SQ[s["buf"]][:, half], src[:, c, half], ACT.Square).then_inc(sq_done, 1)

        def act_rstd(act, B, kind, c):
            s = steps[B][kind, c]
            act.wait_ge(ss_done, s["stat"] + 1)
            nc.scalar.activation(RS[:, c], PS[:, s["bank"], 0:CW], ACT.Ln, bias=EPSC[:], scale=1.0 / D).then_inc(ms_done, 1)
            act.wait_ge(ms_done, s["stat"] + 1)
            nc.scalar.activation(RS[:, c], RS[:, c], ACT.Exp, scale=-0.5).then_inc(rs_done, 1)

        def act_boundary(act, B):
            def square(kind, c):
                act_square(act, B, kind, c)

            def rstd(kind, c):
                act_rstd(act, B, kind, c)

            def hi(kind, c):
                s = steps[B][kind, c]
                if kind == "mix":
                    act.wait_ge(kv_full, 2 * c + 2)
                for n, half in enumerate(HALVES):
                    act.wait_ge(nm_done, 2 * s["act"] + n + 1)
                    nc.scalar.activation(AH[:, half, chunk(c)], SQ[s["buf"]][:, half], ACT.Copy).then_inc(ah_done, 1)

            if B:
                if B == 3:
                    square("post", 0)
                square("post", 1)
                if B == 3:
                    rstd("post", 0)
                square("post", 2)
                rstd("post", 1)
            if B == 4:
                rstd("post", 2)
                return
            pre = "kv" if B == 2 else "pre"
            square(pre, 0)
            if B:
                rstd("post", 2)
                rstd(pre, 0)
                square(pre, 1)
            else:
                rstd(pre, 0)
                square(pre, 1)
                w_round(act, 0, 0, 0)
            hi(pre, 0)
            rstd(pre, 1)
            if B == 0:
                hi(pre, 1)
                w_round(act, 1, 0, 1)
                w_round(act, 2, 0, 2)
                square(pre, 2)
            else:
                square(pre, 2)
                hi(pre, 1)
            rstd(pre, 2)
            hi(pre, 2)
            if B == 2:
                for c in range(NC):
                    if c == 2:
                        act.wait_ge(kv_full, 2 * NC)
                        for x in range(3):
                            w_round(act, W_KV + x + 3, (W_KV + x) // 3 + 1, (W_KV + x) % 3)
                    hi("mix", c)
                    act_kv_copies(act, c)

        def dve_boundary(dve, B):
            def post(c):
                s = steps[B]["post", c]
                dve.wait_ge(rs_done, s["stat"] + 1)
                for m, half in enumerate(HALVES):
                    for n in range(half.start, half.stop):
                        g = POST_G[B] + n
                        last = nc.vector.scalar_tensor_tensor(ACC[:, c, n], ACC[:, c, n], col(g), RS[:, c],
                                                              ALU.mult, ALU.mult)
                    last.then_inc(po_done, 1)
                    if m == 0 and B in (1, 3):
                        dve.wait_ge(h_in[c], 32 if B == 1 else 48)
                    dve.wait_ge(po_done, 2 * s["post"] + m + 1)
                    nc.vector.tensor_tensor(HC[:, c, half], HC[:, c, half], ACC[:, c, half], ALU.add).then_inc(ha_done, 1)

            def pre(kind, c):
                s = steps[B][kind, c]
                dve.wait_ge(rs_done, s["stat"] + 1 if kind != "mix" else steps[B]["kv", c]["stat"] + 1)
                if kind == "mix":
                    free_squares(dve, s)
                for half in HALVES:
                    for n in range(half.start, half.stop):
                        g = PRE_G[B, kind] + n
                        last = nc.vector.scalar_tensor_tensor(SQ[s["buf"]][:, n], HC[:, c, n], col(g), RS[:, c],
                                                              ALU.mult, ALU.mult)
                    last.then_inc(nm_done, 1)
                if shared(s):
                    dve.wait_ge(ah_done, 2 * s["act"] + 1)
                    lo_of(nc.vector, s, HALVES[0]).then_inc(lo_half, 1)

            kind = "kv" if B == 2 else "pre"
            if B:
                post(0)
                post(1)
            if B < 4:
                pre(kind, 0)
            if B:
                post(2)
            else:
                copy_rows(dve, 0, 6)
            if B < 4:
                pre(kind, 1)
                if B == 0:
                    copy_rows(dve, 6, NQ)
                pre(kind, 2)
            if B == 2:
                for c in range(NC):
                    pre("mix", c)

        def shared(s):
            return s["kind"] != "post" and (s["kind"] == "mix" or s["c"] == 2 or s["B"] == 0)

        shared_before = {id(s): sum(shared(x) for x in flat[:s["k"]]) for s in flat}

        def lo_of(engine, s, half):
            return engine.tensor_tensor(AL[:, half, chunk(s["c"])], SQ[s["buf"]][:, half],
                                        AH[:, half, chunk(s["c"])].bitcast(fp32), ALU.subtract)

        def pool_boundary(pool, B):
            for s in steps[B].values():
                if s["kind"] != "post":
                    if s["kind"] == "mix" and s["c"] == 2:
                        w_rests(pool, W_KV + 3, W_M1 + 3)
                    if shared(s):
                        pool.wait_ge(lo_half, shared_before[id(s)] + 1)
                    else:
                        pool.wait_ge(ah_done, 2 * s["act"] + 1)
                        lo_of(nc.gpsimd, s, HALVES[0])
                    pool.wait_ge(ah_done, 2 * s["act"] + 2)
                    lo_of(nc.gpsimd, s, HALVES[1]).then_inc(al_done, 1)
                    if B == 0:
                        w_rest(pool, s["c"], s["c"])

        def zero_acc(pool, B):
            if B:
                pool.wait_ge(ha_done, 2 * POSTS[B])
            else:
                pool.wait_ge(rb_out, 16)
            nc.gpsimd.memset(ACC[:], 0.0).then_inc(az_done, 1)

        def bias_rows(pe, first, end):
            for h in range(first, end):
                if h >= 6:
                    pe.wait_ge(rb_row, h - 5)
                nc.tensor.matmul(PS[:, h % 6, 0:RL], TBB[:, h], OHR[:], start=True, stop=True).then_inc(rb_full, 1)

        def copy_rows(dve, first, end):
            for h in range(first, end):
                dve.wait_ge(rb_full, h + 1)
                nc.vector.tensor_copy(RB[:, h], PS[:, h % 6, 0:RL]).then_inc(rb_row, 1)

        def pe_sums(pe, s):
            st = s["stat"]
            if st >= 2:
                pe.wait_ge(ms_done, st - 1)
            for m, half in enumerate(HALVES):
                pe.wait_ge(sq_done, 2 * st + m + 1)
                for n in range(half.start, half.stop):
                    last = nc.tensor.matmul(PS[:, s["bank"], 0:CW], ones[:], SQ[s["buf"]][:, n],
                                            start=(n == 0), stop=(n == KT - 1))
            last.then_inc(ss_done, 1)

        def last_down(pe, B, *operands, **kw):
            down(pe, *operands, units=range(0, 20), **kw)
            pe_sums(pe, steps[B]["post", 0])
            down(pe, *operands, units=range(20, 24), **kw)

        def pe_boundary(pe, B):
            if B:
                pe.wait_ge(dn_add, 24 * DOWNS[B])
            order = [s for s in steps[B].values() if s["kind"] != "mix"]
            for s in order[0 if B in (0, 3) else 1:5]:
                if B == 0 and s["c"]:
                    bias_rows(pe, *((0, 6), (6, NQ))[s["c"] - 1])
                pe_sums(pe, s)
            if B == 2:
                pe_kv(pe, 0, steps[B]["kv", 0]["act"])
            for s in order[5:]:
                pe_sums(pe, s)
            if B == 2:
                pe_kv(pe, 1, steps[B]["kv", 1]["act"])
                pe_kv(pe, 2, steps[B]["kv", 2]["act"])

        def sp_boundary(sp, B):
            if B == 1:
                sp.wait_ge(st_out, 16 * H)
                sp.wait_ge(gp_out, 16 * H)
            if B in (1, 3):
                sp.wait_ge(dn_full, 24 * DOWNS[B] - 23)
            if B in (0, 1, 3):
                for c in range(NC):
                    if B == 3:
                        sp.wait_ge(h_out[c], 16)
                    sp.dma_start(HC[:, c], h_dram[c] if B == 3 else xT[c]).then_inc(h_in[c], 16)
                    if B == 0 and c == 0:
                        sp.dma_start(WR[:, 0], wall[0]).then_inc(w_in[0], 16)
            if B in (2, 4):
                for c in range(NC):
                    sp.wait_ge(ha_done, 2 * (POSTS[B - 1] + c) + 2)
                    sp.dma_start((h_dram if B == 2 else yT)[c], HC[:, c]).then_inc(h_out[c], 16)

        def w_load(sp, b, slot):
            sp.wait_ge(w_lo, b - 2)
            sp.dma_start(WR[:, slot], wall[bass.ds(b, 1)].rearrange("a p n -> p (a n)")).then_inc(w_in[slot], 16)

        def w_round(act, b, third, slot):
            act.wait_ge(w_in[slot], 16 * third + 16)
            nc.scalar.activation(WH[:, slot], WR[:, slot], ACT.Copy).then_inc(w_hi, 1)

        def w_rest(pool, b, slot):
            pool.wait_ge(w_hi, b + 1)
            nc.gpsimd.tensor_tensor(WL[:, slot], WR[:, slot], WH[:, slot].bitcast(fp32),
                                    ALU.subtract).then_inc(w_lo, 1)

        def w_rests(pool, first, end):
            b = first
            while b < end and b % 3:
                w_rest(pool, b, b % 3)
                b += 1
            whole = (end - b) // 3
            if whole > 0:
                with pool.Fori(0, whole) as i:
                    for s in range(3):
                        w_rest(pool, 3 * i + b + s, s)
            for x in range(b + 3 * max(whole, 0), end):
                w_rest(pool, x, x % 3)

        def w_loads(sp, first, end):
            b = first
            while b < end and b % 3:
                w_load(sp, b, b % 3)
                b += 1
            whole = (end - b) // 3
            if whole > 0:
                with sp.Fori(0, whole) as i:
                    for s in range(3):
                        w_load(sp, 3 * i + b + s, s)
            for x in range(b + 3 * max(whole, 0), end):
                w_load(sp, x, x % 3)

        def project(pe, bank, slot, c, full, hi=None, lo=None):
            for k in range(KT):
                wh, wl = WH[:, slot, k * P:(k + 1) * P], WL[:, slot, k * P:(k + 1) * P]
                for w, a, first in ((wl, AH, True), (wh, AL, False), (wh, AH, False)):
                    last = nc.tensor.matmul(PS[:, bank, 0:CW], w, a[:, k, chunk(c)],
                                            start=(k == 0 and first), stop=(k == KT - 1 and w is wh and a is AH))
            last.then_inc(full, 1)

        def down(pe, slots, hi, lo, n_before, idle=False, units=range(NC * KT)):
            for m in units:
                c, n = divmod(m, KT)
                if m >= 2 or not idle:
                    pe.wait_ge(dn_add, n_before + max(m - 1, 0))
                for t in range(2):
                    wh = WH[:, slots[t], n * P:(n + 1) * P]
                    wl = WL[:, slots[t], n * P:(n + 1) * P]
                    for x, (w, a) in enumerate(((wl, hi), (wh, lo), (wh, hi))):
                        last = nc.tensor.matmul(PS[:, 6 + m % 2, 0:CW], w, a[:, t, chunk(c)],
                                                start=(t == 0 and x == 0), stop=(t == 1 and x == 2))
                last.then_inc(dn_full, 1)

        def down_add(dve, n_before, units=range(NC * KT)):
            for m in units:
                dve.wait_ge(dn_full, n_before + m + 1)
                a = ACC[:, m // KT, m % KT]
                nc.vector.tensor_tensor(a, a, PS[:, 6 + m % 2, 0:CW], ALU.add).then_inc(dn_add, 1)

        GB = W_M0 + 2
        NEXT_HEAD = True

        def turns(eng, turn):
            with eng.Fori(0, H - 1) as h:
                turn(h, NEXT_HEAD)
            turn(H - 1, not NEXT_HEAD)

        def turn_blocks(more):
            return dict(v=(0, 1), r=(2, 3), q=4, k=6, down=(7, 8)) if more else dict(v=(0, 1), r=(2, 3), down=(4, 5))

        def pe_gla(pe):
            pe.wait_ge(w_lo, W_GLR + 1)
            pe.wait_ge(rb_row, NQ)
            for c in range(NC):
                pe.wait_ge(al_done, c + 1)
                project(pe, c, W_GLR % 3, c, glr_full)
            pe.wait_ge(m0c_in, 16 * 4)
            pe.wait_ge(glr_ev, NC + 1)

            def gates(g):
                pe.wait_ge(wg_in, 16 * g + 16)
                for c in range(NC):
                    nc.tensor.matmul(PS[:, 3 + c, 0:CW], WG[:], GLR[:, chunk(c)], start=True, stop=True).then_inc(m0_full, 1)

            gates(0)
            for p in range(2):
                pe.wait_ge(w_lo, W_M0 + p + 1)
                for c in range(NC):
                    if p:
                        pe.wait_ge(m0_ev, c + 1)
                    project(pe, 3 * p + c, (W_M0 + p) % 3, c, m0_full)

            def turn(h, more):
                b0 = HW * h + GB
                blk = turn_blocks(more)

                def slot(p):
                    return (GB + p) % 3

                def level(n):
                    pe.wait_ge(lv_qk, 5 * h + n + 1)
                    if n:
                        pe.wait_ge(lv_m, 5 * h + n)
                    for c in range(NCHUNK):
                        x = slice(c * CH, (c + 1) * CH)
                        last = nc.tensor.matmul(PS[:, 6 + c // 4, (c % 4) * CH:(c % 4 + 1) * CH], KTl[:, x], QT[:, x],
                                                start=True, stop=True)
                    if n == 4:
                        pe.wait_ge(vt_ev, h + 1)
                        x = slice(SEQ, T)
                        last = nc.tensor.matmul(PS[0:SAMP, 4, DV:DV + SAMP], KTl[:, x], QT[:, x], start=True, stop=True)
                    last.then_inc(lv_pe, 1)

                def values(t):
                    pe.wait_ge(w_lo, b0 + t + 1)
                    for c in range(NC):
                        pe.wait_ge(m0_ev, 21 * h + 3 + 3 * t + c + 1)
                        project(pe, 3 * t + c, slot(t), c, m0_full)

                def outgate(u):
                    if u % 3 == 0:
                        pe.wait_ge(w_lo, b0 + 2 + u // 3 + 1)
                    pe.wait_ge(m0_ev, 21 * h + 15 + u)
                    project(pe, 5, slot(2 + u // 3), u % 3, m0_full)

                def by_token():
                    pe.wait_ge(m0_ev, 21 * h + 15)
                    for i in range(9):
                        n = CH if i < 8 else SAMP
                        for d in range(2):
                            last = nc.tensor.transpose(PS[0:n, i // 2, (i % 2) * DV + d * P:(i % 2) * DV + (d + 1) * P],
                                                       O[:, d, i * CH:i * CH + n], ident[:])
                    last.then_inc(vt_full, 1)

                def state_step(c):
                    x = slice(c * CH, (c + 1) * CH)
                    if c >= 2:
                        pe.wait_ge(s_upd, 8 * h + c - 1)
                    nc.tensor.matmul(PS[:, 2 + c % 2, 0:DV], KD[:, c], V[:, c], start=True, stop=True).then_inc(s_full, 1)
                    if c >= 2:
                        pe.wait_ge(o_ev, 8 * h + c - 1)
                    for d in range(2):
                        out = PS[:, c % 2, d * CH:(d + 1) * CH]
                        last = nc.tensor.matmul(out, V[:, c, d * P:(d + 1) * P], AT[:, x], start=True, stop=(c == 0))
                        if c:
                            if d == 0:
                                pe.wait_ge(s_upd, 8 * h + c)
                            last = nc.tensor.matmul(out, S[:, d * P:(d + 1) * P], QT[:, x], start=False, stop=True)
                    last.then_inc(o_full, 1)

                def norm_sums(c):
                    if c == 2:
                        pe.wait_ge(gq_ms, 3 * h + 1)
                    for d in range(2):
                        last = nc.tensor.matmul(PS[:, 6 + c % 2, 0:CW], ones[:], SQ0[:, d, chunk(c)], start=(d == 0), stop=(d == 1))
                    last.then_inc(gq_ss, 1)

                values(0)
                level(0)
                values(1)
                level(1)
                by_token()
                outgate(0)
                level(2)
                outgate(1)
                level(3)
                outgate(2)
                level(4)
                outgate(3)
                pe.wait_ge(in_qk, 2 * h + 1)
                pe.wait_ge(lv_a, 4 * h + 4)
                for c in range(NCHUNK):
                    nc.tensor.transpose(PS[:, 6 + c // 4, (c % 4) * CH:(c % 4 + 1) * CH], KTl[:, c * CH:(c + 1) * CH], ident[:])
                nc.tensor.transpose(PS[0:SAMP, 4, 3 * P:4 * P], KTl[:, SEQ:T], ident[:]).then_inc(kd_full, 1)
                outgate(4)
                pe.wait_ge(in_qk, 2 * h + 2)
                pe.wait_ge(vt_ev, h + 1)
                pe.wait_ge(kd_ev, h + 1)
                for c in range(NCHUNK):
                    state_step(c)
                    if c == 3:
                        outgate(5)
                pe.wait_ge(st_in, 16 * h + 16)
                pe.wait_ge(m0_ev, 21 * h + 21)
                pe.wait_ge(kdm, h + 1)
                for d in range(2):
                    nc.tensor.matmul(PS[:, 4 + d, 0:SAMP], V[0:SAMP, 8, d * P:(d + 1) * P],
                                     AT[0:SAMP, SEQ:T], start=True, stop=False, skip_group_check=True)
                for b in range(NB):
                    x = b * LS
                    for d in range(2):
                        last = nc.tensor.matmul(PS[:, 4 + d, x:x + LS], SB[:, b, d * P:(d + 1) * P],
                                                QT[:, SEQ + x:SEQ + x + LS], start=False, stop=(b == NB - 1),
                                                skip_group_check=True)
                    if b == NB - 1:
                        last.then_inc(os_full, 1)
                    if b >= 2:
                        pe.wait_ge(ss_upd, 8 * h + b - 1)
                    nc.tensor.matmul(PS[:, 6 + b % 2, 0:DV], KDM[:, b], V[0:SAMP, 8, :],
                                     start=True, stop=True).then_inc(ss_full, 1)
                pe.wait_ge(s_upd, 8 * h + 8)
                pe.wait_ge(os_ev, h + 1)
                pe.wait_ge(o_ev, 8 * h + 8)
                if more:
                    gates(h + 1)
                    pe.wait_ge(w_lo, b0 + blk["q"] + 1)
                    project(pe, 0, slot(blk["q"]), 0, m0_full)
                pe.wait_ge(gq_sq, h + 1)
                pe.wait_ge(ss_upd, 8 * h + 8)
                norm_sums(0)
                norm_sums(1)
                if more:
                    project(pe, 1, slot(blk["q"]), 1, m0_full)
                norm_sums(2)
                if more:
                    project(pe, 2, slot(blk["q"]), 2, m0_full)
                    pe.wait_ge(w_lo, b0 + blk["k"] + 1)
                    for c in range(NC):
                        pe.wait_ge(m0_ev, 21 * h + 21 + c + 1)
                        project(pe, 3 + c, slot(blk["k"]), c, m0_full)
                pe.wait_ge(w_lo, b0 + blk["down"][1] + 1)
                pe.wait_ge(gq_l, h + 1)
                slots = [slot(p) for p in blk["down"]]
                if more:
                    down(pe, slots, OH0, OL0, 24 * h, idle=True)
                else:
                    last_down(pe, 1, slots, OHE, OLE, 24 * h, idle=True)

            turns(pe, turn)

        def halves(buf, L):
            v = buf[:, 0:SEQ].rearrange("p (n s) -> p n s", s=2 * L)
            return v[:, :, 0:L], v[:, :, L:2 * L], v[:, :, L - 1:L]

        def dve_gla(dve):
            dve.wait_ge(al_done, ACTS[0])
            nc.vector.memset(GLR[:], 1.0).then_inc(glr_ev, 1)
            dve.wait_ge(m0c_in, 16 * 4)

            def minus_abs(g):
                dve.wait_ge(m0_ev, 21 * g + 3)
                nc.vector.scalar_tensor_tensor(T1[:], Z[:], -1.0, Z[:], ALU.mult, ALU.min).then_inc(az, 1)

            def log_sigmoid(g):
                dve.wait_ge(ln, 2 * g + 2)
                nc.vector.scalar_tensor_tensor(Z[:], Z[:], 0.0, T1[:], ALU.min, ALU.subtract).then_inc(gt, 1)
                dve.wait_ge(gt, 2 * g + 1)
                nc.vector.tensor_scalar(B8[:], Z[:], GATE_FLOOR, None, ALU.max).then_inc(gt, 1)

            def running_sum(g, x):
                dve.wait_ge(gt, 2 * g + 2)
                buf = (Z, B8)[x]
                nc.vector.tensor_tensor_scan(buf[:], SCM[:, x], buf[:], 0.0, ALU.mult, ALU.add).then_inc(cs, 1)

            minus_abs(0)
            log_sigmoid(0)
            running_sum(0, 0)
            running_sum(0, 1)

            def turn(h, more):
                dve.wait_ge(cs, 2 * h + 2)

                def distance(n):
                    if n < 4:
                        L = LEVELS[n]
                        left, right, ref = halves(Z, L)
                        tl, tr, _ = halves(T1, L)
                        shape = list(left.shape)
                        nc.vector.tensor_tensor(tl, ref.broadcast_to(shape), left, ALU.subtract)
                        nc.vector.tensor_tensor(tr, right, ref.broadcast_to(shape), ALU.subtract).then_inc(lv_d, 1)
                        return
                    f = B8[:, 0:SEQ].rearrange("p (n s) -> p n s", s=FINE)
                    o = T1[:, 0:SEQ].rearrange("p (n s) -> p n s", s=FINE)
                    nc.vector.tensor_tensor(o, f, f[:, :, FINE // 2 - 1:FINE // 2].broadcast_to(list(f.shape)), ALU.subtract)
                    f = B8[:, SEQ:T].rearrange("p (n s) -> p n s", s=LS)
                    o = T1[:, SEQ:T].rearrange("p (n s) -> p n s", s=LS)
                    nc.vector.tensor_tensor(o, f, f[:, :, 1:2].broadcast_to(list(f.shape)), ALU.subtract).then_inc(lv_d, 1)

                def decayed(n):
                    dve.wait_ge(lv_e, 5 * h + n + 1)
                    if n < 4:
                        x = slice(0, SEQ)
                        nc.vector.tensor_tensor(QT[:, x], Q[:, x], T1[:, x], ALU.mult)
                        nc.vector.tensor_tensor(KTl[:, x], K[:, x], T1[:, x], ALU.mult).then_inc(lv_qk, 1)
                    else:
                        nc.vector.tensor_tensor(QT[:], Q[:], QT[:], ALU.mult)
                        nc.vector.tensor_tensor(KTl[:], K[:], KTl[:], ALU.mult).then_inc(lv_qk, 1)
                    dve.wait_ge(lv_qk, 5 * h + n + 1)

                distance(0)
                dve.wait_ge(m0_ev, 21 * h + 9)
                decayed(0)
                distance(1)
                for n in range(4):
                    mask_scores(dve, h, n)
                    decayed(n + 1)
                    if n:
                        add_scores(dve, h, n)
                    if n < 3:
                        distance(n + 2)
                f = Z[:, 0:SEQ].rearrange("p (n s) -> p n s", s=CH)
                o = T1[:, 0:SEQ].rearrange("p (n s) -> p n s", s=CH)
                nc.vector.tensor_tensor(o, f[:, :, CH - 1:CH].broadcast_to(list(f.shape)), f, ALU.subtract)
                f = Z[:, SEQ:T].rearrange("p (n s) -> p n s", s=LS)
                o = T1[:, SEQ:T].rearrange("p (n s) -> p n s", s=LS)
                nc.vector.tensor_tensor(o, f[:, :, LS - 1:LS].broadcast_to(list(f.shape)), f, ALU.subtract).then_inc(in_d, 1)
                mask_scores(dve, h, 4)
                dve.wait_ge(in_e, h + 1)
                nc.vector.tensor_tensor(KTl[:], K[:], T1[:], ALU.mult).then_inc(in_qk, 1)
                nc.vector.tensor_tensor(QT[:], Q[:], QT[:], ALU.mult).then_inc(in_qk, 1)
                add_scores(dve, h, 4)
                dve.wait_ge(kd_ev, h + 1)
                nc.vector.tensor_tensor(KDM[:], KDS[:].unsqueeze(1).broadcast_to([SAMP, NB, P]), bc(BMASK[:], P),
                                        ALU.mult).then_inc(kdm, 1)
                for c in range(NCHUNK):
                    dve.wait_ge(s_full, 8 * h + c + 1)
                    if c == 0:
                        nc.vector.tensor_copy(S[:], PS[:, 2, 0:DV]).then_inc(s_upd, 1)
                    else:
                        dve.wait_ge(o_full, 8 * h + c + 1)
                        dve.wait_ge(s_upd, 8 * h + c)
                        nc.vector.scalar_tensor_tensor(S[:], S[:], EL[:, c:c + 1], PS[:, 2 + c % 2, 0:DV],
                                                       ALU.mult, ALU.add).then_inc(s_upd, 1)
                for b in range(NB):
                    dve.wait_ge(ss_full, 8 * h + b + 1)
                    nc.vector.scalar_tensor_tensor(SB[:, b], SB[:, b], EL[:, 8 + b:9 + b], PS[:, 6 + b % 2, 0:DV],
                                                   ALU.mult, ALU.add).then_inc(ss_upd, 1)
                dve.wait_ge(gq_rs, h + 1)
                for d in range(2):
                    nc.vector.scalar_tensor_tensor(O[:, d], O[:, d], col(G_GLA + d), RS0[:], ALU.mult, ALU.mult).then_inc(gq_o, 1)
                dve.wait_ge(gq_o, 3 * h + 2)
                dve.wait_ge(gq_si, h + 1)
                nc.vector.tensor_tensor(O[:], O[:], R[:], ALU.mult).then_inc(gq_o, 1)
                dve.wait_ge(st_out, 16 * h + 16)
                if more:
                    minus_abs(h + 1)
                else:
                    dve.wait_ge(gp_out, 16 * h + 16)
                dve.wait_ge(gq_h, h + 1)
                oh, ol = (OH0, OL0) if more else (OHE, OLE)
                nc.vector.tensor_tensor(ol[:], O[:], oh[:].bitcast(fp32), ALU.subtract).then_inc(gq_l, 1)
                dve.wait_ge(az_done, 1)
                down_add(dve, 24 * h, units=range(0, 6))
                if more:
                    log_sigmoid(h + 1)
                down_add(dve, 24 * h, units=range(6, 11))
                if more:
                    running_sum(h + 1, 0)
                down_add(dve, 24 * h, units=range(11, 16))
                if more:
                    running_sum(h + 1, 1)
                down_add(dve, 24 * h, units=range(16, 24))

            turns(dve, turn)

        def masked(n):
            if n == 0:
                return AT[:, 0:SEQ]
            return V[:].rearrange("p a b -> p (a b)")[:, 0:SEQ] if n == 1 else O[:, 0, 0:SEQ]

        def mask_scores(dve, h, n):
            dve.wait_ge(lv_pe, 5 * h + n + 1)
            if n == 2:
                dve.wait_ge(vt_full, h + 1)
            if n > 2:
                dve.wait_ge(lv_a, 4 * h + n - 1)
            if n == 4:
                nc.vector.tensor_tensor(AT[0:SAMP, SEQ:T], PS[0:SAMP, 4, DV:DV + SAMP], SMASK[:], ALU.mult)
            nc.vector.tensor_tensor(masked(n).rearrange("p (c i) -> p c i", i=CH),
                                    PS[:, 6:8].rearrange("p b (c i) -> p (b c) i", i=CH),
                                    MLEV[:, n:n + 1].broadcast_to([P, NCHUNK, CH]), ALU.mult).then_inc(lv_m, 1)

        def add_scores(dve, h, n):
            dve.wait_ge(lv_m, 5 * h + n + 1)
            nc.vector.tensor_tensor(AT[:, 0:SEQ], AT[:, 0:SEQ], masked(n), ALU.add).then_inc(lv_a, 1)

        def act_gla(act):
            act.wait_ge(al_done, ACTS[0])
            for c in range(NC):
                act.wait_ge(glr_full, c + 1)
                act.wait_ge(glr_ev, 1)
                nc.scalar.activation(GLR[0:RANK, chunk(c)], PS[0:RANK, c, 0:CW], ACT.Copy).then_inc(glr_ev, 1)
            w_round(act, 3, 1, 0)

            def copy(g, dst, x, bank, **kw):
                act.wait_ge(m0_full, 21 * g + x + 1)
                nc.scalar.activation(dst[:, chunk(x % NC)], PS[:, bank, 0:CW], ACT.Copy, **kw).then_inc(m0_ev, 1)

            def gates(g):
                for c in range(NC):
                    copy(g, Z, c, 3 + c)

            def softplus(g):
                act.wait_ge(az, g + 1)
                nc.scalar.activation(T1[:], T1[:], ACT.Exp).then_inc(ln, 1)
                act.wait_ge(ln, 2 * g + 1)
                nc.scalar.activation(T1[:], T1[:], ACT.Ln, bias=1.0).then_inc(ln, 1)

            gates(0)
            softplus(0)
            for c in range(NC):
                copy(0, Q, 3 + c, c, scale=DK ** -0.5)
            w_round(act, 4, 1, 1)
            for c in range(NC):
                copy(0, K, 6 + c, 3 + c)
            w_round(act, 5, 1, 2)

            def turn(h, more):
                def round_next(p):
                    b = GB + p + 3
                    w_round(act, HW * h + b, 3 * h + b // 3, b % 3)

                def level(n):
                    act.wait_ge(lv_d, 5 * h + n + 1)
                    x = slice(0, SEQ)
                    if n < 4:
                        nc.scalar.activation(T1[:, x], T1[:, x], ACT.Exp, scale=1.0 / TAU).then_inc(lv_e, 1)
                    else:
                        act.wait_ge(lv_pe, 5 * h + 4)
                        nc.scalar.activation(QT[:], T1[:], ACT.Exp, scale=1.0 / TAU)
                        nc.scalar.activation(KTl[:], T1[:], ACT.Exp, scale=-1.0 / TAU).then_inc(lv_e, 1)

                def values(t):
                    for c in range(NC):
                        copy(h, O[:, t], 9 + 3 * t + c, 3 * t + c)
                    round_next(t)

                def outgate(u):
                    copy(h, R[:, u // 3], 15 + u, 5)
                    if u % 3 == 2:
                        round_next(2 + u // 3)

                level(0)
                values(0)
                level(1)
                values(1)
                level(2)
                act.wait_ge(vt_full, h + 1)
                act.wait_ge(lv_a, 4 * h + 1)
                for i in range(4):
                    nc.scalar.activation(V[:, 2 * i:2 * i + 2], PS[:, i].rearrange("p (a n) -> p a n", a=2), ACT.Copy)
                nc.scalar.activation(V[0:SAMP, 8], PS[0:SAMP, 4, 0:DV], ACT.Copy).then_inc(vt_ev, 1)
                outgate(0)
                level(3)
                outgate(1)
                level(4)
                outgate(2)
                act.wait_ge(in_d, h + 1)
                nc.scalar.activation(T1[:], T1[:], ACT.Exp, scale=1.0 / TAU)
                nc.scalar.activation(EL[:, 0:8], Z[:, CH - 1:SEQ:CH], ACT.Exp, scale=1.0 / TAU)
                nc.scalar.activation(EL[:, 8:16], Z[:, SEQ + LS - 1:T:LS], ACT.Exp, scale=1.0 / TAU)
                act.wait_ge(lv_pe, 5 * h + 5)
                nc.scalar.activation(QT[:], Z[:], ACT.Exp, scale=1.0 / TAU).then_inc(in_e, 1)
                outgate(3)
                act.wait_ge(kd_full, h + 1)
                act.wait_ge(in_qk, 2 * h + 2)
                nc.scalar.activation(KD[:].rearrange("p c n -> p (c n)").rearrange("p (b x) -> p b x", b=2), PS[:, 6:8], ACT.Copy)
                nc.scalar.activation(KDS[:], PS[0:SAMP, 4, 3 * P:4 * P], ACT.Copy).then_inc(kd_ev, 1)
                act.dma_start(SB[:], state[bass.ds(h, 1)].rearrange("a k b v -> k (a b) v")).then_inc(st_in, 16)
                outgate(4)
                for c in range(NCHUNK):
                    act.wait_ge(o_full, 8 * h + c + 1)
                    nc.scalar.activation(O[:, :, c * CH:(c + 1) * CH],
                                         PS[:, c % 2, 0:2 * CH].rearrange("p (d i) -> p d i", d=2), ACT.Copy).then_inc(o_ev, 1)
                    if c == 3:
                        outgate(5)
                act.wait_ge(os_full, h + 1)
                nc.scalar.activation(O[:, :, SEQ:T], PS[:, 4:6, 0:SAMP], ACT.Copy).then_inc(os_ev, 1)
                act.wait_ge(s_upd, 8 * h + 8)
                act.dma_start(gla_p[bass.ds(h, 1)].rearrange("a k v -> k (a v)"), S[:]).then_inc(gp_out, 16)
                act.wait_ge(o_ev, 8 * h + 8)
                act.wait_ge(os_ev, h + 1)
                nc.scalar.activation(SQ0[:], O[:], ACT.Square).then_inc(gq_sq, 1)
                act.wait_ge(ss_upd, 8 * h + 8)
                act.dma_start(gla_s[bass.ds(h, 1)].rearrange("a k b v -> k (a b) v"), SB[:]).then_inc(st_out, 16)
                if more:
                    act.wait_ge(gp_out, 16 * h + 16)
                    gates(h + 1)
                nc.scalar.activation(R[:], R[:], ACT.Silu).then_inc(gq_si, 1)
                if more:
                    copy(h + 1, Q, 3, 0, scale=DK ** -0.5)

                def norm_log(c):
                    act.wait_ge(gq_ss, 3 * h + c + 1)
                    nc.scalar.activation(RS0[:, chunk(c)], PS[:, 6 + c % 2, 0:CW], ACT.Ln,
                                         bias=EPSC[:], scale=1.0 / DV).then_inc(gq_ms, 1)

                norm_log(0)
                norm_log(1)
                norm_log(2)
                act.wait_ge(gq_ms, 3 * h + 3)
                nc.scalar.activation(RS0[:], RS0[:], ACT.Exp, scale=-0.5).then_inc(gq_rs, 1)
                if more:
                    copy(h + 1, Q, 4, 1, scale=DK ** -0.5)
                    copy(h + 1, Q, 5, 2, scale=DK ** -0.5)
                    round_next(4)
                    round_next(5)
                    copy(h + 1, K, 6, 3)
                act.wait_ge(gq_o, 3 * h + 3)
                nc.scalar.activation((OH0 if more else OHE)[:], O[:], ACT.Copy).then_inc(gq_h, 1)
                if more:
                    copy(h + 1, K, 7, 4)
                    softplus(h + 1)
                    copy(h + 1, K, 8, 5)
                    round_next(6)
                if not more:
                    act_square(act, 1, "post", 0)
                    act_rstd(act, 1, "post", 0)
                act.wait_ge(dn_full, 24 * h + 24)
                for p in turn_blocks(more)["down"]:
                    round_next(p)

            turns(act, turn)

        def sp_gla(sp):
            sp.wait_ge(al_done, ACTS[0])
            for dst, src in ((MLEV, masks), (SMASK, smask), (BMASK, bmask), (SCM, scanm)):
                sp.dma_start(dst[:], src).then_inc(m0c_in, 16)
            sp.dma_start(WG[:], wgate[0]).then_inc(wg_in, 16)
            w_loads(sp, 3, GB + 3)

            def turn(h, more):
                if more:
                    sp.wait_ge(m0_ev, 21 * h + 3)
                    sp.dma_start(WG[:], wgate[bass.ds(h + 1, 1)].rearrange("a r n -> r (a n)")).then_inc(wg_in, 16)
                for p in range(HW if more else 6):
                    w_load(sp, HW * h + GB + p + 3, (GB + p) % 3)

            turns(sp, turn)

        def pe_kv(pe, c, act):
            pe.wait_ge(al_done, act + 1)
            for x in range(2):
                if c == 0:
                    pe.wait_ge(w_lo, W_KV + x + 1)
                project(pe, 3 * x + c, (W_KV + x) % 3, c, kv_full)

        def act_kv_copies(act, c):
            if c == 0:
                act.wait_ge(cn_out, 16)
            for x, dst in ((0, KTT), (1, VTT)):
                act.wait_ge(kv_full, 2 * c + x + 1)
                nc.scalar.activation(dst[:, chunk(c)], PS[:, 3 * x + c, 0:CW], ACT.Copy).then_inc(kv_ev, 1)

        def act_kv(act):
            act.wait_ge(kt_full, 1)
            act.wait_ge(al_done, ACTS[2])
            for i in range(3):
                n = 4 if i < 2 else 3
                last = nc.scalar.activation(KVTOK[:, 4 * i:4 * i + n].rearrange("p a n -> p (a n)"), PS[:, i, 0:n * P], ACT.Copy)
            last.then_inc(kt_ev, 1)

        def pe_kv_tokens(pe):
            pe.wait_ge(kv_ev, 2 * NC)
            tiles = [(VTT, i) for i in range(9)] + [(KTT, 7), (KTT, 8)]
            for x, (src, i) in enumerate(tiles):
                n = CH if i < 8 else SAMP
                last = nc.tensor.transpose(PS[0:n, x // 4, (x % 4) * P:(x % 4 + 1) * P], src[:, i * CH:i * CH + n], ident[:])
            last.then_inc(kt_full, 1)

        def sp_kv(sp):
            sp.wait_ge(kv_ev, 2 * NC)
            sp.dma_start(kt_dram, KTT[:]).then_inc(kv_out, 16)
            sp.wait_ge(kt_ev, 1)
            sp.dma_start(v_dram[0:SEQ].rearrange("(t p) d -> p t d", p=P), KVTOK[:, 0:8]).then_inc(kv_out, 16)
            sp.dma_start(v_dram[SEQ:T], KVTOK[0:SAMP, 8]).then_inc(kv_out, 16)
            sp.dma_start(vwin_p, KVTOK[:, 7]).then_inc(kw_out, 16)
            sp.dma_start(kwin_p, KVTOK[:, 9]).then_inc(kw_out, 16)
            for dst, tile, old in ((vwin_s, 8, cv), (kwin_s, 10, ck)):
                for b in range(NB):
                    sp.dma_start(dst[b, WIN - LS:WIN], KVTOK[b * LS:(b + 1) * LS, tile]).then_inc(kw_out, 16)
                sp.dma_start(dst[:, 0:WIN - LS], old[:, LS:WIN]).then_inc(kw_out, 16)

        def first_of_all(T_):
            return isinstance(T_, int) and T_ == 0

        def pe_ffn(pe, l):
            w0, d0, acts = (W_F0, W_F1)[l], (DOWNS[1], DOWNS[3])[l], (ACTS[1], ACTS[3])[l]

            def tile(T_, b, s, first):
                pe.wait_ge(w_lo, b + 1)
                if first:
                    pe.wait_ge(w_lo, b + 2)
                    for c in range(NC):
                        pe.wait_ge(al_done, acts - NC + c + 1)
                        if not first_of_all(T_):
                            pe.wait_ge(u_ev, 3 * T_ + c - 2)
                            pe.wait_ge(h_made, 3 * T_ + c - 2)
                        project(pe, c, s % 3, c, u_full)
                        project(pe, 3 + c, (s + 1) % 3, c, v_full)
                    return
                for c in range(NC):
                    if not first_of_all(T_):
                        pe.wait_ge(u_ev, 3 * T_ + c - 2)
                    project(pe, c, s % 3, c, u_full)
                pe.wait_ge(w_lo, b + 2)
                for c in range(NC):
                    if not first_of_all(T_):
                        pe.wait_ge(h_made, 3 * T_ + c - 2)
                    project(pe, 3 + c, (s + 1) % 3, c, v_full)

            def downs(D_, T_, b, s, last=False):
                pe.wait_ge(w_lo, b + 2)
                pe.wait_ge(hl, T_ + 1)
                if last:
                    last_down(pe, 2 * l + 2, (s % 3, (s + 1) % 3), HH, HL, 24 * D_)
                else:
                    down(pe, (s % 3, (s + 1) % 3), HH, HL, 24 * D_)

            t0 = FT * l
            tile(t0, w0, w0, True)
            tile(t0 + 1, w0 + 2, w0 + 2, False)
            with pe.Fori(1, FG) as g:
                b = w0 - 2 + 6 * g
                s = w0 + 4
                tile(2 * g + t0, b, s, False)
                downs(g + (d0 - 1), 2 * g + (t0 - 1), b + 2, s + 2)
                tile(2 * g + (t0 + 1), b + 4, s + 4, False)
            downs(d0 + FG - 1, t0 + FT - 1, w0 + 4 + 6 * (FG - 1), w0 + 4, last=True)

        def act_ffn(act, l):
            w0, d0, t0 = (W_F0, W_F1)[l], (DOWNS[1], DOWNS[3])[l], FT * l
            acts = ACTS[2 * l + 1]
            act.wait_ge(al_done, acts)
            act.wait_ge(u0_set, l + 1)

            def bias(T_):
                for c in range(NC):
                    act.wait_ge(u_full, 3 * T_ + c + 1)
                    if c == 0 and not first_of_all(T_):
                        act.wait_ge(cn, T_)
                    n = CW if c < 2 else SEQ - 2 * CW
                    last = nc.scalar.activation(U[:, 2 + c * CW:2 + c * CW + n], PS[:, c, 0:n], ACT.Copy)
                    if c == 2:
                        last = nc.scalar.activation(U[:, UP:UW].rearrange("p (b s) -> p b s", s=2 + LS)[:, :, 2:2 + LS],
                                                    PS[:, 2, n:CW].rearrange("p (b s) -> p b s", s=LS), ACT.Copy)
                    last.then_inc(u_ev, 1)
                act.wait_ge(u_ev, 3 * T_ + 3)
                act.wait_ge(pre, T_ + 1)
                if not first_of_all(T_):
                    act.wait_ge(h_made, 3 * T_)
                nc.scalar.activation(C[:, 0:CV], U[:, 2:UW], ACT.Identity, bias=PC[:, 19:20], scale=PC[:, 18:19]).then_inc(cb, 1)

            def gelu(T_):
                act.wait_ge(cv2, T_ + 1)
                nc.scalar.activation(C[:, 0:CV], C[:, 0:CV], ACT.Gelu_apprx_tanh).then_inc(gl, 1)

            def hi(T_, t):
                act.wait_ge(h_made, 3 * T_ + 3)
                nc.scalar.activation(HH[:, t], HF[:], ACT.Copy).then_inc(hh, 1)

            def tile(T_, nxt):
                bias(T_)
                nxt(0)
                gelu(T_)
                act.wait_ge(v_full, 3 * T_ + 3)
                nxt(1)

            def rnd(b, third, s):
                w_round(act, b, third, s % 3)

            for t in range(2):
                tile(t0 + t, lambda x: rnd(w0 + 2 * t + x + 3, (w0 + 2 * t + x + 3) // 3, w0 + 2 * t + x))
                hi(t0 + t, t)
            with act.Fori(1, FG) as g:
                b = w0 - 2 + 6 * g
                s = w0 + 4

                def at(p):
                    rnd(b + p + 3, 2 * g + (s + p + 3) // 3 - 2, s + p)

                tile(2 * g + t0, at)
                act.wait_ge(dn_full, 24 * g + 24 * d0)
                at(2)
                at(3)
                hi(2 * g + t0, 0)
                tile(2 * g + (t0 + 1), lambda x: at(4 + x))
                hi(2 * g + (t0 + 1), 1)
            act_square(act, 2 * l + 2, "post", 0)
            act_rstd(act, 2 * l + 2, "post", 0)
            act.wait_ge(dn_full, 24 * (d0 + FG))
            for x in range(2):
                b = w0 + 4 + 6 * (FG - 1) + x + 3
                if b < W_END:
                    rnd(b, b // 3, b)

        def dve_ffn(dve, l):
            d0, t0 = (DOWNS[1], DOWNS[3])[l], FT * l
            dve.wait_ge(al_done, ACTS[2 * l + 1])
            nc.vector.memset(U[:, 0:2], 0.0).then_inc(u0_set, 1)
            dve.wait_ge(fp_in, 16 * (l + 1))

            def conv(T_, t):
                if not first_of_all(T_):
                    dve.wait_ge(cb, T_)
                    dve.wait_ge(cv2, T_)
                nc.vector.tensor_copy(PC[:], PAR[:, bass.ds(t, 1)].rearrange("p a n -> p (a n)")).then_inc(pc, 1)
                dve.wait_ge(pc, T_ + 1)
                if not first_of_all(T_):
                    dve.wait_ge(cn, T_)
                nc.vector.tensor_copy(U[:, UP:UW].rearrange("p (b s) -> p b s", s=2 + LS)[:, :, 0:2],
                                      PC[:, 0:16].rearrange("p (b s) -> p b s", s=2)).then_inc(pre, 1)
                dve.wait_ge(cb, T_ + 1)
                nc.vector.scalar_tensor_tensor(C[:, 0:CV], U[:, 1:1 + CV], PC[:, 17:18], C[:, 0:CV], ALU.mult, ALU.add).then_inc(cv1, 1)
                dve.wait_ge(cv1, T_ + 1)
                nc.vector.scalar_tensor_tensor(C[:, 0:CV], U[:, 0:CV], PC[:, 16:17], C[:, 0:CV], ALU.mult, ALU.add).then_inc(cv2, 1)
                nc.vector.tensor_copy(CN[:, bass.ds(t, 1), 0:2].rearrange("p a n -> p (a n)"), U[:, SEQ:SEQ + 2])
                nc.vector.tensor_copy(CN[:, bass.ds(t, 1), 2:18].rearrange("p a (b s) -> p (a b) s", s=2),
                                      U[:, UP:UW].rearrange("p (b s) -> p b s", s=2 + LS)[:, :, LS:LS + 2]).then_inc(cn, 1)

            def product(T_):
                dve.wait_ge(gl, T_ + 1)
                if not first_of_all(T_):
                    dve.wait_ge(hl, T_)
                for c in range(NC):
                    dve.wait_ge(v_full, 3 * T_ + c + 1)
                    n = CW if c < 2 else SEQ - 2 * CW
                    last = nc.vector.tensor_tensor(HF[:, c * CW:c * CW + n], C[:, c * CW:c * CW + n], PS[:, 3 + c, 0:n], ALU.mult)
                    if c == 2:
                        last = nc.vector.tensor_tensor(
                            HF[:, SEQ:T].rearrange("p (b s) -> p b s", s=LS),
                            C[:, UP:UW].rearrange("p (b s) -> p b s", s=2 + LS)[:, :, 0:LS],
                            PS[:, 5, n:CW].rearrange("p (b s) -> p b s", s=LS), ALU.mult)
                    last.then_inc(h_made, 1)

            def lo(T_, t):
                dve.wait_ge(hh, T_ + 1)
                nc.vector.tensor_tensor(HL[:, t], HF[:], HH[:, t].bitcast(fp32), ALU.subtract).then_inc(hl, 1)

            for t in range(2):
                conv(t0 + t, t)
                product(t0 + t)
                lo(t0 + t, t)
            dve.wait_ge(az_done, 2 * l + 2)
            with dve.Fori(1, FG) as g:
                conv(2 * g + t0, 2 * g)
                product(2 * g + t0)
                down_add(dve, 24 * g + 24 * (d0 - 1))
                lo(2 * g + t0, 0)
                conv(2 * g + (t0 + 1), 2 * g + 1)
                product(2 * g + (t0 + 1))
                lo(2 * g + (t0 + 1), 1)
            down_add(dve, 24 * (d0 + FG - 1))

        def sp_ffn(sp, l):
            w0 = (W_F0, W_F1)[l]
            sp.wait_ge(al_done, ACTS[2 * l + 1])
            if l:
                sp.wait_ge(cn_out, 16)
            sp.dma_start(PAR[:], ffnpar[l]).then_inc(fp_in, 16)
            w_loads(sp, w0 + 3, min(w0 + 3 * FT + 3, W_END))
            sp.wait_ge(cn, FT * (l + 1))
            sp.dma_start(conv_new[l], CN[:]).then_inc(cn_out, 16)

        NIT = 4 * NBLK
        UT = (T - SEQ) * 2

        def pe_attn(pe):
            pe.wait_ge(kt_ev, 1)
            pe.wait_ge(one, 1)
            with pe.Fori(0, NKV) as n:
                slot = [(W_M1 + p) % 3 for p in range(HW)]
                b = HW * n + W_M1
                pe.wait_ge(dn_add, 48 * n + 24 * DOWNS[2])

                def query(x):
                    t, c = divmod(x, NC)
                    if c == 0:
                        pe.wait_ge(w_lo, b + t + 1)
                    if t == 0:
                        pe.wait_ge(al_done, ACTS[2] - NC + c + 1)
                    if x >= 8:
                        pe.wait_ge(q_ev, 12 * n + x - 1)
                    project(pe, x if x < 6 else 6 + x % 2, slot[t], c, q_full)

                def scores(it):
                    t, i = divmod(it, NBLK)
                    if it >= 2:
                        pe.wait_ge(sa, NIT * n + it - 1)
                    for e in range(2):
                        x = slice(64 * e, 64 * e + 64)
                        q = Q1[x, t, i * WIN:(i + 1) * WIN]
                        bank = 2 * (it % 2) + e
                        if i:
                            last = nc.tensor.matmul(PS[:, bank, 0:2 * WIN], q, KG[x, (i - 1) * WIN:(i + 1) * WIN],
                                                    start=True, stop=True)
                        else:
                            last = nc.tensor.matmul(PS[:, bank, WIN:2 * WIN], q, KG[x, 0:WIN], start=True, stop=True)
                    last.then_inc(sf, 1)

                def transposed(it):
                    i = it % NBLK
                    pe.wait_ge(es, NIT * n + it + 1)
                    if it >= 2:
                        pe.wait_ge(te, NIT * n + it - 1)
                    else:
                        pe.wait_ge(xol, 4 * n + 2)
                    for e in range(2):
                        for k in range(0 if i else 1, 2):
                            m = 2 * e + k
                            last = nc.tensor.transpose(PS[:, 4 + it % 2, m * P:(m + 1) * P],
                                                       SS[:, it % 3, e, k * WIN:(k + 1) * WIN], ident[:])
                    last.then_inc(tf, 1)

                def values(it):
                    i = it % NBLK
                    pe.wait_ge(te, NIT * n + it + 1)
                    if it:
                        pe.wait_ge(on, NIT * n + it)
                    for e in range(2):
                        for k in range(0 if i else 1, 2):
                            last = nc.tensor.matmul(PS[:, 6, 64 * e:64 * e + 64], PT[:, it % 2, 2 * e + k],
                                                    VG[:, i - 1 + k], start=(k == 0 or i == 0), stop=(k == 1))
                    last.then_inc(of, 1)

                def turned(it):
                    pe.wait_ge(on, NIT * n + it + 1)
                    if it:
                        pe.wait_ge(xh, NIT * n + it)
                    nc.tensor.transpose(PS[:, 7, 0:P], OT[:, it % 2], ident[:]).then_inc(xf, 1)

                def s_scores(j):
                    for e in range(2):
                        x = slice(64 * e, 64 * e + 64)
                        q = QS[x, 2 * j:2 * j + 2].rearrange("p t m -> p (t m)")
                        for half in range(2):
                            nc.tensor.matmul(PS[x, 2 * e + half, :], q,
                                             KCG[x, 4 * half:4 * half + 4].rearrange("p b k -> p (b k)"), start=True, stop=True)
                        last = nc.tensor.matmul(PS[x, 4 + e, 0:SAMP], q, KG[x, SEQ:T], start=True, stop=True)
                    last.then_inc(xsf, 1)

                def s_transposed(j):
                    pe.wait_ge(xsc, 2 * n + j + 1)
                    for b_ in range(NB):
                        nc.tensor.transpose(PS[:, b_ // 4, (b_ % 4) * P:(b_ % 4 + 1) * P], SX[:, b_ * WIN:(b_ + 1) * WIN], ident[:])
                    nc.tensor.transpose(PS[0:SAMP, 2, 0:P], SX[:, SEQ:T], ident[:]).then_inc(xtf, 1)

                def s_values(j):
                    pe.wait_ge(xte, 2 * n + j + 1)
                    for e in range(2):
                        y = slice(64 * e, 64 * e + 64)
                        for b_ in range(NB):
                            nc.tensor.matmul(PS[y, 4 + e, 0:UT], VCG[:, b_], PX[:, b_, y], start=(b_ == 0), stop=False)
                        last = nc.tensor.matmul(PS[y, 4 + e, 0:UT], VG[0:SAMP, 8], PXN[:, y], start=False, stop=True)
                    last.then_inc(xof, 1)

                for x in range(7):
                    query(x)
                pe.wait_ge(kg_in, 112 * n + 112)
                pe.wait_ge(q_ev, 12 * n + 6)
                query(7)
                s_scores(0)
                query(8)
                query(9)
                query(10)
                s_transposed(0)
                s_values(0)
                for s in range(NIT + 7):
                    if s < NIT:
                        scores(s)
                    if s == 1:
                        query(11)
                    if s == 5:
                        pe.wait_ge(q_ev, 12 * n + 12)
                    if 3 <= s < NIT + 3:
                        transposed(s - 3)
                    if 5 <= s < NIT + 5:
                        values(s - 5)
                    if s == NIT + 4:
                        s_scores(1)
                    if s >= 7:
                        turned(s - 7)

                pe.wait_ge(w_lo, b + 6)
                pe.wait_ge(xh, NIT * n + NIT)
                pe.wait_ge(xl, 4 * n + 2)
                pe.wait_ge(xol, 4 * n + 2)
                before = 48 * n + 24 * DOWNS[2]
                down(pe, (slot[4], slot[5]), OH1, OL1, before, idle=True, units=range(0, 14))
                s_transposed(1)
                down(pe, (slot[4], slot[5]), OH1, OL1, before, units=range(14, 18))
                s_values(1)
                down(pe, (slot[4], slot[5]), OH1, OL1, before, units=range(18, 24))
                pe.wait_ge(w_lo, b + 8)
                pe.wait_ge(xol, 4 * n + 4)
                pe.wait_ge(xl, 4 * n + 4)
                down(pe, (slot[6], slot[7]), OH2, OL2, before + 24)

        def dve_attn(dve):
            dve.wait_ge(a_c_in, 16 * 3)
            dve.wait_ge(az_done, 3)
            with dve.Fori(0, NKV) as n:
                nc.vector.tensor_copy(SKG[:, 0:8], SINK[:, bass.ds(8 * n, 8)])
                nc.vector.tensor_copy(SKG[:, 8:10], SKS[:, bass.ds(2 * n, 2)]).then_inc(skg, 1)
                dve.wait_ge(skg, 2 * n + 1)
                nc.vector.tensor_scalar(SKN[:], SKG[:, 0:8], -1.0, None, ALU.mult).then_inc(skg, 1)
                dve.wait_ge(skg, 2 * n + 2)
                dve.wait_ge(bi_in, 256 * n + 256)

                def biased(it):
                    t, i = divmod(it, NBLK)
                    u, r = it % 3, it % 8
                    x0 = 0 if i else WIN
                    dve.wait_ge(sf, NIT * n + it + 1)
                    if it >= 3:
                        dve.wait_ge(tf, NIT * n + it - 2)
                    bank = 2 * (it % 2)
                    nc.vector.tensor_tensor(SS[:, u, :, x0:], PS[:, bank:bank + 2, x0:2 * WIN],
                                            BI[:, 2 * t:2 * t + 2, x0:], ALU.add).then_inc(sa, 1)
                    dve.wait_ge(sa, NIT * n + it + 1)
                    nc.vector.tensor_reduce(ST[:, r, 0:2], SS[:, u, :, x0:], AX.X, ALU.max).then_inc(mx, 1)
                    dve.wait_ge(mx, NIT * n + it + 1)
                    nc.vector.scalar_tensor_tensor(ST[:, r, 2:4], ST[:, r, 0:2], -1.0, SKN[:, 2 * t:2 * t + 2],
                                                   ALU.mult, ALU.min).then_inc(mm_, 1)
                    dve.wait_ge(mm_, NIT * n + it + 1)
                    nc.vector.tensor_tensor(ST[:, r, 4:6], SKG[:, 2 * t:2 * t + 2], ST[:, r, 2:4], ALU.add).then_inc(nm, 1)

                def scaled(it):
                    r = it % 8
                    dve.wait_ge(es, NIT * n + it + 1)
                    nc.vector.tensor_tensor(ST[:, r, 6:8], ST[:, r, 6:8], ST[:, r, 8:10], ALU.add).then_inc(den, 1)
                    dve.wait_ge(den, NIT * n + it + 1)
                    nc.vector.reciprocal(ST[:, r, 10:12], ST[:, r, 6:8]).then_inc(rc, 1)
                    dve.wait_ge(rc, NIT * n + it + 1)
                    dve.wait_ge(of, NIT * n + it + 1)
                    if it >= 2:
                        dve.wait_ge(xf, NIT * n + it - 1)
                    nc.vector.tensor_tensor(OT[:, it % 2].rearrange("p (e d) -> p e d", e=2),
                                            PS[:, 6, 0:P].rearrange("p (e d) -> p e d", e=2),
                                            bc(ST[:, r, 10:12], HD), ALU.mult).then_inc(on, 1)

                def s_max(j):
                    I = 2 * n + j
                    dve.wait_ge(xsb, I + 1)
                    nc.vector.tensor_reduce(SST[:, 0:1], SX[:], AX.X, ALU.max).then_inc(xmx, 1)
                    dve.wait_ge(xmx, 3 * I + 1)
                    nc.vector.tensor_tensor(SST[:, 0:1], SST[:, 0:1], SKG[:, 8 + j:9 + j], ALU.max).then_inc(xmx, 1)
                    dve.wait_ge(xmx, 3 * I + 2)
                    nc.vector.tensor_tensor(SST[:, 2:3], SKG[:, 8 + j:9 + j], SST[:, 0:1], ALU.subtract)
                    nc.vector.tensor_scalar(SST[:, 1:2], SST[:, 0:1], -1.0, None, ALU.mult).then_inc(xmx, 1)

                def s_scaled(j):
                    I = 2 * n + j
                    dve.wait_ge(xex, I + 1)
                    nc.vector.tensor_tensor(SST[:, 4:5], SST[:, 4:5], SST[:, 5:6], ALU.add).then_inc(xrc, 1)
                    dve.wait_ge(xrc, 2 * I + 1)
                    nc.vector.reciprocal(SST[:, 6:7], SST[:, 4:5]).then_inc(xrc, 1)
                    dve.wait_ge(xrc, 2 * I + 2)
                    nc.vector.tensor_scalar(SX[:], SX[:], SST[:, 6:7], None, ALU.mult).then_inc(xsc, 1)

                def s_lo(j):
                    oh, ol = (OH1, OL1) if j == 0 else (OH2, OL2)
                    for e in range(2):
                        y = slice(64 * e, 64 * e + 64)
                        dve.wait_ge(xoh, 2 * (2 * n + j) + 2)
                        nc.vector.tensor_tensor(ol[y, :, SEQ:T], PS[y, 4 + e, 0:UT].rearrange("p (t m) -> p t m", t=2),
                                                oh[y, :, SEQ:T].bitcast(fp32), ALU.subtract).then_inc(xol, 1)

                for e in range(2):
                    s_add(dve, n, 0, e)
                s_masked(dve, n, 0)
                s_max(0)
                s_scaled(0)
                s_lo(0)
                for s in range(1, NIT + 6):
                    if s >= 6:
                        scaled(s - 6)
                    if s <= NIT:
                        biased(s - 1)
                before = 48 * n + 24 * DOWNS[2]
                for m in range(NC * KT):
                    down_add(dve, before, units=[m])
                    if m < 2:
                        s_add(dve, n, 1, m)
                    elif m == 2:
                        s_masked(dve, n, 1)
                    elif m == 4:
                        s_max(1)
                    elif m == 8:
                        s_scaled(1)
                    elif m == 21:
                        s_lo(1)
                down_add(dve, before + 24)

        def pool_attn(pool):
            with pool.Fori(0, NKV) as n:
                for p in range(3, 7):
                    w_rest(pool, HW * n + W_M1 + p, (W_M1 + p) % 3)
                for t in range(4):
                    oh, ol, whole = (OH1, OL1, OW1) if t < 2 else (OH2, OL2, OW2)
                    pool.wait_ge(xt, 4 * n + t + 1)
                    nc.gpsimd.tensor_tensor(ol[:, t % 2, 0:SEQ], whole[:, t % 2, 0:SEQ],
                                            oh[:, t % 2, 0:SEQ].bitcast(fp32), ALU.subtract).then_inc(xl, 1)
                for p in range(7, 12):
                    w_rest(pool, HW * n + W_M1 + p, (W_M1 + p) % 3)

        def s_add(dve, n, j, e):
            y = slice(64 * e, 64 * e + 64)
            dve.wait_ge(xsf, 2 * n + j + 1)
            nc.vector.tensor_tensor(SX[y, 0:SEQ].rearrange("p (b k) -> p b k", b=NB),
                                    PS[y, 2 * e:2 * e + 2].rearrange("p h (b k) -> p (h b) k", b=4),
                                    SBC[y, j, 0:WIN].unsqueeze(1).broadcast_to([64, NB, WIN]), ALU.add)
            nc.vector.tensor_tensor(SX[y, SEQ:T].rearrange("p (b k) -> p b k", b=NB),
                                    PS[y, 4 + e, 0:SAMP].rearrange("p (b k) -> p b k", b=NB),
                                    SBC[y, j, WIN:WIN + LS].unsqueeze(1).broadcast_to([64, NB, LS]), ALU.add).then_inc(xsa, 1)

        def s_masked(dve, n, j):
            dve.wait_ge(xsa, 2 * (2 * n + j) + 2)
            nc.vector.tensor_tensor(SX[:, 0:SEQ].rearrange("p (b k) -> p b k", b=NB),
                                    SX[:, 0:SEQ].rearrange("p (b k) -> p b k", b=NB), bc(BM4[:], WIN), ALU.add)
            nc.vector.tensor_tensor(SX[:, SEQ:T], SX[:, SEQ:T], SM4[:], ALU.add).then_inc(xsb, 1)

        def act_attn(act):
            act.wait_ge(kw_out, 16 * 20)
            act.wait_ge(kv_out, 16 * 3)
            for c in range(NC):
                act.wait_ge(h_out[c], 16)
            with act.Fori(0, NKV) as n:
                slot = [(W_M1 + p) % 3 for p in range(HW)]
                third = [(W_M1 + p) // 3 for p in range(HW + 3)]

                def round_next(p):
                    w_round(act, HW * n + W_M1 + p + 3, 3 * n + third[p + 3], slot[p])

                def query(x):
                    t, c = divmod(x, NC)
                    act.wait_ge(q_full, 12 * n + x + 1)
                    bank = x if x < 6 else 6 + x % 2
                    if c == 2:
                        nc.scalar.activation(QS[:, t], PS[:, bank, CW - SAMP:CW], ACT.Copy, scale=HD ** -0.5)
                    nc.scalar.activation(Q1[:, t, chunk(c)], PS[:, bank, 0:CW], ACT.Copy, scale=HD ** -0.5).then_inc(q_ev, 1)
                    if c == 2:
                        round_next(t)

                def exps(it):
                    u, r, i = it % 3, it % 8, it % NBLK
                    x0 = 0 if i else WIN
                    act.wait_ge(nm, NIT * n + it + 1)
                    for e in range(2):
                        nc.scalar.activation(SS[:, u, e, x0:], SS[:, u, e, x0:], ACT.Exp, bias=ST[:, r, 2 + e:3 + e],
                                             accum_out=ST[:, r, 6 + e:7 + e])
                    nc.scalar.activation(ST[:, r, 8:10], ST[:, r, 4:6], ACT.Exp).then_inc(es, 1)

                def turn(it):
                    u, i = it % 2, it % NBLK
                    act.wait_ge(tf, NIT * n + it + 1)
                    if it >= 2:
                        act.wait_ge(of, NIT * n + it - 1)
                    if i:
                        nc.scalar.activation(PT[:, u].rearrange("p m q -> p (m q)"), PS[:, 4 + u], ACT.Copy).then_inc(te, 1)
                    else:
                        nc.scalar.activation(PT[:, u, 1:4:2], PS[:, 4 + u].rearrange("p (m q) -> p m q", q=P)[:, 1:4:2],
                                             ACT.Copy).then_inc(te, 1)

                def kept(it):
                    t, i = divmod(it, NBLK)
                    oh, whole = (OH1, OW1) if t < 2 else (OH2, OW2)
                    act.wait_ge(xf, NIT * n + it + 1)
                    nc.scalar.activation(whole[:, t % 2, i * WIN:(i + 1) * WIN], PS[:, 7, 0:P], ACT.Copy).then_inc(xh, 1)
                    if i == NBLK - 1:
                        act.wait_ge(xh, NIT * n + it + 1)
                        nc.scalar.activation(oh[:, t % 2, 0:SEQ], whole[:, t % 2, 0:SEQ], ACT.Copy).then_inc(xt, 1)

                def s_exps(j):
                    act.wait_ge(xmx, 3 * (2 * n + j) + 3)
                    nc.scalar.activation(SX[:], SX[:], ACT.Exp, bias=SST[:, 1:2], accum_out=SST[:, 4:5])
                    nc.scalar.activation(SST[:, 5:6], SST[:, 2:3], ACT.Exp).then_inc(xex, 1)

                def s_turn(j):
                    act.wait_ge(xtf, 2 * n + j + 1)
                    nc.scalar.activation(PX[:].rearrange("p (h b) n -> p h (b n)", h=2), PS[:, 0:2], ACT.Copy)
                    nc.scalar.activation(PXN[:], PS[0:SAMP, 2, 0:P], ACT.Copy).then_inc(xte, 1)

                def s_hi(j):
                    oh = OH1 if j == 0 else OH2
                    for e in range(2):
                        y = slice(64 * e, 64 * e + 64)
                        act.wait_ge(xof, 2 * n + j + 1)
                        nc.scalar.activation(oh[y, :, SEQ:T], PS[y, 4 + e, 0:UT].rearrange("p (t m) -> p t m", t=2),
                                             ACT.Copy).then_inc(xoh, 1)

                for x in range(10):
                    query(x)
                s_exps(0)
                query(10)
                s_turn(0)
                s_hi(0)
                for s in range(2, NIT + 8):
                    if s == 3:
                        query(11)
                    if s >= 8:
                        kept(s - 8)
                    if 4 <= s < NIT + 4:
                        turn(s - 4)
                    if s < NIT + 2:
                        exps(s - 2)
                s_exps(1)
                s_turn(1)
                s_hi(1)
                act.wait_ge(dn_full, 48 * n + 24 * DOWNS[2] + 24)
                round_next(4)
                round_next(5)
                act.wait_ge(dn_full, 48 * n + 24 * DOWNS[2] + 48)
                for p in range(6, HW):
                    round_next(p)

        def sp_attn(sp):
            sp.wait_ge(kv_out, 16 * 3)
            sp.wait_ge(kw_out, 16 * 20)
            sp.wait_ge(al_done, ACTS[2])
            for c in range(NC):
                sp.wait_ge(h_out[c], 16)
            for dst, src in ((BM4, bmask4), (SM4, smask4), (SKS, sinks[1, :, 0:2 * NKV])):
                sp.dma_start(dst[:], src).then_inc(a_c_in, 16)
            with sp.Fori(0, NKV) as n:
                for p in range(3):
                    w_load(sp, HW * n + W_M1 + p + 3, (W_M1 + p) % 3)
                sp.wait_ge(dn_full, 48 * n + 24 * DOWNS[2])
                for e in range(2):
                    x = slice(64 * e, 64 * e + 64)
                    sp.dma_start(KG[x], kt_dram[bass.ds(64 * n, 64)]).then_inc(kg_in, 16)
                    sp.dma_start(KCG[x], kcT[bass.ds(64 * n, 64)]).then_inc(kg_in, 16)
                sp.dma_start(VG[:, 0:8], v_dram[0:SEQ].rearrange("(t p) d -> p t d", p=P)[:, :, bass.ds(64 * n, 64)]).then_inc(kg_in, 16)
                sp.dma_start(VG[0:SAMP, 8], v_dram[SEQ:T, bass.ds(64 * n, 64)]).then_inc(kg_in, 16)
                sp.dma_start(VCG[:], vc[:, :, bass.ds(64 * n, 64)]).then_inc(kg_in, 16)
                for x in range(8):
                    h0 = (8 * n + x) * (P * RL)
                    sp.dma_start(BI[:, x], bass.AP(r_dram.tensor, h0 + (WIN - 1), [[RL - 1, P], [1, 2 * WIN]])).then_inc(bi_in, 16)
                    j, t, e = x // 4, x // 2 % 2, x % 2
                    y = 64 * e + 32 * t
                    sp.dma_start(SBC[y:y + 32, j], bass.AP(r_dram.tensor, h0 + (WIN - 1), [[0, NB], [RL - 1, LS], [1, WIN + LS]])).then_inc(bi_in, 16)
                for p in range(3, HW):
                    w_load(sp, HW * n + W_M1 + p + 3, (W_M1 + p) % 3)

        block = ctx.enter_context(nc.Block())

        @block.sync
        def _(sp):
            sp.dma_start(OHR[:], onehot).then_inc(tb_in, 16)
            for dst, src in ((ident, ident_in), (GC, gains), (SINK, sinks[0])):
                sp.dma_start(dst[:], src).then_inc(c_in, 16)
            sp.wait_ge(tb_one, 1)
            sp.dma_start(TBL[0:32], table).then_inc(tb_in, 16)
            sp_boundary(sp, 0)
            for b in range(1, 3):
                sp.dma_start(WR[:, b], wall[b]).then_inc(w_in[b], 16)
            sp.wait_ge(rb_row, NQ)
            sp.dma_start(r_dram.rearrange("(h p m) -> p h m", p=P, m=RL), RB[:]).then_inc(rb_out, 16)
            sp_gla(sp)
            sp_boundary(sp, 1)
            sp_ffn(sp, 0)
            sp_boundary(sp, 2)
            w_loads(sp, W_KV + 3, W_M1 + 3)
            sp_kv(sp)
            sp_attn(sp)
            sp_boundary(sp, 3)
            sp_ffn(sp, 1)
            sp_boundary(sp, 4)
            for c in range(NC):
                sp.wait_ge(h_out[c], 32)
            sp.wait_ge(cn_out, 32)
            sp.wait_ge(gp_out, 16 * H)
            sp.wait_ge(st_out, 16 * H)
            sp.wait_ge(kw_out, 16 * 20)
            sp.wait_ge(kv_out, 16 * 3)
            sp.wait_ge(rb_out, 16)

        @block.gpsimd
        def _(pool):
            pool_boundary(pool, 0)
            w_rests(pool, 3, 4)
            zero_acc(pool, 0)
            w_rests(pool, 4, W_F0 + 3)
            pool_boundary(pool, 1)
            w_rests(pool, W_F0 + 3, W_F0 + 4)
            zero_acc(pool, 1)
            w_rests(pool, W_F0 + 4, W_KV + 3)
            pool_boundary(pool, 2)
            zero_acc(pool, 2)
            pool_attn(pool)
            pool_boundary(pool, 3)
            w_rests(pool, W_F1 + 3, W_F1 + 4)
            zero_acc(pool, 3)
            w_rests(pool, W_F1 + 4, W_END)

        @block.vector
        def _(dve):
            nc.vector.memset(EPSC[:], EPS)
            nc.vector.memset(ones[:], 1.0).then_inc(one, 1)
            nc.vector.memset(TBL[:], 1.0).then_inc(tb_one, 1)
            dve.wait_ge(tb_in, 32)
            nc.vector.tensor_copy(TBB[:], bc(TBL[:], P)).then_inc(tb_cols, 1)
            dve.wait_ge(c_in, 48)
            dve_boundary(dve, 0)
            dve_gla(dve)
            dve_boundary(dve, 1)
            dve_ffn(dve, 0)
            dve_boundary(dve, 2)
            dve_attn(dve)
            dve_boundary(dve, 3)
            dve_ffn(dve, 1)
            dve_boundary(dve, 4)

        @block.scalar
        def _(act):
            act.wait_ge(one, 1)
            act_boundary(act, 0)
            act_gla(act)
            act_boundary(act, 1)
            act_ffn(act, 0)
            act_boundary(act, 2)
            act_kv(act)
            act_attn(act)
            act_boundary(act, 3)
            act_ffn(act, 1)
            act_boundary(act, 4)

        @block.tensor
        def _(pe):
            pe.wait_ge(tb_cols, 1)
            pe.wait_ge(c_in, 48)
            pe.wait_ge(one, 1)
            pe_boundary(pe, 0)
            pe_gla(pe)
            pe_boundary(pe, 1)
            pe_ffn(pe, 0)
            pe_boundary(pe, 2)
            pe_kv_tokens(pe)
            pe_attn(pe)
            pe_boundary(pe, 3)
            pe_ffn(pe, 1)
            pe_boundary(pe, 4)


def _constants():
    one = np.zeros((33, RL), np.float32)
    for m in range(RL):
        n = 255 - m
        if 0 <= n < WIN:
            if n < 16:
                bucket = n
            else:
                large = 16 + int(np.float32(np.float32(np.log(np.float32(n / 16.0))) / np.float32(math.log(8.0)) * 16))
                bucket = min(large, 31)
            one[bucket, m] = 1.0
        else:
            one[32, m] = NEG
    j, i = np.arange(CH)[:, None], np.arange(CH)[None, :]
    masks = np.zeros((CH, 5, CH), np.float32)
    for n, L in enumerate(LEVELS):
        masks[:, n] = (j // (2 * L) == i // (2 * L)) & (j % (2 * L) < L) & (i % (2 * L) >= L)
    masks[:, 4] = (j // FINE == i // FINE) & (j <= i)
    j, i = np.arange(SAMP)[:, None], np.arange(SAMP)[None, :]
    same = (j // LS == i // LS)
    smask = (same & (j <= i)).astype(np.float32)
    bmask = (np.arange(SAMP)[:, None] // LS == np.arange(NB)[None, :]).astype(np.float32)
    scan = np.ones((2, T), np.float32)
    scan[0, 0:SEQ:CH] = 0
    scan[0, SEQ::LS] = 0
    scan[1, 0:SEQ:FINE] = 0
    scan[1, SEQ::LS] = 0
    bf = mybir.dt.np(bf16)
    b4 = np.where(np.tile(bmask, (4, 1)) > 0, 0.0, NEG).astype(np.float32)
    s4 = np.where(np.tile(same, (4, 1)), 0.0, NEG).astype(np.float32)
    return dict(onehot=one, masks=masks.astype(bf), smask=smask.astype(bf), bmask=bmask,
                scanm=np.ascontiguousarray(np.broadcast_to(scan, (P, 2, T))).astype(bf),
                ident_in=np.eye(P, dtype=np.float32), bmask4=b4, smask4=s4)


def _column_block(w, x):
    return w[:, x:x + P].reshape(KT, P, P).transpose(1, 0, 2).reshape(P, KT * P)


def _lay_out(i):
    w_in, w_up, w_down = i["w_in_a"][0], i["w_up"], i["w_down"]
    wall = np.zeros((W_END, P, KT * P), np.float32)
    wall[W_GLR].reshape(P, KT, P)[:, :, 0:RANK] = w_in[:, 3072:3088].reshape(KT, P, RANK).transpose(1, 0, 2)
    for h in range(H):
        b = W_M0 + 2 + HW * h
        at_q, at_k = (W_M0, W_M0 + 1) if h == 0 else (b - HW + 4, b - HW + 6)
        wall[at_q] = _column_block(w_in, h * P)
        wall[at_k] = _column_block(w_in, 512 + h * P)
        for t in range(2):
            wall[b + t] = _column_block(w_in, 1024 + h * DV + t * P)
            wall[b + 2 + t] = _column_block(w_in, 2048 + h * DV + t * P)
            wall[b + (7 if h < H - 1 else 4) + t] = i["w_out_a"][0, h * DV + t * P:h * DV + (t + 1) * P]
    for l, w0 in enumerate((W_F0, W_F1)):
        for g in range(FG):
            b = w0 if g == 0 else w0 + 4 + 6 * (g - 1)
            for t in range(2):
                bt = b + 2 * t + (2 * t if g else 0)
                x = (2 * g + t) * P
                wall[bt] = _column_block(w_up[l], x)
                wall[bt + 1] = _column_block(w_up[l], FF + x)
                bd = w0 + 4 + 6 * g + 2 + t if g < FG - 1 else w0 + 4 + 6 * (FG - 1) + t
                wall[bd] = w_down[l, x:x + P]
    for x in range(2):
        wall[W_KV + x] = _column_block(i["w_kv"], x * P)
    for n in range(NKV):
        for j in range(2):
            for t in range(2):
                x = (4 * n + 2 * j + t) * P
                wall[W_M1 + HW * n + 2 * j + t] = _column_block(i["w_q_b"][0], x)
                wall[W_M1 + HW * n + 4 + 2 * j + t] = i["w_o_b"][0, x:x + P]
    x = np.concatenate([i["x_prompt"][0], i["x_sample"].reshape(SAMP, D)], 0)
    xT = x.reshape(NC, CW, KT, P).transpose(0, 3, 2, 1)
    rows = [i[n].reshape(-1, P) for n in ("g_mix_pre", "g_mix_post", "g_ffn_pre", "g_ffn_post", "g_kv", "g_gla_out")]
    par = np.zeros((2, P, FT, 20), np.float32)
    par[:, :, :, 0:16] = i["cache_conv"].reshape(2, 16, FT, P).transpose(0, 3, 2, 1)
    par[:, :, :, 16:19] = i["conv_w"].reshape(2, 3, FT, P).transpose(0, 3, 2, 1)
    par[:, :, :, 19] = i["conv_b"].reshape(2, FT, P).transpose(0, 2, 1)
    wg = np.concatenate([i["w_gate_up"][0], i["b_gate"][0][None]], 0).reshape(RANK + 1, H, P).transpose(1, 0, 2)
    s = i["sinks"][0]
    sinks = np.stack([np.broadcast_to(s, (P, NQ)), np.zeros((P, NQ), np.float32)])
    sinks[1, :, 0:4] = np.repeat(s.reshape(4, 2, 2).transpose(0, 2, 1).reshape(4, 4), 32, axis=1).T
    out = dict(wall=wall, xT=xT, gains=np.concatenate(rows, 0).T, ffnpar=par, wgate=wg,
               state=i["state_gla"][0].transpose(1, 2, 0, 3),
               kcT=i["cache_k_win"].transpose(2, 3, 0, 1).reshape(P, NB, WIN),
               vc=i["cache_v_win"].transpose(1, 0, 2, 3).reshape(WIN, NB, P),
               ck=i["cache_k_win"].reshape(NB, WIN, P), cv=i["cache_v_win"].reshape(NB, WIN, P),
               table=i["rel_bias"], sinks=sinks, **_constants())
    return {k: np.ascontiguousarray(v) for k, v in out.items()}


_OUTS = dict(yT=(NC, P, KT, CW), gla_p=(H, DK, DV), gla_s=(H, DK, NB, DV), conv_new=(2, P, FT, 18),
             kwin_p=(WIN, P), kwin_s=(NB, WIN, P), vwin_p=(WIN, P), vwin_s=(NB, WIN, P))


def kernel(**inputs):
    import concourse.bacc as bacc
    from concourse.bass_utils import run_bass_kernel_spmd

    arrays = _lay_out({k: np.asarray(v) for k, v in inputs.items()})
    nc = bacc.Bacc("TRN2", target_bir_lowering=False, num_devices=1)
    aps = {n: nc.dram_tensor(n, a.shape, mybir.dt.from_np(a.dtype), kind="ExternalInput").ap() for n, a in arrays.items()}
    for n, shape in _OUTS.items():
        aps[n] = nc.dram_tensor(n, shape, fp32, kind="ExternalOutput").ap()
    build(nc, **aps)
    r = run_bass_kernel_spmd(nc, [arrays], core_ids=[0]).results[0]
    y = np.asarray(r["yT"]).transpose(0, 3, 2, 1).reshape(T, D)
    conv = np.asarray(r["conv_new"]).transpose(0, 3, 2, 1).reshape(2, 18, FF)
    window = (NKV, HD)
    c = np.ascontiguousarray
    return (c(y[0:SEQ].reshape(1, SEQ, D)), c(y[SEQ:].reshape(NB, LS, D)),
            c(np.asarray(r["gla_p"]).reshape(1, 1, H, DK, DV)), c(np.asarray(r["gla_s"]).transpose(2, 0, 1, 3).reshape(1, NB, H, DK, DV)),
            c(conv[:, 0:2].reshape(2, 1, 2, FF)), c(conv[:, 2:18].reshape(2, NB, 2, FF)),
            c(np.asarray(r["kwin_p"]).reshape(1, WIN, *window)), c(np.asarray(r["kwin_s"]).reshape(NB, WIN, *window)),
            c(np.asarray(r["vwin_p"]).reshape(1, WIN, *window)), c(np.asarray(r["vwin_s"]).reshape(NB, WIN, *window)))
```
